# Optimizing a Trainium2 kernel written in Bass

```python
import math
import jax, jax.numpy as jnp
from jax import lax
import numpy as np
import jax
import jax.numpy as jnp

D_MODEL = 1024
BATCH = 1
SEQ = 256
DEPTH = 2

CHUNK = 128
N_SGU_GROUPS = 8
SGU_WIDTH = D_MODEL
SGU_GROUP = SGU_WIDTH // N_SGU_GROUPS
DIFF_HEAD_DIM = 64
N_DIFF_HEADS = D_MODEL // (2 * DIFF_HEAD_DIM)
DIFF_QK_WIDTH = N_DIFF_HEADS * 2 * DIFF_HEAD_DIM
DIFF_V_WIDTH = N_DIFF_HEADS * 2 * DIFF_HEAD_DIM
Q_BLOCK = 128
ROPE_THETA = 10000.0
N_BRANCH = 2
IN_WIDTH = 2 * SGU_WIDTH + 2 * DIFF_QK_WIDTH + DIFF_V_WIDTH + N_BRANCH * D_MODEL
SPLITS = [SGU_WIDTH, 2 * SGU_WIDTH, 2 * SGU_WIDTH + DIFF_QK_WIDTH,
          2 * SGU_WIDTH + 2 * DIFF_QK_WIDTH,
          2 * SGU_WIDTH + 2 * DIFF_QK_WIDTH + DIFF_V_WIDTH]
D_FF = 2816
ALPHA = (2.0 * DEPTH) ** 0.25
BETA = (8.0 * DEPTH) ** -0.25
LN_EPS = 1e-5


def _lambda_init(layer):
    return 0.8 - 0.6 * math.exp(-0.3 * layer)

def _layernorm(x, g, b):
    xf = x.astype(jnp.float32)
    mu = jnp.mean(xf, axis=-1, keepdims=True)
    var = jnp.mean(jnp.square(xf - mu), axis=-1, keepdims=True)
    y = (xf - mu) * lax.rsqrt(var + LN_EPS)
    return (y * g.astype(jnp.float32) + b.astype(jnp.float32)).astype(x.dtype)

def _rmsnorm(x, g):
    xf = x.astype(jnp.float32)
    y = xf * lax.rsqrt(jnp.mean(jnp.square(xf), axis=-1, keepdims=True) + LN_EPS)
    return (y * g.astype(jnp.float32)).astype(x.dtype)

def _swiglu(x, w1, w3, w2):
    return (jax.nn.silu(x @ w1) * (x @ w3)) @ w2

def _rope(x, cos, sin):
    c = cos[None, :, None, None, :]
    s = sin[None, :, None, None, :]
    xf = x.astype(jnp.float32)
    x1, x2 = jnp.split(xf, 2, axis=-1)
    out = jnp.concatenate([x1 * c - x2 * s, x2 * c + x1 * s], axis=-1)
    return out.astype(x.dtype)

def _chunked_sgu(u, v, g, b, w_s, b_s):
    bsz, seq, _ = v.shape
    v = _layernorm(v, g, b)
    n_chunks = seq // CHUNK
    vb = v.reshape(bsz, n_chunks, CHUNK, N_SGU_GROUPS, SGU_GROUP)
    causal = jnp.tril(jnp.ones((CHUNK, CHUNK), dtype=bool))
    w = jnp.where(causal[None], w_s, jnp.zeros((), w_s.dtype))
    s = jnp.einsum('gtr,bnrgc->bntgc', w, vb) + b_s.T[None, None, :, :, None]
    return u * s.reshape(bsz, seq, SGU_WIDTH).astype(u.dtype)

def _diff_attention(q, k, v, lam):
    bsz, seq = q.shape[:2]
    n_blocks = seq // Q_BLOCK
    qb = q.reshape(bsz, n_blocks, Q_BLOCK, N_DIFF_HEADS, 2, DIFF_HEAD_DIM).swapaxes(0, 1)
    k_pos = jnp.arange(seq)
    scale = DIFF_HEAD_DIM ** -0.5
    neg = jnp.finfo(jnp.float32).min

    def one_block(args):
        q_blk, i = args
        s = jnp.einsum('bqhmd,bkhmd->bhmqk', q_blk, k).astype(jnp.float32) * scale
        q_pos = i * Q_BLOCK + jnp.arange(Q_BLOCK)
        mask = k_pos[None, :] <= q_pos[:, None]
        s = jnp.where(mask, s, neg)
        p = jax.nn.softmax(s, axis=-1)
        a = p[:, :, 0] - lam * p[:, :, 1]
        return jnp.einsum('bhqk,bkhe->bqhe', a.astype(v.dtype), v)

    out = lax.map(one_block, (qb, jnp.arange(n_blocks)))
    return out.swapaxes(0, 1).reshape(bsz, seq, N_DIFF_HEADS, 2 * DIFF_HEAD_DIM)

def _mixer(x, layer, w_in, gate_b, sgu_ln_g, sgu_ln_b, sgu_w, sgu_b, lam, diff_ln_g,
           w_branch, w_out, cos, sin):
    bsz, seq, _ = x.shape
    z = x @ w_in
    u, v, q, k, val, gates = jnp.split(z, SPLITS, axis=-1)
    u = jax.nn.gelu(u, approximate=False)
    v = jax.nn.gelu(v, approximate=False)
    h_a = _chunked_sgu(u, v, sgu_ln_g, sgu_ln_b, sgu_w, sgu_b)
    q = _rope(q.reshape(bsz, seq, N_DIFF_HEADS, 2, DIFF_HEAD_DIM), cos, sin)
    k = _rope(k.reshape(bsz, seq, N_DIFF_HEADS, 2, DIFF_HEAD_DIM), cos, sin)
    val = val.reshape(bsz, seq, N_DIFF_HEADS, 2 * DIFF_HEAD_DIM)
    lam_init = _lambda_init(layer)
    lf = lam.astype(jnp.float32)
    lam_full = (jnp.exp(jnp.sum(lf[0] * lf[1])) - jnp.exp(jnp.sum(lf[2] * lf[3]))
                + lam_init)
    o = _diff_attention(q, k, val, lam_full)
    o = _rmsnorm(o, diff_ln_g) * (1.0 - lam_init)
    h_b = o.reshape(bsz, seq, DIFF_V_WIDTH)
    g = jax.nn.sigmoid(gates.reshape(bsz, seq, N_BRANCH, D_MODEL) + gate_b)
    m = g[:, :, 0] * (h_a @ w_branch[0]) + g[:, :, 1] * (h_b @ w_branch[1])
    return m @ w_out

def first_inputs(seed: int = 0) -> dict:
    key = jax.random.key(seed)
    ks = jax.random.split(key, 20)
    f32 = jnp.float32
    nrm = lambda k, shape, s: jax.random.normal(k, shape, f32) * s
    x = jax.random.normal(ks[0], (BATCH, SEQ, D_MODEL), f32)
    w_in = nrm(ks[1], (DEPTH, D_MODEL, IN_WIDTH), D_MODEL ** -0.5)
    gate_b = nrm(ks[2], (DEPTH, N_BRANCH, D_MODEL), 0.02)
    sgu_ln_g = 1.0 + nrm(ks[3], (DEPTH, SGU_WIDTH), 0.02)
    sgu_ln_b = nrm(ks[4], (DEPTH, SGU_WIDTH), 0.02)
    sgu_w = nrm(ks[5], (DEPTH, N_SGU_GROUPS, CHUNK, CHUNK), CHUNK ** -0.5)
    sgu_b = 1.0 + nrm(ks[6], (DEPTH, N_SGU_GROUPS, CHUNK), 0.02)
    lam = nrm(ks[7], (DEPTH, 4, DIFF_HEAD_DIM), 0.1)
    diff_ln_g = 1.0 + nrm(ks[8], (DEPTH, 2 * DIFF_HEAD_DIM), 0.02)
    w_branch = jnp.concatenate([
        nrm(ks[9], (DEPTH, 1, SGU_WIDTH, D_MODEL), BETA * SGU_WIDTH ** -0.5),
        nrm(ks[10], (DEPTH, 1, DIFF_V_WIDTH, D_MODEL), BETA * DIFF_V_WIDTH ** -0.5)], axis=1)
    w_out = nrm(ks[11], (DEPTH, D_MODEL, D_MODEL), BETA * D_MODEL ** -0.5)
    ffn_w1 = nrm(ks[12], (DEPTH, 2, D_MODEL, D_FF), D_MODEL ** -0.5)
    ffn_w3 = nrm(ks[13], (DEPTH, 2, D_MODEL, D_FF), D_MODEL ** -0.5)
    ffn_w2 = nrm(ks[14], (DEPTH, 2, D_FF, D_MODEL), BETA * D_FF ** -0.5)
    ln_g = 1.0 + nrm(ks[15], (DEPTH, 3, D_MODEL), 0.02)
    ln_b = nrm(ks[16], (DEPTH, 3, D_MODEL), 0.02)
    return {"x": x, "w_in": w_in, "gate_b": gate_b, "sgu_ln_g": sgu_ln_g,
            "sgu_ln_b": sgu_ln_b, "sgu_w": sgu_w, "sgu_b": sgu_b, "lam": lam,
            "diff_ln_g": diff_ln_g, "w_branch": w_branch, "w_out": w_out,
            "ffn_w1": ffn_w1, "ffn_w3": ffn_w3, "ffn_w2": ffn_w2,
            "ln_g": ln_g, "ln_b": ln_b}

def first_block(x, w_in, gate_b, sgu_ln_g, sgu_ln_b, sgu_w, sgu_b, lam, diff_ln_g,
              w_branch, w_out, ffn_w1, ffn_w3, ffn_w2, ln_g, ln_b):
    seq = x.shape[1]
    pos = jnp.arange(seq, dtype=jnp.float32)
    inv_freq = ROPE_THETA ** (-jnp.arange(0, DIFF_HEAD_DIM, 2, dtype=jnp.float32) / DIFF_HEAD_DIM)
    ang = pos[:, None] * inv_freq[None, :]
    cos, sin = jnp.cos(ang), jnp.sin(ang)
    for l in range(DEPTH):
        h = _swiglu(x, ffn_w1[l, 0], ffn_w3[l, 0], ffn_w2[l, 0])
        x = _layernorm(ALPHA * x + 0.5 * h, ln_g[l, 0], ln_b[l, 0])
        h = _mixer(x, l, w_in[l], gate_b[l], sgu_ln_g[l], sgu_ln_b[l], sgu_w[l], sgu_b[l],
                   lam[l], diff_ln_g[l], w_branch[l], w_out[l], cos, sin)
        x = _layernorm(ALPHA * x + h, ln_g[l, 1], ln_b[l, 1])
        h = _swiglu(x, ffn_w1[l, 1], ffn_w3[l, 1], ffn_w2[l, 1])
        x = _layernorm(ALPHA * x + 0.5 * h, ln_g[l, 2], ln_b[l, 2])
    return x


HEAD_DIM = 64
EPS = 1e-6
MLA_HEADS = 8
MLA_NOPE = 64
MLA_ROPE = 32
MLA_V = 64
Q_LORA = 384
KV_LORA = 256
DIL_HEADS = 8
DIL_PATTERNS = ((128, 1), (512, 4), (2048, 16))
DIL_BLOCK = max(w // d for (w, d) in DIL_PATTERNS)
MOBA_HEADS = 16
MOBA_BLOCK = 256
MOBA_TOPK = 3
MOBA_QCHUNK = 16
D_FF_2 = 4 * D_MODEL
PLE_DIM = 256
N_EVEN = (DEPTH + 1) // 2
N_ODD = DEPTH // 2
EVEN_IN = Q_LORA + KV_LORA + MLA_ROPE + 3 * DIL_HEADS * HEAD_DIM
EVEN_MIX = MLA_HEADS * MLA_V + DIL_HEADS * HEAD_DIM
ODD_MIX = MOBA_HEADS * HEAD_DIM


def rms_norm(x, g):
    xf = x.astype(jnp.float32)
    y = xf * lax.rsqrt(jnp.mean(xf * xf, axis=-1, keepdims=True) + EPS)
    return (y * g.astype(jnp.float32)).astype(x.dtype)

def alibi_slopes(n):
    return 2.0 ** (-8.0 * jnp.arange(1, n + 1, dtype=jnp.float32) / n)

def apply_rope(x, positions):
    half = x.shape[-1] // 2
    inv_freq = ROPE_THETA ** (-jnp.arange(half, dtype=jnp.float32) / half)
    ang = positions.astype(jnp.float32)[..., None] * inv_freq
    ang = ang.reshape(ang.shape[:2] + (1,) * (x.ndim - 3) + (half,))
    cos, sin = jnp.cos(ang), jnp.sin(ang)
    xf = x.astype(jnp.float32)
    x1, x2 = xf[..., :half], xf[..., half:]
    return jnp.concatenate([x1 * cos - x2 * sin, x1 * sin + x2 * cos], axis=-1).astype(x.dtype)

def causal_attention_blocks(q, k, v, scale):
    B, S, H, Dk = q.shape
    nq = S // Q_BLOCK
    qb = q.reshape(B, nq, Q_BLOCK, H, Dk).swapaxes(0, 1)
    kpos = jnp.arange(S)

    def one(args):
        qi, i = args
        s = jnp.einsum('bqhd,bkhd->bhqk', qi, k, preferred_element_type=jnp.float32) * scale
        qpos = i * Q_BLOCK + jnp.arange(Q_BLOCK)
        s = jnp.where(kpos[None, :] <= qpos[:, None], s, -jnp.inf)
        pr = jax.nn.softmax(s, axis=-1).astype(v.dtype)
        return jnp.einsum('bhqk,bkhd->bqhd', pr, v)

    out = lax.map(one, (qb, jnp.arange(nq)))
    return out.swapaxes(0, 1).reshape(B, S, H, v.shape[-1])

def dilated_branch(q, k, v, slopes, scale, window, dil):
    B, S, H, Dh = q.shape
    L = S // dil
    nb = -(-L // DIL_BLOCK)
    Lp = nb * DIL_BLOCK
    reach = window // dil

    def to_class(a):
        a = a.reshape(B, L, dil, H, Dh).transpose(0, 2, 1, 3, 4)
        a = jnp.pad(a, ((0, 0), (0, 0), (0, Lp - L), (0, 0), (0, 0)))
        return a.reshape(B, dil, nb, DIL_BLOCK, H, Dh)

    def with_prev(a):
        prev = jnp.pad(a, ((0, 0), (0, 0), (1, 0), (0, 0), (0, 0), (0, 0)))[:, :, :nb]
        return jnp.concatenate([prev, a], axis=3)

    qc = to_class(q)
    kk = with_prev(to_class(k))
    vv = with_prev(to_class(v))
    s = jnp.einsum('bgnqhd,bgnkhd->bghnqk', qc, kk, preferred_element_type=jnp.float32) * scale
    qi = jnp.arange(DIL_BLOCK)[:, None]
    ki = jnp.arange(2 * DIL_BLOCK)[None, :]
    step = DIL_BLOCK + qi - ki
    key_idx = jnp.arange(nb)[:, None, None] * DIL_BLOCK - DIL_BLOCK + ki[None]
    mask = (step >= 0) & (step <= reach) & (key_idx >= 0)
    bias = slopes[:, None, None, None] * (step * dil).astype(jnp.float32)
    s = jnp.where(mask, s - bias, -jnp.inf)
    m = jnp.max(s, axis=-1, keepdims=True)
    e = jnp.exp(s - m)
    den = jnp.sum(e, axis=-1, keepdims=True)
    o = jnp.einsum('bghnqk,bgnkhd->bgnqhd', (e / den).astype(v.dtype), vv)
    lse = (m + jnp.log(den))[..., 0]
    o = o.reshape(B, dil, Lp, H, Dh)[:, :, :L].transpose(0, 2, 1, 3, 4).reshape(B, S, H, Dh)
    lse = lse.reshape(B, dil, H, Lp)[..., :L].transpose(0, 3, 1, 2).reshape(B, S, H)
    return o, lse

def dilated_attention(q, k, v, slopes, scale):
    outs, lses = [], []
    for (w, d) in DIL_PATTERNS:
        o, l = dilated_branch(q, k, v, slopes, scale, w, d)
        outs.append(o)
        lses.append(l)
    wts = jax.nn.softmax(jnp.stack(lses, axis=0), axis=0)
    out = jnp.einsum('pbsh,pbshd->bshd', wts, jnp.stack(outs, axis=0).astype(jnp.float32))
    return out.astype(q.dtype)

def moba_attention(q, k, v, slopes, scale):
    B, S, H, Dh = q.shape
    nb = -(-S // MOBA_BLOCK)
    Sp = nb * MOBA_BLOCK

    def to_blocks(a):
        a = jnp.pad(a, ((0, 0), (0, Sp - S), (0, 0), (0, 0)))
        return a.reshape(B, nb, MOBA_BLOCK, H, Dh).transpose(0, 3, 1, 2, 4)

    kb, vb = to_blocks(k), to_blocks(v)
    k_mean = jnp.mean(kb.astype(jnp.float32), axis=3)
    t = jnp.arange(S)
    own = t // MOBA_BLOCK
    gate = jnp.einsum('bshd,bhnd->bshn', q.astype(jnp.float32), k_mean)
    fully_past = jnp.arange(nb)[None, :] < own[:, None]
    gate = jnp.where(fully_past[None, :, None, :], gate, -jnp.inf)
    n_sel = min(MOBA_TOPK, nb)
    _, sel = lax.top_k(gate, n_sel)
    sel_ok = sel < own[None, :, None, None]
    nc = S // MOBA_QCHUNK

    def chunk(a):
        return a.reshape((B, nc, MOBA_QCHUNK) + a.shape[2:]).swapaxes(0, 1)

    b_ix = jnp.arange(B)[:, None, None, None]
    h_ix = jnp.arange(H)[None, None, :, None]
    k_in = jnp.arange(MOBA_BLOCK)
    n_sel_keys = n_sel * MOBA_BLOCK

    def one(args):
        qi, si, oki, ti = args
        ob = ti[0] // MOBA_BLOCK
        k_own = lax.dynamic_index_in_dim(kb, ob, axis=2, keepdims=False)
        v_own = lax.dynamic_index_in_dim(vb, ob, axis=2, keepdims=False)
        k_sel = kb[b_ix, h_ix, si]
        v_sel = vb[b_ix, h_ix, si]
        s_sel = jnp.einsum('bqhd,bqhjkd->bqhjk', qi, k_sel, preferred_element_type=jnp.float32) * scale
        s_own = jnp.einsum('bqhd,bhkd->bqhk', qi, k_own, preferred_element_type=jnp.float32) * scale
        d_sel = (ti[None, :, None, None, None] - (si[..., None] * MOBA_BLOCK + k_in)).astype(jnp.float32)
        s_sel = jnp.where(oki[..., None], s_sel - slopes[:, None, None] * d_sel, -jnp.inf)
        d_own = ti[:, None] - (ob * MOBA_BLOCK + k_in)[None, :]
        s_own = jnp.where((d_own >= 0)[None, :, None, :],
                          s_own - slopes[None, None, :, None] * d_own.astype(jnp.float32)[None, :, None, :],
                          -jnp.inf)
        s_all = jnp.concatenate([s_sel.reshape(s_sel.shape[:3] + (n_sel_keys,)), s_own], axis=-1)
        probs = jax.nn.softmax(s_all, axis=-1).astype(v.dtype)
        p_sel = probs[..., :n_sel_keys].reshape(s_sel.shape)
        p_own = probs[..., n_sel_keys:]
        return (jnp.einsum('bqhjk,bqhjkd->bqhd', p_sel, v_sel)
                + jnp.einsum('bqhk,bhkd->bqhd', p_own, v_own))

    out = lax.map(one, (chunk(q), chunk(sel), chunk(sel_ok), t.reshape(nc, MOBA_QCHUNK)))
    return out.swapaxes(0, 1).reshape(B, S, H, Dh)

def even_mixer(hn, positions, w_in, cq_norm, ckv_norm, w_uq, w_ukv, qn_nope, qn_rope,
               kn_nope, kn_rope, dil_qn, dil_kn, w_out):
    B, S, _ = hn.shape
    z = hn @ w_in
    o1 = Q_LORA
    o2 = o1 + KV_LORA
    o3 = o2 + MLA_ROPE
    dw = DIL_HEADS * HEAD_DIM
    c_q = rms_norm(z[..., :o1], cq_norm)
    c_kv = rms_norm(z[..., o1:o2], ckv_norm)
    q = (c_q @ w_uq).reshape(B, S, MLA_HEADS, MLA_NOPE + MLA_ROPE)
    q_nope = rms_norm(q[..., :MLA_NOPE], qn_nope)
    q_rope = apply_rope(rms_norm(q[..., MLA_NOPE:], qn_rope), positions)
    kv = (c_kv @ w_ukv).reshape(B, S, MLA_HEADS, MLA_NOPE + MLA_V)
    k_nope = rms_norm(kv[..., :MLA_NOPE], kn_nope)
    v_a = kv[..., MLA_NOPE:]
    k_rope = apply_rope(rms_norm(z[..., o2:o3], kn_rope), positions)
    k_rope = jnp.broadcast_to(k_rope[:, :, None, :], (B, S, MLA_HEADS, MLA_ROPE))
    q_a = jnp.concatenate([q_nope, q_rope], axis=-1)
    k_a = jnp.concatenate([k_nope, k_rope], axis=-1)
    out_a = causal_attention_blocks(q_a, k_a, v_a, (MLA_NOPE + MLA_ROPE) ** -0.5)
    q_b = rms_norm(z[..., o3:o3 + dw].reshape(B, S, DIL_HEADS, HEAD_DIM), dil_qn)
    k_b = rms_norm(z[..., o3 + dw:o3 + 2 * dw].reshape(B, S, DIL_HEADS, HEAD_DIM), dil_kn)
    v_b = z[..., o3 + 2 * dw:o3 + 3 * dw].reshape(B, S, DIL_HEADS, HEAD_DIM)
    out_b = dilated_attention(q_b, k_b, v_b, alibi_slopes(DIL_HEADS), HEAD_DIM ** -0.5)
    mixed = jnp.concatenate([out_a.reshape(B, S, MLA_HEADS * MLA_V),
                             out_b.reshape(B, S, dw)], axis=-1)
    return mixed @ w_out

def odd_mixer(hn, w_in, qn, kn, w_out):
    B, S, _ = hn.shape
    z = (hn @ w_in).reshape(B, S, 3, MOBA_HEADS, HEAD_DIM)
    q = rms_norm(z[:, :, 0], qn)
    k = rms_norm(z[:, :, 1], kn)
    v = z[:, :, 2]
    o = moba_attention(q, k, v, alibi_slopes(MOBA_HEADS), HEAD_DIM ** -0.5)
    return o.reshape(B, S, ODD_MIX) @ w_out

def second_inputs(seed: int = 0) -> dict:
    key = jax.random.key(seed)
    ks = iter(jax.random.split(key, 32))

    def w(shape, fan_in):
        return jax.random.normal(next(ks), shape, jnp.float32) * (fan_in ** -0.5)

    def gain(shape):
        return 1.0 + 0.05 * jax.random.normal(next(ks), shape, jnp.float32)

    x = jax.random.normal(next(ks), (BATCH, SEQ, D_MODEL), jnp.float32)
    p = jax.random.normal(next(ks), (DEPTH, BATCH, SEQ, PLE_DIM), jnp.float32)
    positions = jnp.broadcast_to(jnp.arange(SEQ, dtype=jnp.int32), (BATCH, SEQ))
    return {
        'x': x,
        'p': p,
        'positions': positions,
        'e_w_in': w((N_EVEN, D_MODEL, EVEN_IN), D_MODEL),
        'e_cq_norm': gain((N_EVEN, Q_LORA)),
        'e_ckv_norm': gain((N_EVEN, KV_LORA)),
        'e_w_uq': w((N_EVEN, Q_LORA, MLA_HEADS * (MLA_NOPE + MLA_ROPE)), Q_LORA),
        'e_w_ukv': w((N_EVEN, KV_LORA, MLA_HEADS * (MLA_NOPE + MLA_V)), KV_LORA),
        'e_qn_nope': gain((N_EVEN, MLA_NOPE)),
        'e_qn_rope': gain((N_EVEN, MLA_ROPE)),
        'e_kn_nope': gain((N_EVEN, MLA_NOPE)),
        'e_kn_rope': gain((N_EVEN, MLA_ROPE)),
        'e_dil_qn': gain((N_EVEN, HEAD_DIM)),
        'e_dil_kn': gain((N_EVEN, HEAD_DIM)),
        'e_w_out': w((N_EVEN, EVEN_MIX, D_MODEL), EVEN_MIX),
        'o_w_in': w((N_ODD, D_MODEL, 3 * ODD_MIX), D_MODEL),
        'o_qn': gain((N_ODD, HEAD_DIM)),
        'o_kn': gain((N_ODD, HEAD_DIM)),
        'o_w_out': w((N_ODD, ODD_MIX, D_MODEL), ODD_MIX),
        'mix_norm': gain((DEPTH, D_MODEL)),
        'ff_norm': gain((DEPTH, D_MODEL)),
        'w_ff1': w((DEPTH, D_MODEL, D_FF_2), D_MODEL),
        'w_ff2': w((DEPTH, D_FF_2, D_MODEL), D_FF_2),
        'ple_norm': gain((DEPTH, D_MODEL)),
        'w_ple_gate': w((DEPTH, D_MODEL, D_MODEL), D_MODEL),
        'w_ple_proj': w((DEPTH, PLE_DIM, D_MODEL), PLE_DIM),
    }

def second_block(x, p, positions, e_w_in, e_cq_norm, e_ckv_norm, e_w_uq, e_w_ukv, e_qn_nope,
              e_qn_rope, e_kn_nope, e_kn_rope, e_dil_qn, e_dil_kn, e_w_out, o_w_in, o_qn,
              o_kn, o_w_out, mix_norm, ff_norm, w_ff1, w_ff2, ple_norm, w_ple_gate, w_ple_proj):
    h = x
    for i in range(DEPTH):
        j = i // 2
        hn = rms_norm(h, mix_norm[i])
        if i % 2 == 0:
            mix = even_mixer(hn, positions, e_w_in[j], e_cq_norm[j], e_ckv_norm[j], e_w_uq[j],
                             e_w_ukv[j], e_qn_nope[j], e_qn_rope[j], e_kn_nope[j], e_kn_rope[j],
                             e_dil_qn[j], e_dil_kn[j], e_w_out[j])
        else:
            mix = odd_mixer(hn, o_w_in[j], o_qn[j], o_kn[j], o_w_out[j])
        h = h + mix
        u = jax.nn.relu(rms_norm(h, ff_norm[i]) @ w_ff1[i])
        h = h + (u * u) @ w_ff2[i]
        g = jax.nn.sigmoid(rms_norm(h, ple_norm[i]) @ w_ple_gate[i])
        h = h + g * (p[i] @ w_ple_proj[i])
    return h


def setup_inputs(seed=0):
    out = dict(first_inputs(seed))
    for name, value in second_inputs(seed + 1).items():
        if name != "x":
            out[name + "_2"] = value
    return out


def reference(
    x, w_in, gate_b, sgu_ln_g, sgu_ln_b, sgu_w, sgu_b, lam, diff_ln_g, w_branch, w_out, ffn_w1,
    ffn_w3, ffn_w2, ln_g, ln_b, p_2, positions_2, e_w_in_2, e_cq_norm_2, e_ckv_norm_2, e_w_uq_2,
    e_w_ukv_2, e_qn_nope_2, e_qn_rope_2, e_kn_nope_2, e_kn_rope_2, e_dil_qn_2, e_dil_kn_2,
    e_w_out_2, o_w_in_2, o_qn_2, o_kn_2, o_w_out_2, mix_norm_2, ff_norm_2, w_ff1_2, w_ff2_2,
    ple_norm_2, w_ple_gate_2, w_ple_proj_2,
):
    x = first_block(
        x, w_in, gate_b, sgu_ln_g, sgu_ln_b, sgu_w, sgu_b, lam, diff_ln_g, w_branch, w_out,
        ffn_w1, ffn_w3, ffn_w2, ln_g, ln_b,
    )
    return second_block(
        x, p_2, positions_2, e_w_in_2, e_cq_norm_2, e_ckv_norm_2, e_w_uq_2, e_w_ukv_2,
        e_qn_nope_2, e_qn_rope_2, e_kn_nope_2, e_kn_rope_2, e_dil_qn_2, e_dil_kn_2, e_w_out_2,
        o_w_in_2, o_qn_2, o_kn_2, o_w_out_2, mix_norm_2, ff_norm_2, w_ff1_2, w_ff2_2,
        ple_norm_2, w_ple_gate_2, w_ple_proj_2,
    )


_drawn_inputs = setup_inputs


def setup_inputs(seed=0):
    import zlib

    import numpy as np

    out = dict(_drawn_inputs(seed))
    spreads = {}
    factors = {'gate_b': 8.0,
     'sgu_ln_g': 8.0,
     'sgu_ln_b': 8.0,
     'sgu_b': 8.0,
     'lam': 3.167,
     'diff_ln_g': 8.0,
     'e_cq_norm_2': 8.0,
     'e_ckv_norm_2': 5.27,
     'e_qn_nope_2': 8.0,
     'e_qn_rope_2': 8.0,
     'e_kn_nope_2': 8.0,
     'e_kn_rope_2': 8.0,
     'e_dil_qn_2': 5.787,
     'e_dil_kn_2': 5.672,
     'o_qn_2': 8.0,
     'o_kn_2': 8.0,
     'ple_norm_2': 19.472}
    for name, (base, spread) in spreads.items():
        noise = np.random.default_rng([zlib.crc32(name.encode()), seed]).standard_normal(out[name].shape)
        drawn = base * np.exp(spread * noise) if base else spread * noise
        out[name] = jnp.asarray(drawn.astype(out[name].dtype))
    for name, factor in factors.items():
        out[name] = (out[name] * factor).astype(out[name].dtype)
    return out
```

```python
from contextlib import ExitStack

import numpy as np

import concourse.bass as bass
from concourse import mybir

F32 = mybir.dt.float32
F32R = mybir.dt.float32r
I32 = mybir.dt.int32
ALU = mybir.AluOpType
ACT = mybir.ActivationFunctionType
AX_X = mybir.AxisListType.X

P = 128
S = 256
NT = S // P
D = 1024
KT = D // P
DEPTH = 2
RING = 4
UNIT = 2048
NC = 512
NEG = -1.0e30

F1 = 2816
FB = 256
NF = F1 // FB
H1 = 8
HD = 64
ALPHA = (2.0 * DEPTH) ** 0.25
LN_EPS = 1e-5
CH = 20
IN_COLS = [1024, 1536, 0, 512, 2048, 2560, 3072, 3584, 4096, 4608, 5120, 5632, 6144, 6656]
HEAD_UNITS = [[20, 21], [22, 23], [24, 25], [26, 27], [28], [29], [30], [31]]

ACC_LAYER = 2 + CH // 2
SLOT_LAYER = tuple((2 * NF if s < 3 else 0) + CH // 2 for s in range(RING))
AUX_LAYER = tuple((2 * NF if b < 3 else 0) + 6 + 2 + 1 + (1 if b < 2 else 0) + H1 for b in range(4))

EPS = 1e-6
F2 = 4096
FB2 = 512
NF2 = F2 // FB2
Q_LORA, KV_LORA, ROPE2 = 384, 256, 32
MLA_H, MLA_N, MLA_V = 8, 64, 64
MLA_D = MLA_N + ROPE2
DIL_H = 8
MOBA_H = 16
EVEN_GAINS = [("e_cq_norm_2", Q_LORA), ("e_ckv_norm_2", KV_LORA), ("e_qn_nope_2", MLA_N),
              ("e_qn_rope_2", ROPE2), ("e_kn_nope_2", MLA_N), ("e_kn_rope_2", ROPE2),
              ("e_dil_qn_2", HD), ("e_dil_kn_2", HD)]
ODD_GAINS = [("o_qn_2", HD), ("o_kn_2", HD)]
PI = float(np.pi)
RSQRT_MAGIC = float(0x5F3759DF)


def jobs_of_block2():
    jobs = []

    def chunk(name, w, row0, col0, cols, kts, split):
        units = [(k0, k1, cols, w, row0 + k0 * P, col0) for k0, k1 in split]
        jobs.append(dict(name=name, units=units, wide=False, cols=cols, kts=kts))

    full = [(0, 4), (4, 8)]
    chunk("cq", "e_w_in_2", 0, 0, Q_LORA, KT, full)
    chunk("ckv", "e_w_in_2", 0, Q_LORA, KV_LORA + ROPE2, KT, full)
    for k, name in enumerate(("qb", "kb", "vb")):
        chunk(name, "e_w_in_2", 0, Q_LORA + KV_LORA + ROPE2 + k * NC, NC, KT, full)
    for k in range(2):
        chunk(f"uq{k}", "e_w_uq_2", 0, k * 384, 384, 3, [(0, 3)])
    for k in range(2):
        chunk(f"ukv{k}", "e_w_ukv_2", 0, k * NC, NC, 2, [(0, 2)])
    for k in range(2):
        chunk(f"eout{k}", "e_w_out_2", 0, k * NC, NC, KT, full)

    def ff_and_side(i):
        jobs.append(dict(name=f"ff{i}", units=None, wide=True, i=i))
        for k in range(2):
            chunk(f"g{i}{k}", "w_ple_gate_2", i * D, k * NC, NC, KT, full)
        jobs.append(dict(name=f"side{i}", units=[(0, 2, D, "w_ple_proj_2", i * 256, 0)], wide=True, kts=2))

    ff_and_side(0)
    for k in range(6):
        chunk(f"z{k}", "o_w_in_2", 0, k * NC, NC, KT, full)
    for k in range(2):
        chunk(f"oout{k}", "o_w_out_2", 0, k * NC, NC, KT, full)
    ff_and_side(1)
    u, acc, par, slots = 0, [0, 0], 0, [0] * RING
    for g in jobs:
        g["u0"] = u
        g["slots"] = []
        if g["units"] is None:
            s0 = u % RING
            g["s0"], g["n0"] = s0, list(slots)
            for s in range(RING):
                slots[s] += NF2
            g["nu"] = NF2 * RING
            u += RING * NF2
        else:
            for _ in g["units"]:
                g["slots"].append((u % RING, slots[u % RING]))
                slots[u % RING] += 1
                u += 1
            g["nu"] = len(g["units"])
        if g["wide"]:
            g["acc"] = [(0, acc[0]), (1, acc[1])]
            acc = [acc[0] + 1, acc[1] + 1]
        else:
            g["acc"] = [(par, acc[par])]
            acc[par] += 1
            par = 1 - par
    return jobs


JOBS = jobs_of_block2()
JOB = {g["name"]: g for g in JOBS}


def job_of_unit(u):
    return next(g for g in JOBS if g["u0"] <= u < g["u0"] + g["nu"])


def units_after(g):
    end = g["u0"] + g["nu"]
    last = JOBS[-1]["u0"] + JOBS[-1]["nu"]
    if g["units"] is None:
        first = end + 2
    else:
        first = g["u0"] + RING
    return [u for u in range(first, min(end + RING, last)) if not in_ff(u)]


def in_ff(u):
    g = job_of_unit(u)
    return g["units"] is None and u - g["u0"] >= 2


class Uses:

    def __init__(self, per):
        self.per = per
        self.k = 0

    def at(self, layer):
        return layer * self.per + self.k

    def take(self, layer):
        n = self.at(layer)
        self.k += 1
        return n

    def layer_ends(self):
        assert self.k == self.per, (self.k, self.per)
        self.k = 0


def rows(ap, row0, n, col0, nc):
    r = ap[row0:row0 + n, :] if isinstance(row0, int) else ap[bass.ds(row0, n), :]
    r = r[:, col0:col0 + nc] if isinstance(col0, int) else r[:, bass.ds(col0, nc)]
    return r.rearrange("(k p) n -> p k n", p=P)


def slope(h, n):
    return float(np.float32(2.0) ** np.float32(-8.0 * (h + 1) / n))


def build(nc, a, out, stop=None):
    ctx = ExitStack()
    with ctx:
        def sb(name, shape, dt=F32):
            return ctx.enter_context(nc.sbuf_tensor(name, shape, dt))

        def sem(name):
            return ctx.enter_context(nc.semaphore(name))

        raw = sb("w_raw", [P, RING, UNIT])
        whi = sb("w_high", [P, RING, UNIT], F32R)
        wlo = sb("w_low", [P, RING, UNIT], F32R)
        x = sb("x_res", [P, NT, D])
        xTh = sb("xT_high", [P, KT, S], F32R)
        xTl = sb("xT_low", [P, KT, S], F32R)
        yTh = sb("yT_high", [P, KT, S], F32R)
        yTl = sb("yT_low", [P, KT, S], F32R)
        bv = sb("buf_v", [P, NT, D])
        bu = sb("buf_u", [P, NT, D])
        bq = sb("buf_q", [P, NT, D])
        bk = sb("buf_k", [P, NT, D])
        bval = sb("buf_val", [P, NT, D])
        bg = sb("buf_gates", [P, 2, NT, D])
        ln_par = sb("ln_param", [P, 2, D])
        mix_par = sb("mix_param", [P, 2, D])
        ident = sb("ident", [P, P])
        tri = sb("tri", [P, P])
        causal = sb("causal", [P, 3 * P])
        rope = sb("rope_tab", [P, 2, NT, HD])
        lam_init = sb("lam_init", [P, 2])
        diff_g = sb("diff_g", [P, 2 * HD])
        sgu_bT = sb("sgu_bT", [P, 8])
        aT = sb("probs_T", [P, 3 * P])
        junk = sb("junk", [P, 4])
        stat = sb("stat", [P, NT, 2, 6])
        mv = sb("mean_var", [P, NT, 2])
        nv = sb("newton_v", [P, 32])
        ny = sb("newton_y", [P, 32])
        nz = sb("newton_t", [P, 32])
        lam_t = sb("lam_t", [P, 4])
        neg_lam = sb("neg_lam", [P, 1])
        rmax = sb("row_max", [P, 2, 4])
        rsum = sb("row_sum", [P, 2, 4])
        rinv = sb("row_inv", [P, 2, 4])
        ssq = sb("sum_sq", [P, NT, H1])
        dist = sb("neg_distance", [P, 2, 3 * P])
        times = sb("pattern_count", [P, 3 * P])
        pos_i = sb("pos_i", [P, NT], I32)
        rope2 = sb("rope2", [P, 2, NT, ROPE2])
        k_rope = sb("k_rope", [P, NT, ROPE2])

        def flat(t):
            return t[:, :, :].rearrange("p t d -> p (t d)")

        bg_flat = bg[:, :, :, :].rearrange("p a t d -> p (a t d)")
        ang = flat(bval)[:, 0:P].rearrange("p (k t c) -> p k t c", k=4, t=NT)
        inv_freq = flat(bval)[:, P:P + ROPE2 // 2]
        lam_w = bg_flat[:, 2 * D:2 * D + 4 * HD]
        act_b = flat(bk)[:, 0:NT * NC].rearrange("p (t f) -> p t f", t=NT)
        gate_b = flat(bk)[:, NT * NC:2 * NT * NC].rearrange("p (t f) -> p t f", t=NT)
        sgu_raw = bval[:, 0, :].rearrange("p (g r) -> p g r", g=8)
        wT = bg_flat[:, 0:D].rearrange("p (g r) -> p g r", g=8)
        qT = flat(bv).rearrange("p (h s) -> p h s", s=S)
        kT = flat(bq).rearrange("p (h s) -> p h s", s=S)
        SE = flat(bk)[:, 0:4 * 3 * P].rearrange("p (b m c) -> p b m c", b=2, m=2)
        pa = flat(bk)[:, 4 * 3 * P:5 * 3 * P]
        sq_junk = flat(bk)[:, 15 * P:16 * P]

        acc = ctx.enter_context(nc.psum_tensor("acc", [P, 2, NT, NC], F32))
        aux = ctx.enter_context(nc.psum_tensor("aux", [P, 4, NC], F32))

        slot_full = [sem(f"slot_full{s}") for s in range(RING)]
        slot_hi = [sem(f"slot_hi{s}") for s in range(RING)]
        slot_lo = [sem(f"slot_lo{s}") for s in range(RING)]
        acc_full = [sem("acc_full0"), sem("acc_full1")]
        acc_read = [sem("acc_read0"), sem("acc_read1")]
        aux_full = [sem(f"aux_full{b}") for b in range(4)]
        aux_read = [sem(f"aux_read{b}") for b in range(4)]
        t_hi = sem("t_hi")
        act_done = sem("act_done")
        x_ready = sem("x_ready")
        tanh_done = sem("tanh_done")
        vn_ready = sem("vn_ready")
        roped = sem("roped")
        s_ready = sem("s_ready")
        e_ready = sem("e_ready")
        a_ready = sem("a_ready")
        hb_ready = sem("hb_ready")
        m_ready = sem("m_ready")
        lam_dot = sem("lam_dot")
        lam_exp = sem("lam_exp")
        const_in = sem("const_in")
        x_in = sem("x_in")
        ln_in = sem("ln_in")
        ln_free = sem("ln_free")
        mix_in = sem("mix_in")
        mix_free = sem("mix_free")
        small_in = sem("small_in")
        small_free = sem("small_free")
        gains_in = sem("gains_in")
        gains_free = sem("gains_free")
        side_in = sem("side_in")
        sumsq = sem("sumsq")
        xn_ready = sem("xn_ready")
        low_ready = sem("low_ready")
        heads_ready = sem("heads_ready")
        angles = sem("angles")
        sines = sem("sines")
        o_ready = sem("o_ready")
        out_done = sem("out_done")

        block = ctx.enter_context(nc.Block())
        L2 = DEPTH

        def cast(ap):
            return ap.bitcast(F32)

        def slot_n2(s, n):
            return L2 * SLOT_LAYER[s] + n

        def acc_n2(p, n):
            return L2 * ACC_LAYER + n

        def mixer_n(l, u):
            s = u % RING
            return l * SLOT_LAYER[s] + (NF if s < 3 else 0) + u // RING

        @block.sync
        def _(sp):
            sp.dma_start(x[:], a["x"].rearrange("b (t p) d -> p (b t) d", p=P)).then_inc(x_in, 16)

            def load(s, n, parts):
                sp.wait_ge(slot_lo[s], n + 1)
                for dst, src in parts:
                    sp.dma_start(dst, src).then_inc(slot_full[s], 32 // len(parts))

            def ffn1(l, which):
                n0 = l * SLOT_LAYER[0] + (NF + CH // 2) * which
                with sp.Fori(0, NF) as i:
                    for j in range(2):
                        dst = raw[:, j, :].rearrange("p (m k n) -> p m k n", m=2, k=4)
                        r0 = (l * 2 + which) * D + j * 4 * P
                        load(j, n0 + i, [(dst[:, 0], rows(a["ffn_w1"], r0, 4 * P, i * FB, FB)),
                                         (dst[:, 1], rows(a["ffn_w3"], r0, 4 * P, i * FB, FB))])
                    dst = raw[:, 2, :].rearrange("p (k n) -> p k n", k=2)
                    load(2, n0 + i, [(dst, rows(a["ffn_w2"], (l * 2 + which) * F1 + i * FB, FB, 0, D))])

            with sp.Fori(0, DEPTH) as l:
                ffn1(l, 0)
                for u in range(2 * CH):
                    c, j = divmod(u, 2)
                    if u in (4, 5, 36, 37):
                        w = a["w_in" if c == 2 else "w_out"]
                        src = tuple(rows(w, l * D + (4 * j + k) * P, 2 * P, 0, NC) for k in (2, 0))
                    elif c < 14:
                        src = rows(a["w_in"], l * D + j * 4 * P, 4 * P, IN_COLS[c], NC)
                    elif c < 18:
                        src = rows(a["w_branch"], (l * 2 + (c - 14) // 2) * D + j * 4 * P, 4 * P,
                                   (c % 2) * NC, NC)
                    else:
                        src = rows(a["w_out"], l * D + j * 4 * P, 4 * P, (c % 2) * NC, NC)
                    dst = raw[:, u % RING, :].rearrange("p (k n) -> p k n", k=4)
                    if isinstance(src, tuple):
                        parts = [(dst[:, 2:4], src[0]), (dst[:, 0:2], src[1])]
                    else:
                        parts = [(dst, src)]
                    load(u % RING, mixer_n(l, u), parts)
                ffn1(l, 1)
            for g in (JOBS if stop is None else JOBS[:1]):
                if g["units"] is None:
                    with sp.Fori(0, NF2) as i:
                        for j in range(RING):
                            s = (g["s0"] + j) % RING
                            k = 4 if j < 2 else 2
                            dst = raw[:, s, :].rearrange("p (k n) -> p k n", k=k)
                            if j < 2:
                                src = rows(a["w_ff1_2"], g["i"] * D + j * 4 * P, 4 * P, i * FB2, FB2)
                            else:
                                src = rows(a["w_ff2_2"], g["i"] * F2 + i * FB2 + (j - 2) * 2 * P, 2 * P, 0, D)
                            load(s, slot_n2(s, g["n0"][s]) + i, [(dst, src)])
                else:
                    for (s, n), (k0, k1, cols, w, r0, c0) in zip(g["slots"], g["units"]):
                        dst = raw[:, s, 0:(k1 - k0) * cols].rearrange("p (k n) -> p k n", k=k1 - k0)
                        load(s, slot_n2(s, n), [(dst, rows(a[w], r0, (k1 - k0) * P, c0, cols))])
            sp.wait_ge(x_ready, 2 + 6 * DEPTH + (6 if stop is None else 0))
            sp.dma_start(out.rearrange("b (t p) d -> p (b t) d", p=P), x[:]).then_inc(out_done, 16)
            sp.wait_ge(out_done, 16)

        @block.gpsimd
        def _(pool):
            consts = ((ident[:], a["c_ident"]), (tri[:], a["c_tri"]), (causal[:], a["c_causal"]),
                      (rope[:], a["c_rope"]), (dist[:], a["c_dist"]),
                      (times[:], a["c_times"]), (inv_freq, a["c_inv_freq"]))
            for dst, src in consts:
                pool.dma_start(dst, src).then_inc(const_in, 16)
            with nc.allow_non_contiguous_dma(reason="256 positions onto partitions"):
                pool.dma_start(pos_i[:], a["positions_2"].rearrange("b (t p) -> p (b t)", p=P))\
                    .then_inc(const_in, 16)

            def norm_params(l, k):
                n = l * 3 + k
                pool.wait_ge(ln_free, n + 1)
                for w, name in enumerate(("ln_g", "ln_b")):
                    pool.dma_start(ln_par[:, w, :], a[name][bass.ds(n, 1), :].partition_broadcast(P))\
                        .then_inc(ln_in, 16)

            with pool.Fori(0, DEPTH) as l:
                norm_params(l, 0)
                pool.wait_ge(small_free, l + 1)
                pool.dma_start(sgu_raw, a["sgu_w"][bass.ds(l * 8, 8), :, :].rearrange("g t r -> t g r"))\
                    .then_inc(small_in, 16)
                with nc.allow_non_contiguous_dma(reason="1024 biases onto partitions"):
                    pool.dma_start(sgu_bT[:], a["sgu_b"][bass.ds(l * 8, 8), :].rearrange("g t -> t g"))\
                        .then_inc(small_in, 16)
                pool.dma_start(diff_g[:], a["diff_ln_g"][bass.ds(l, 1), :].partition_broadcast(P))\
                    .then_inc(small_in, 16)
                pool.dma_start(lam_w, a["lam"][bass.ds(l, 1), :].partition_broadcast(P))\
                    .then_inc(small_in, 16)
                pool.dma_start(lam_init[:], a["c_lam"][bass.ds(l, 1), :].partition_broadcast(P))\
                    .then_inc(small_in, 16)
                pool.wait_ge(mix_free, 2 * l + 1)
                for w, name in enumerate(("sgu_ln_g", "sgu_ln_b")):
                    pool.dma_start(mix_par[:, w, :], a[name][bass.ds(l, 1), :].partition_broadcast(P))\
                        .then_inc(mix_in, 16)
                norm_params(l, 1)
                pool.wait_ge(mix_free, 2 * l + 2)
                for w in range(2):
                    pool.dma_start(mix_par[:, w, :], a["gate_b"][bass.ds(l * 2 + w, 1), :].partition_broadcast(P))\
                        .then_inc(mix_in, 16)
                norm_params(l, 2)
            if stop == 1:
                return
            pool.wait_ge(ln_free, 3 * DEPTH + 1)
            n = 0
            for i in range(2):
                for name, n_rms in (("mix_norm_2", 0), ("ff_norm_2", 1), ("ple_norm_2", 2)):
                    pool.wait_ge(ln_free, 3 * DEPTH + 1 + n)
                    pool.dma_start(ln_par[:, 0, :], a[name][i:i + 1, :].partition_broadcast(P))\
                        .then_inc(ln_in, 32)
                    n += 1
                    if n_rms == 0:
                        c0 = 0
                        gains = EVEN_GAINS if i == 0 else ODD_GAINS
                        if i == 1:
                            pool.wait_ge(gains_free, 1)
                        for gname, w in gains:
                            pool.dma_start(ln_par[:, 1, c0:c0 + w], a[gname].partition_broadcast(P))\
                                .then_inc(gains_in, 16)
                            c0 += w
                    if n_rms == 1:
                        pool.wait_ge(ln_free, 3 * DEPTH + 1 + n)
                        pool.dma_start(bq[:, :, 0:256],
                                       a["p_2"][i * S:(i + 1) * S, :].rearrange("(t p) n -> p t n", p=P))\
                            .then_inc(side_in, 16)

        @block.tensor
        def _(pe):
            n_acc = [Uses(ACC_LAYER), Uses(ACC_LAYER)]
            n_aux = [Uses(k) for k in AUX_LAYER]

            pe.wait_ge(const_in, 8 * 16)

            def aux_wait(l, b):
                pe.wait_ge(aux_read[b], n_aux[b].at(l) + 1)

            def aux_all(l, banks=range(4)):
                for b in banks:
                    aux_wait(l, b)

            def aux_end(b, last):
                last.then_inc(aux_full[b], 1)
                n_aux[b].k += 1

            def products(dst, tiles, k_first, k_last, lh, ll, t, rh, rl):
                tok = slice(t * P, (t + 1) * P)
                for kt, j in tiles:
                    for q, (lhs, rhs) in enumerate(((lh, rh), (lh, rl), (ll, rh))):
                        last = nc.tensor.matmul(dst, lhs[:, kt, tok], rhs(j),
                                                start=(kt == k_first and q == 0),
                                                stop=(kt == k_last and q == 2))
                return last

            def transpose_x(l, src):
                for t in range(NT):
                    for half in range(2):
                        b = 2 * t + half
                        aux_wait(l, b)
                        for k in range(4):
                            kt = half * 4 + k
                            last = nc.tensor.transpose(aux[:, b, k * P:(k + 1) * P],
                                                       src[:, t, kt * P:(kt + 1) * P], ident[:])
                        aux_end(b, last)

            def feed_forward(l, slot0, which_slots, hid_view, n_f, iters):
                aux0 = [n_aux[b].at(l) for b in range(4)]
                t_banks = [2] if n_f == 2 else [2, 3]
                down_slots = which_slots[2:]

                def hidden(i):
                    for j in range(2):
                        s = which_slots[j]
                        pe.wait_ge(slot_lo[s], slot0(s) + i + 2)
                        vh, vl = hid_view(whi[:, s, :]), hid_view(wlo[:, s, :])
                        for t in range(NT):
                            if j == 0:
                                pe.wait_ge(aux_read[t], aux0[t] + i + 1)
                            dst = aux[:, t, :]
                            if n_f == 2:
                                dst = dst.rearrange("p (m n) -> p m n", m=2)
                            last = products(dst, [(4 * j + k, k) for k in range(4)], 0, KT - 1,
                                            xTh, xTl, t, vh, vl)
                            if j == 1:
                                last.then_inc(aux_full[t], 1)

                def transposes(i):
                    for t in range(NT):
                        pe.wait_ge(aux_read[t], aux0[t] + i + 2)
                    for b in t_banks:
                        pe.wait_ge(aux_read[b], aux0[b] + i + 1)
                        for f in range(2):
                            for t in range(NT):
                                f0 = ((b - 2) * 2 + f) * P
                                last = nc.tensor.transpose(aux[:, b, (2 * f + t) * P:(2 * f + t + 1) * P],
                                                           gate_b[:, t, f0:f0 + P], ident[:])
                        last.then_inc(aux_full[b], 1)

                def down(i, first, final):
                    if first:
                        for p in range(2):
                            pe.wait_ge(acc_read[p], n_acc[p].at(l) + 1)
                    for q, s in enumerate(down_slots):
                        pe.wait_ge(slot_lo[s], slot0(s) + i + 2)
                        pe.wait_ge(aux_read[2 + q], aux0[2 + q] + i + 2)
                        vh, vl = (w[:, s, :].rearrange("p (k n) -> p k n", k=2) for w in (whi, wlo))
                        for half in range(2):
                            col = slice(half * NC, (half + 1) * NC)
                            for t in range(NT):
                                last = products(acc[:, half, t, :], [(2 * q + k, k) for k in range(2)],
                                                0 if first else -1, n_f - 1 if final else -1, yTh, yTl, t,
                                                lambda k: vh[:, k, col], lambda k: vl[:, k, col])
                            if final and q == len(down_slots) - 1:
                                last.then_inc(acc_full[half], 1)

                hidden(0)
                transposes(0)
                hidden(1)
                down(0, True, False)
                transposes(1)
                with pe.Fori(2, iters) as i:
                    hidden(i)
                    down(i - 1, False, False)
                    transposes(i)
                down(iters - 1, False, True)
                for b in [0, 1, *t_banks]:
                    n_aux[b].k += iters
                for p in range(2):
                    n_acc[p].k += 1

            def ffn1(l, which):
                def view(w):
                    v = w.rearrange("p (m k n) -> p m k n", m=2, k=4)
                    return lambda k: v[:, :, k, :]

                feed_forward(l, lambda s: l * SLOT_LAYER[s] + (NF + CH // 2) * which, [0, 1, 2], view, 2, NF)

            def chunk_unit(l, u, lh, ll):
                c, j = divmod(u, 2)
                s, p = u % RING, c % 2
                pe.wait_ge(slot_lo[s], mixer_n(l, u) + 2)
                if j == 0:
                    pe.wait_ge(acc_read[p], n_acc[p].take(l) + 1)
                vh, vl = (w[:, s, :].rearrange("p (k n) -> p k n", k=4) for w in (whi, wlo))
                for t in range(NT):
                    last = products(acc[:, p, t, :], [(4 * j + k, k) for k in range(4)], 0, KT - 1, lh, ll, t,
                                    lambda k: vh[:, k, :], lambda k: vl[:, k, :])
                if j == 1:
                    last.then_inc(acc_full[p], 1)

            def chunk(l, c, lh=xTh, ll=xTl):
                chunk_unit(l, 2 * c, lh, ll)
                chunk_unit(l, 2 * c + 1, lh, ll)

            def transpose_heads(l, src, n, width=P, banks=range(4), heads=2):
                for q, b in enumerate(banks):
                    aux_wait(l, b)
                    for k in range(heads):
                        for t in range(NT):
                            h = heads * q + k
                            last = nc.tensor.transpose(aux[0:width, b, (2 * k + t) * P:(2 * k + t + 1) * P],
                                                       src(t, h), ident[:])
                    aux_end(b, last)

            def scores(l, h):
                for m in range(2):
                    aux_wait(l, m)
                    d = slice(m * HD, (m + 1) * HD)
                    nc.tensor.matmul(aux[:, m, 0:P], qT[d, h, 0:P], kT[d, h, 0:P], start=True, stop=True)
                    last = nc.tensor.matmul(aux[:, m, P:3 * P], qT[d, h, P:S], kT[d, h, 0:S],
                                            start=True, stop=True)
                    aux_end(m, last)

            def prob_transposes(l, src):
                aux_wait(l, 2)
                for k in range(3):
                    last = nc.tensor.transpose(aux[:, 2, k * P:(k + 1) * P], src[:, k * P:(k + 1) * P], ident[:])
                aux_end(2, last)

            def values(l, v, width):
                aux_wait(l, 2)
                aux_wait(l, 3)
                nc.tensor.matmul(aux[:, 3, 0:width], aT[:, 0:P], v[0], start=True, stop=True)
                o1 = aux[:, 3, width:2 * width]
                nc.tensor.matmul(o1, aT[:, P:2 * P], v[0], start=True, stop=False)
                last = nc.tensor.matmul(o1, aT[:, 2 * P:3 * P], v[1], start=False, stop=True)
                aux_end(3, last)

            def mixer(l):
                pe.wait_ge(x_ready, 6 * l + 4)
                transpose_x(l, x)
                aux_all(l)
                chunk(l, 0)
                chunk(l, 1)
                pe.wait_ge(small_in, 80 * l + 80)
                for b in range(2):
                    aux_wait(l, b)
                    for k in range(4):
                        last = nc.tensor.transpose(aux[:, b, k * P:(k + 1) * P], sgu_raw[:, 4 * b + k, :], ident[:])
                    aux_end(b, last)
                chunk(l, 2)
                chunk(l, 3)
                chunk(l, 4)
                aux_all(l)
                pe.wait_ge(vn_ready, l + 1)
                for b in range(4):
                    for k in range(2):
                        g = 2 * b + k
                        last = nc.tensor.matmul(aux[:, b, k * S:(k + 1) * S].rearrange("p (t c) -> p t c", t=NT),
                                                wT[:, g, :], bv[:, :, g * P:(g + 1) * P], start=True, stop=True)
                    aux_end(b, last)
                chunk(l, 5)
                aux_all(l)
                transpose_x(l, bu)
                chunk(l, 6)
                pe.wait_ge(roped, 4 * l + 2)
                transpose_heads(l, lambda t, h: bq[:, t, h * P:(h + 1) * P], 8)
                chunk(l, 7)
                chunk(l, 8)
                pe.wait_ge(roped, 4 * l + 4)
                transpose_heads(l, lambda t, h: bk[:, t, h * P:(h + 1) * P], 8)
                chunk(l, 9)
                aux_all(l)
                scores(l, 0)
                for h in range(H1):
                    for u in HEAD_UNITS[h]:
                        chunk_unit(l, u, *((xTh, xTl) if u < 28 else (yTh, yTl)))
                    pe.wait_ge(a_ready, l * H1 + h + 1)
                    prob_transposes(l, pa)
                    if h + 1 < H1:
                        scores(l, h + 1)
                    if h == 0:
                        for p in range(2):
                            pe.wait_ge(acc_read[p], l * ACC_LAYER + 7)
                    values(l, [bval[:, t, h * P:(h + 1) * P] for t in range(NT)], P)
                pe.wait_ge(hb_ready, l + 1)
                transpose_x(l, bu)
                aux_all(l)
                chunk(l, 16)
                chunk(l, 17)
                pe.wait_ge(m_ready, 2 * l + 2)
                transpose_x(l, bg[:, 0])
                aux_all(l)
                chunk(l, 18, yTh, yTl)
                chunk(l, 19, yTh, yTl)

            with pe.Fori(0, DEPTH) as l:
                pe.wait_ge(x_ready, 6 * l + 2)
                transpose_x(l, x)
                aux_all(l)
                ffn1(l, 0)
                mixer(l)
                pe.wait_ge(x_ready, 6 * l + 6)
                transpose_x(l, x)
                aux_all(l)
                ffn1(l, 1)
                for c in n_aux + n_acc:
                    c.layer_ends()
            if stop == 1:
                return

            l = L2

            def job(name, lh=xTh, ll=xTl, kt0=0):
                g = JOB[name]
                if not g["wide"]:
                    p, n = g["acc"][0]
                    pe.wait_ge(acc_read[p], acc_n2(p, n) + 1)
                    for (s, n), (k0, k1, cols, *_) in zip(g["slots"], g["units"]):
                        pe.wait_ge(slot_lo[s], slot_n2(s, n) + 2)
                        vh, vl = (w[:, s, 0:(k1 - k0) * cols].rearrange("p (k n) -> p k n", k=k1 - k0)
                                  for w in (whi, wlo))
                        for t in range(NT):
                            last = products(acc[:, p, t, 0:cols],
                                            [(kt0 + k, k - k0) for k in range(k0, k1)], kt0, kt0 + g["kts"] - 1,
                                            lh, ll, t, lambda k: vh[:, k, :], lambda k: vl[:, k, :])
                    last.then_inc(acc_full[p], 1)
                    n_acc[p].k += 1
                else:
                    for p, n in g["acc"]:
                        pe.wait_ge(acc_read[p], acc_n2(p, n) + 1)
                        n_acc[p].k += 1
                    (s, n), = g["slots"]
                    pe.wait_ge(slot_lo[s], slot_n2(s, n) + 2)
                    vh, vl = (w[:, s, :].rearrange("p (k n) -> p k n", k=2) for w in (whi, wlo))
                    for half in range(2):
                        col = slice(half * NC, (half + 1) * NC)
                        for t in range(NT):
                            last = products(acc[:, half, t, :], [(k, k) for k in range(2)], 0, 1, lh, ll, t,
                                            lambda k: vh[:, k, col], lambda k: vl[:, k, col])
                        last.then_inc(acc_full[half], 1)

            rms = [0]

            def norm_x():
                rms[0] += 1
                pe.wait_ge(xn_ready, rms[0])
                transpose_x(l, bv)
                aux_all(l)

            def heads2(n_heads, q, k, v, ready, n0):
                def score(h):
                    b = h % 2
                    aux_wait(l, b)
                    nc.tensor.matmul(aux[:, b, 0:P], q(h, 0), k(h, 0, P), start=True, stop=True)
                    last = nc.tensor.matmul(aux[:, b, P:3 * P], q(h, 1), k(h, 0, S), start=True, stop=True)
                    aux_end(b, last)

                score(0)
                score(1)
                for h in range(n_heads):
                    pe.wait_ge(ready, n0 + h + 1)
                    prob_transposes(l, SE[:, h % 2, 0, :])
                    if h + 2 < n_heads:
                        score(h + 2)
                    values(l, v(h), HD)

            def feed_forward2(i):
                g = JOB[f"ff{i}"]

                def view(w):
                    v = w.rearrange("p (k n) -> p k n", k=4)
                    return lambda k: v[:, k, :]

                feed_forward(l, lambda s: slot_n2(s, g["n0"][s]),
                             [(g["s0"] + j) % RING for j in range(RING)], view, 4, NF2)

            def ff_and_side(i):
                norm_x()
                feed_forward2(i)
                norm_x()
                pe.wait_ge(side_in, 16 * (i + 1))
                aux_wait(l, 2)
                for f in range(2):
                    for t in range(NT):
                        last = nc.tensor.transpose(aux[:, 2, (2 * f + t) * P:(2 * f + t + 1) * P],
                                                   bq[:, t, f * P:(f + 1) * P], ident[:])
                aux_end(2, last)
                job(f"g{i}0")
                job(f"g{i}1")
                aux_wait(l, 2)
                job(f"side{i}", yTh, yTl)

            norm_x()
            job("cq")
            job("ckv")
            job("qb")
            pe.wait_ge(low_ready, 1)
            for t in range(NT):
                aux_wait(l, t)
                for k in range(3):
                    c0 = t * Q_LORA + k * P
                    last = nc.tensor.transpose(aux[:, t, k * P:(k + 1) * P], flat(mix_par)[:, c0:c0 + P],
                                               ident[:])
                aux_end(t, last)
            job("kb")
            pe.wait_ge(low_ready, 2)
            aux_wait(l, 2)
            for k in range(2):
                for t in range(NT):
                    c0 = 2 * Q_LORA + t * (KV_LORA + ROPE2) + k * P
                    last = nc.tensor.transpose(aux[:, 2, (2 * k + t) * P:(2 * k + t + 1) * P],
                                               flat(mix_par)[:, c0:c0 + P], ident[:])
            aux_end(2, last)
            job("vb")
            aux_all(l)
            job("uq0", yTh, yTl, 0)
            job("uq1", yTh, yTl, 0)
            job("ukv0", yTh, yTl, 3)
            job("ukv1", yTh, yTl, 3)
            qb, kb, vb, qbT = (bg_flat[:, k * D:(k + 1) * D] for k in range(4))
            kbT = qb
            for q, src in enumerate((qb, kb)):
                pe.wait_ge(heads_ready, q + 1)
                aux_all(l)
                transpose_heads(l, lambda t, h: src[:, t * NC + h * P:t * NC + (h + 1) * P], 4, banks=[0, 1])
            pe.wait_ge(heads_ready, 3)
            transpose_heads(l, lambda t, h: flat(bu)[:, t * 768 + h * MLA_D:t * 768 + (h + 1) * MLA_D], 8,
                            width=MLA_D)
            pe.wait_ge(heads_ready, 4)
            transpose_heads(l, lambda t, h: flat(mix_par)[:, t * 768 + h * MLA_D:t * 768 + (h + 1) * MLA_D], 8,
                            width=MLA_D)
            aux_all(l)
            heads2(MLA_H, lambda h, t: qT[0:MLA_D, h, t * P:(t + 1) * P], lambda h, k0, k1: kT[0:MLA_D, h, k0:k1],
                   lambda h: [bval[:, t, h * P + MLA_N:(h + 1) * P] for t in range(NT)], e_ready, DEPTH * H1)

            def half(t_, h, c0, c1):
                return t_[(h % 2) * HD:(h % 2 + 1) * HD, (h // 2) * S + c0:(h // 2) * S + c1]

            heads2(DIL_H, lambda h, t: half(qbT, h, t * P, (t + 1) * P), lambda h, k0, k1: half(kbT, h, k0, k1),
                   lambda h: [vb[:, t * NC + h * HD:t * NC + (h + 1) * HD] for t in range(NT)], a_ready,
                   DEPTH * H1)
            pe.wait_ge(o_ready, 1)
            transpose_x(l, bu)
            aux_all(l)
            job("eout0", yTh, yTl)
            job("eout1", yTh, yTl)
            ff_and_side(0)
            norm_x()
            for k in range(4):
                job(f"z{k}")
            pe.wait_ge(heads_ready, 5)
            transpose_heads(l, lambda t, h: bq[:, t, h * P:(h + 1) * P], 8)
            job("z4")
            job("z5")
            pe.wait_ge(heads_ready, 6)
            transpose_heads(l, lambda t, h: bu[:, t, h * P:(h + 1) * P], 8)
            aux_all(l)
            for name in ("z4", "z5"):
                p, n = JOB[name]["acc"][0]
                pe.wait_ge(acc_read[p], acc_n2(p, n) + 2)
            heads2(MOBA_H, lambda h, t: half(flat(bv), h, t * P, (t + 1) * P),
                   lambda h, k0, k1: half(flat(bq), h, k0, k1),
                   lambda h: [bval[:, t, h * HD:(h + 1) * HD] for t in range(NT)], e_ready,
                   DEPTH * H1 + MLA_H + DIL_H)
            pe.wait_ge(o_ready, 2)
            transpose_x(l, bu)
            aux_all(l)
            job("oout0", yTh, yTl)
            job("oout1", yTh, yTl)
            ff_and_side(1)

        def places_x():
            for t in range(NT):
                for half in range(2):
                    yield (2 * t + half, aux[:, 2 * t + half, :].rearrange("p (k c) -> p k c", k=4),
                           (slice(4 * half, 4 * half + 4), slice(t * P, (t + 1) * P)))

        def place_pair(b, k0):
            return b, aux[:, b, :].rearrange("p (k c) -> p k c", k=2), (slice(k0, k0 + 2), slice(0, S))

        def places_cq():
            for t in range(NT):
                yield t, aux[:, t, 0:3 * P].rearrange("p (k c) -> p k c", k=3), (slice(0, 3), slice(t * P, (t + 1) * P))

        @block.scalar
        def _(act):
            n_acc = [Uses(ACC_LAYER), Uses(ACC_LAYER)]
            n_aux = [Uses(k) for k in AUX_LAYER]

            def high(s, n, size=UNIT):
                act.wait_ge(slot_full[s], 32 * n + 32)
                nc.scalar.copy(whi[:, s, 0:size], raw[:, s, 0:size]).then_inc(slot_hi[s], 1)

            def high_T(l, places, dst):
                for b, src, (k, tok) in places:
                    act.wait_ge(aux_full[b], n_aux[b].take(l) + 1)
                    nc.scalar.copy(dst[:, k, tok], src).then_inc(t_hi, 1)

            def acc_done(l, p):
                act.wait_ge(acc_full[p], n_acc[p].take(l) + 1)

            def copy_banks(l, dst, banks=range(4), parts=P):
                for q, b in enumerate(banks):
                    act.wait_ge(aux_full[b], n_aux[b].take(l) + 1)
                    nc.scalar.copy(dst[0:parts, q * NC:(q + 1) * NC], aux[0:parts, b, :])\
                        .then_inc(aux_read[b], 1)

            def feed_forward(l, slot0, which_slots, func, cols, t_banks, iters):
                aux0 = [n_aux[b].at(l) for b in range(4)]
                with act.Fori(0, iters) as i:
                    for t in range(NT):
                        act.wait_ge(aux_full[t], aux0[t] + i + 1)
                        nc.scalar.activation(act_b[:, t, 0:cols], aux[:, t, 0:cols], func).then_inc(act_done, 1)
                    for s in which_slots[:2]:
                        high(s, slot0(s) + i + 1)
                    for b in t_banks:
                        act.wait_ge(aux_full[b], aux0[b] + i + 1)
                        _, src, (k, tok) = place_pair(b, 2 * (b - 2))
                        nc.scalar.copy(yTh[:, k, tok], src).then_inc(t_hi, 1)
                    for s in which_slots[2:]:
                        high(s, slot0(s) + i)
                for b in [0, 1, *t_banks]:
                    n_aux[b].k += iters
                for p in range(2):
                    n_acc[p].k += 1

            def mixer(l):
                high_T(l, places_x(), xTh)
                for u in (2, 3):
                    high(u % RING, mixer_n(l, u))

                def split(u):
                    if u < 2 * CH + 2:
                        high(u % RING, mixer_n(l, u))

                def to_sbuf(c, dst, func):
                    p = c % 2
                    col = slice(p * NC, (p + 1) * NC)
                    nc.scalar.activation(dst[:, :, col], acc[:, p], func).then_inc(acc_read[p], 1)

                def head_exp(h):
                    act.wait_ge(s_ready, l * H1 + h + 1)
                    for m in range(2):
                        for t, c in ((0, slice(0, P)), (1, slice(P, 3 * P))):
                            last = nc.scalar.activation(SE[:, h % 2, m, c], SE[:, h % 2, m, c], ACT.Exp,
                                                        bias=rmax[:, h % 2, 2 * m + t:2 * m + t + 1],
                                                        scale=HD ** -0.5,
                                                        accum_out=rsum[:, h % 2, 2 * m + t:2 * m + t + 1])
                    last.then_inc(e_ready, 1)

                def probs_T(h):
                    act.wait_ge(aux_full[2], n_aux[2].take(l) + 1)
                    nc.scalar.copy(aT[:], aux[:, 2, 0:3 * P]).then_inc(aux_read[2], 1)

                def head_out(h):
                    act.wait_ge(aux_full[3], n_aux[3].take(l) + 1)
                    for t in range(NT):
                        nc.scalar.activation(sq_junk, aux[:, 3, t * P:(t + 1) * P], ACT.Square,
                                             accum_out=ssq[:, t, h:h + 1])
                        act.drain()
                    nc.scalar.copy(bu[:, :, h * P:(h + 1) * P],
                                   aux[:, 3, 0:S].rearrange("p (t c) -> p t c", t=NT)).then_inc(aux_read[3], 1)

                for c in range(10):
                    acc_done(l, c % 2)
                    split(2 * c + 4)
                    split(2 * c + 5)
                    if c < 2:
                        to_sbuf(c, bv, ACT.Gelu)
                    elif c < 4:
                        to_sbuf(c, bu, ACT.Gelu)
                    elif c >= 8:
                        to_sbuf(c, bval, ACT.Copy)
                    if c == 1:
                        for b in range(2):
                            n_aux[b].k += 1
                    if c == 4:
                        for b in range(4):
                            n_aux[b].k += 1
                    if c == 5:
                        high_T(l, places_x(), yTh)
                    if c == 6:
                        copy_banks(l, flat(bv))
                    if c == 8:
                        copy_banks(l, flat(bq))
                act.wait_ge(lam_dot, l + 1)
                nc.scalar.activation(lam_t[:, 2:4], lam_t[:, 0:2], ACT.Exp).then_inc(lam_exp, 1)
                for m in range(2):
                    n_aux[m].k += H1
                head_exp(0)
                for h in range(H1):
                    probs_T(h)
                    ends = [u // 2 for u in HEAD_UNITS[h] if u % 2]
                    for c in ends:
                        acc_done(l, c % 2)
                        split(2 * c + 4)
                    if h + 1 < H1:
                        head_exp(h + 1)
                    for c in ends:
                        split(2 * c + 5)
                        if c < 14:
                            w, p = divmod(c - 10, 2)
                            act.wait_ge(acc_read[p], l * ACC_LAYER + 1 + c // 2 + 2)
                            g = bg[:, w, :, p * NC:(p + 1) * NC]
                            nc.scalar.activation(g, g, ACT.Tanh, scale=0.5).then_inc(tanh_done, 1)
                    head_out(h)
                high_T(l, places_x(), xTh)
                for c in range(16, CH):
                    acc_done(l, c % 2)
                    split(2 * c + 4)
                    split(2 * c + 5)
                    if c == 17:
                        high_T(l, places_x(), yTh)

            act.wait_ge(angles, 1)
            nc.scalar.activation(ang[:, 2:4], ang[:, 2:4], ACT.Sin).then_inc(sines, 1)
            for s in range(2):
                high(s, 0)
            with act.Fori(0, DEPTH) as l:
                high_T(l, places_x(), xTh)
                for which in range(2):
                    feed_forward(l, lambda s: l * SLOT_LAYER[s] + (NF + CH // 2) * which, [0, 1, 2],
                                 ACT.Silu, FB, [2], NF)
                    if which == 0:
                        mixer(l)
                        high_T(l, places_x(), xTh)
                for c in n_aux + n_acc:
                    c.layer_ends()
            if stop == 1:
                return

            l = L2
            n_norm = [0]

            def split_after(name):
                g = JOB[name]
                for u in units_after(g):
                    high_unit(u)

            def high_unit(u):
                g = job_of_unit(u)
                if g["units"] is None:
                    s = (g["s0"] + u - g["u0"]) % RING
                    high(s, slot_n2(s, g["n0"][s]))
                else:
                    s, n = g["slots"][u - g["u0"]]
                    k0, k1, cols = g["units"][u - g["u0"]][:3]
                    high(s, slot_n2(s, n), (k1 - k0) * cols)

            def done(name):
                for p, n in JOB[name]["acc"]:
                    act.wait_ge(acc_full[p], acc_n2(p, n) + 1)
                    n_acc[p].k += 1
                split_after(name)

            def to_sbuf(name, dst, func=ACT.Copy, scale=1.0):
                g = JOB[name]
                p = g["acc"][0][0]
                nc.scalar.activation(dst, acc[:, p, :, 0:g["cols"]], func, scale=scale).then_inc(acc_read[p], 1)

            def norm_x():
                act.wait_ge(x_ready, 2 + 6 * DEPTH + n_norm[0])
                n_norm[0] += 1
                for t in range(NT):
                    last = nc.scalar.activation(bv[:, t, :], x[:, t, :], ACT.Square, accum_out=ssq[:, t, 0:1])
                last.then_inc(sumsq, 1)
                high_T(l, places_x(), xTh)

            def heads2(n_heads, n0):
                def exps(h):
                    act.wait_ge(s_ready, n0 + h + 1)
                    b = h % 2
                    for t, c in ((0, slice(0, P)), (1, slice(P, 3 * P))):
                        last = nc.scalar.activation(SE[:, b, 0, c], SE[:, b, 0, c], ACT.Exp,
                                                    bias=rmax[:, b, t:t + 1], accum_out=rsum[:, b, t:t + 1])
                    last.then_inc(e_ready, 1)

                exps(0)
                for h in range(n_heads):
                    if h + 1 < n_heads:
                        exps(h + 1)
                    act.wait_ge(aux_full[2], n_aux[2].take(l) + 1)
                    if h > 0:
                        act.wait_ge(aux_full[3], n_aux[3].at(l) + h)
                    nc.scalar.copy(aT[:], aux[:, 2, 0:3 * P]).then_inc(aux_read[2], 1)
                for b in range(2):
                    n_aux[b].k += n_heads // 2
                n_aux[3].k += n_heads

            def ff_and_side(i):
                norm_x()
                g = JOB[f"ff{i}"]
                feed_forward(l, lambda s: slot_n2(s, g["n0"][s]), [(g["s0"] + j) % RING for j in range(RING)],
                             ACT.Relu, NC, [2, 3], NF2)
                for p, n in g["acc"]:
                    act.wait_ge(acc_full[p], acc_n2(p, n) + 1)
                split_after(f"ff{i}")
                norm_x()
                high_T(l, [place_pair(2, 0)], yTh)
                for k in range(2):
                    done(f"g{i}{k}")
                    to_sbuf(f"g{i}{k}", bg[:, 0, :, k * NC:(k + 1) * NC], ACT.Tanh, 0.5)
                done(f"side{i}")

            norm_x()
            for u in (2, 3):
                high_unit(u)
            mixf = flat(mix_par)
            done("cq")
            p = JOB["cq"]["acc"][0][0]
            for t in range(NT):
                nc.scalar.activation(aT[:], acc[:, p, t, 0:Q_LORA], ACT.Square, accum_out=ssq[:, t, 1:2])
                act.drain()
            to_sbuf("cq", mixf[:, 0:NT * Q_LORA].rearrange("p (t c) -> p t c", t=NT))
            done("ckv")
            p = JOB["ckv"]["acc"][0][0]
            for t in range(NT):
                nc.scalar.activation(aT[:, 0:KV_LORA], acc[:, p, t, 0:KV_LORA], ACT.Square,
                                     accum_out=ssq[:, t, 2:3])
                act.drain()
            w = KV_LORA + ROPE2
            to_sbuf("ckv", mixf[:, NT * Q_LORA:NT * (Q_LORA + w)].rearrange("p (t c) -> p t c", t=NT))
            done("qb")
            to_sbuf("qb", bg_flat[:, 0:D].rearrange("p (t c) -> p t c", t=NT))
            high_T(l, places_cq(), yTh)
            done("kb")
            to_sbuf("kb", bg_flat[:, D:2 * D].rearrange("p (t c) -> p t c", t=NT))
            high_T(l, [place_pair(2, 3)], yTh)
            done("vb")
            to_sbuf("vb", bg_flat[:, 2 * D:3 * D].rearrange("p (t c) -> p t c", t=NT))
            qa = flat(bu)[:, 0:NT * MLA_H * MLA_D].rearrange("p (t c) -> p t c", t=NT)
            for k in range(2):
                done(f"uq{k}")
                to_sbuf(f"uq{k}", qa[:, :, k * 384:(k + 1) * 384])
            for k in range(2):
                done(f"ukv{k}")
                to_sbuf(f"ukv{k}", bval[:, :, k * NC:(k + 1) * NC])
            copy_banks(l, bg_flat[:, 3 * D:4 * D], banks=[0, 1])
            copy_banks(l, bg_flat[:, 0:D], banks=[0, 1])
            copy_banks(l, flat(bv), parts=MLA_D)
            copy_banks(l, flat(bq), parts=MLA_D)
            heads2(MLA_H, DEPTH * H1)
            heads2(DIL_H, DEPTH * H1 + MLA_H)
            high_T(l, places_x(), yTh)
            for k in range(2):
                done(f"eout{k}")
            ff_and_side(0)
            norm_x()
            for k in range(6):
                done(f"z{k}")
                dst = (bq, bu, bval)[k // 2]
                to_sbuf(f"z{k}", dst[:, :, (k % 2) * NC:(k % 2 + 1) * NC])
                if k == 3:
                    copy_banks(l, flat(bv))
            copy_banks(l, flat(bq))
            heads2(MOBA_H, DEPTH * H1 + MLA_H + DIL_H)
            high_T(l, places_x(), yTh)
            for k in range(2):
                done(f"oout{k}")
            ff_and_side(1)

        @block.vector
        def _(dve):
            n_acc = [Uses(ACC_LAYER), Uses(ACC_LAYER)]
            n_aux = [Uses(k) for k in AUX_LAYER]
            n_hi = Uses(2 * NF + 6 * 4)
            V = nc.vector

            def low(s, n, size=UNIT):
                dve.wait_ge(slot_hi[s], n + 1)
                V.tensor_tensor(wlo[:, s, 0:size], raw[:, s, 0:size], cast(whi[:, s, 0:size]), ALU.subtract)\
                    .then_inc(slot_lo[s], 1)

            def low_T(l, places, dst_l, dst_h):
                for b, src, (k, tok) in places:
                    dve.wait_ge(t_hi, n_hi.take(l) + 1)
                    V.tensor_tensor(dst_l[:, k, tok], src, cast(dst_h[:, k, tok]), ALU.subtract)\
                        .then_inc(aux_read[b], 1)
                    n_aux[b].k += 1

            def newton(n):
                v, y, z = nv[:, 0:n], ny[:, 0:n], nz[:, 0:n]
                dve.drain()
                V.tensor_scalar(z.bitcast(I32), v.bitcast(I32), 1, None, ALU.logical_shift_right)
                dve.drain()
                V.tensor_scalar(y.bitcast(I32), z.bitcast(I32), -1.0, RSQRT_MAGIC, ALU.mult, ALU.add)
                for _ in range(3):
                    dve.drain()
                    V.scalar_tensor_tensor(z, y, -0.5, y, ALU.mult, ALU.mult)
                    dve.drain()
                    V.tensor_tensor(z, z, v, ALU.mult)
                    dve.drain()
                    V.scalar_tensor_tensor(y, z, 1.5, y, ALU.add, ALU.mult)
                dve.drain()

            def mean_and_rstd(src, eps):
                for t in range(NT):
                    for half in range(2):
                        V.bn_stats(stat[:, t, half, :], src[:, t, half * NC:(half + 1) * NC])
                dve.drain()
                for t in range(NT):
                    V.bn_aggr(mv[:, t, :], stat[:, t, :, :].rearrange("p a b -> p (a b)"))
                dve.drain()
                V.tensor_scalar(nv[:, 0:NT], mv[:, :, 1], eps, None, ALU.add)
                newton(NT)

            def scale_shift(src, par, ready):
                for t in range(NT):
                    V.scalar_tensor_tensor(src[:, t, :], src[:, t, :], mv[:, t, 0:1], par[:, 0, :],
                                           ALU.subtract, ALU.mult)
                    dve.drain()
                    last = V.scalar_tensor_tensor(src[:, t, :], src[:, t, :], ny[:, t:t + 1], par[:, 1, :],
                                                  ALU.mult, ALU.add)
                    if ready is x_ready or t == NT - 1:
                        last.then_inc(ready, 1)

            def acc_wait(l, p):
                dve.wait_ge(acc_full[p], n_acc[p].take(l) + 1)

            def add_norm(l, k):
                for p in range(2):
                    acc_wait(l, p)
                    col = slice(p * NC, (p + 1) * NC)
                    V.scalar_tensor_tensor(x[:, :, col], x[:, :, col], 2 * ALPHA, acc[:, p], ALU.mult, ALU.add)\
                        .then_inc(acc_read[p], 1)
                dve.drain()
                mean_and_rstd(x, 4 * LN_EPS)
                dve.wait_ge(ln_in, 32 * (3 * l + k) + 32)
                scale_shift(x, ln_par, x_ready)
                dve.drain().then_inc(ln_free, 1)

            n_act = [0]

            def feed_forward(l, slot0, which_slots, act0, other, cols, t_banks, iters):
                h0 = n_hi.at(l)
                with dve.Fori(0, iters) as i:
                    for t in range(NT):
                        dve.wait_ge(act_done, act0 + 2 * i + t + 1)
                        V.tensor_tensor(gate_b[:, t, 0:cols], act_b[:, t, 0:cols], other(t), ALU.mult)\
                            .then_inc(aux_read[t], 1)
                    for s in which_slots[:2]:
                        low(s, slot0(s) + i + 1)
                    for q, b in enumerate(t_banks):
                        dve.wait_ge(t_hi, h0 + len(t_banks) * i + q + 1)
                        _, src, (k, tok) = place_pair(b, 2 * (b - 2))
                        V.tensor_tensor(yTl[:, k, tok], src, cast(yTh[:, k, tok]), ALU.subtract)\
                            .then_inc(aux_read[b], 1)
                    for s in which_slots[2:]:
                        low(s, slot0(s) + i)
                for b in [0, 1, *t_banks]:
                    n_aux[b].k += iters
                n_hi.k += len(t_banks) * iters

            def rotate(l, c, dst):
                p = c % 2
                dve.drain()
                acc_wait(l, p)
                src = acc[:, p].rearrange("p t (h d) -> p t h d", d=HD)
                out_ = dst[:, :, p * NC:(p + 1) * NC].rearrange("p t (h d) -> p t h d", d=HD)
                tmp = bg_flat[:, D:2 * D].rearrange("p (t h d) -> p t h d", t=NT, d=HD)
                half = HD // 2

                def table(k, c0, c1):
                    return rope[:, k, :, c0:c1].unsqueeze(2).to_broadcast([P, NT, NC // HD, c1 - c0])

                V.tensor_tensor(out_, src, table(0, 0, HD), ALU.mult)
                V.tensor_tensor(tmp[:, :, :, 0:half], src[:, :, :, half:HD], table(1, 0, half), ALU.mult)
                dve.drain()
                V.tensor_tensor(tmp[:, :, :, half:HD], src[:, :, :, 0:half], table(1, half, HD), ALU.mult)\
                    .then_inc(acc_read[p], 1)
                dve.drain()
                V.tensor_tensor(out_, out_, tmp, ALU.add).then_inc(roped, 1)

            def mixer(l):
                low_T(l, places_x(), xTl, xTh)
                for u in (2, 3):
                    low(u % RING, mixer_n(l, u))

                def split(u):
                    if u < 2 * CH + 2:
                        low(u % RING, mixer_n(l, u))

                def head_scores(h):
                    for m in range(2):
                        dve.wait_ge(aux_full[m], n_aux[m].take(l) + 1)
                        V.tensor_tensor(SE[:, h % 2, m, :], aux[:, m, 0:3 * P], causal[:], ALU.add)\
                            .then_inc(aux_read[m], 1)
                    dve.drain()
                    rm = rmax[:, h % 2, :].rearrange("p (m t) -> p m t", m=2)
                    V.tensor_reduce(rm[:, :, 0], SE[:, h % 2, :, 0:P], AX_X, ALU.max)
                    V.tensor_reduce(rm[:, :, 1], SE[:, h % 2, :, P:3 * P], AX_X, ALU.max)
                    dve.drain()
                    V.tensor_scalar(rmax[:, h % 2, :], rmax[:, h % 2, :], -(HD ** -0.5), None, ALU.mult)\
                        .then_inc(s_ready, 1)

                def head_probs(h):
                    dve.wait_ge(e_ready, l * H1 + h + 1)
                    r = rinv[:, h % 2, :]
                    V.reciprocal(r, rsum[:, h % 2, :])
                    dve.drain()
                    V.tensor_scalar(r[:, 2:4], r[:, 2:4], neg_lam[:], None, ALU.mult)
                    for t, c in ((0, slice(0, P)), (1, slice(P, 3 * P))):
                        V.tensor_scalar(pa[:, c], SE[:, h % 2, 0, c], r[:, t:t + 1], None, ALU.mult)
                    dve.drain()
                    for t, c in ((0, slice(0, P)), (1, slice(P, 3 * P))):
                        last = V.scalar_tensor_tensor(pa[:, c], SE[:, h % 2, 1, c], r[:, 2 + t:3 + t], pa[:, c],
                                                      ALU.mult, ALU.add)
                        if t == 0:
                            dve.drain()
                    last.then_inc(a_ready, 1)

                for c in range(10):
                    split(2 * c + 4)
                    split(2 * c + 5)
                    if 4 <= c < 8:
                        rotate(l, c, bq if c < 6 else bk)
                    else:
                        n_acc[c % 2].k += 1
                    if c == 1:
                        for b in range(2):
                            dve.wait_ge(aux_full[b], n_aux[b].take(l) + 1)
                            V.tensor_tensor(wT[:, 4 * b:4 * b + 4, :],
                                            aux[:, b, :].rearrange("p (g t) -> p g t", g=4),
                                            tri[:].unsqueeze(1).to_broadcast([P, 4, P]), ALU.mult)\
                                .then_inc(aux_read[b], 1)
                        for p in range(2):
                            dve.wait_ge(acc_read[p], n_acc[p].at(l) + 1)
                        mean_and_rstd(bv, LN_EPS)
                        dve.wait_ge(mix_in, 64 * l + 32)
                        scale_shift(bv, mix_par, vn_ready)
                        dve.drain().then_inc(mix_free, 1)
                    if c == 4:
                        for p in range(2):
                            dve.wait_ge(acc_read[p], l * ACC_LAYER + 1 + 2 + 1)
                        for b in range(4):
                            dve.wait_ge(aux_full[b], n_aux[b].take(l) + 1)
                            for k in range(2):
                                g = 2 * b + k
                                u = bu[:, :, g * P:(g + 1) * P]
                                last = V.scalar_tensor_tensor(
                                    u, aux[:, b, k * S:(k + 1) * S].rearrange("p (t c) -> p t c", t=NT),
                                    sgu_bT[:, g:g + 1], u, ALU.add, ALU.mult)
                            last.then_inc(aux_read[b], 1)
                    if c == 5:
                        low_T(l, places_x(), yTl, yTh)
                    if c in (6, 8):
                        for b in range(4):
                            n_aux[b].k += 1
                lw = lam_w.rearrange("p (a b d) -> p a b d", a=2, b=2)
                V.tensor_tensor(pa[:, 0:2 * HD].rearrange("p (a d) -> p a d", a=2), lw[:, :, 0], lw[:, :, 1],
                                ALU.mult)
                dve.drain()
                V.tensor_reduce(lam_t[:, 0:2], pa[:, 0:2 * HD].rearrange("p (a d) -> p a d", a=2), AX_X, ALU.add)\
                    .then_inc(lam_dot, 1)
                dve.wait_ge(lam_exp, l + 1)
                V.tensor_tensor(lam_t[:, 0:1], lam_t[:, 3:4], lam_t[:, 2:3], ALU.subtract)
                dve.drain()
                V.tensor_tensor(neg_lam[:], lam_t[:, 0:1], lam_init[:, 0:1], ALU.subtract)
                dve.drain()
                head_scores(0)
                head_probs(0)
                for h in range(H1):
                    ends = [u // 2 for u in HEAD_UNITS[h] if u % 2]
                    if h + 1 < H1:
                        head_scores(h + 1)
                    for c in ends:
                        split(2 * c + 4)
                    if h + 1 < H1:
                        head_probs(h + 1)
                    for c in ends:
                        split(2 * c + 5)
                        w, p = divmod(c - 10, 2)
                        acc_wait(l, p)
                        g = bg[:, w % 2, :, p * NC:(p + 1) * NC]
                        if c < 14:
                            if c == 10:
                                dve.wait_ge(mix_in, 64 * l + 64)
                            V.tensor_tensor(g, acc[:, p], mix_par[:, w, p * NC:(p + 1) * NC].unsqueeze(1)
                                            .to_broadcast([P, NT, NC]), ALU.add).then_inc(acc_read[p], 1)
                            if c == 13:
                                dve.drain().then_inc(mix_free, 1)
                        else:
                            dve.wait_ge(tanh_done, 4 * l + 4)
                            V.scalar_tensor_tensor(g, g, 1.0, acc[:, p], ALU.add, ALU.mult)\
                                .then_inc(acc_read[p], 1)
                n_aux[2].k += H1
                n_aux[3].k += H1
                dve.wait_ge(aux_read[3], n_aux[3].at(l) + 1)
                V.tensor_scalar(nv[:, 0:NT * H1], ssq[:, :, :].rearrange("p t h -> p (t h)"), 1.0 / (2 * HD),
                                LN_EPS, ALU.mult, ALU.add)
                newton(NT * H1)
                V.tensor_scalar(ny[:, 0:NT * H1], ny[:, 0:NT * H1], lam_init[:, 1:2], None, ALU.mult)
                dve.drain()
                o = flat(bu).rearrange("p (h c) -> p h c", c=P)
                V.tensor_tensor(o, o, ny[:, 0:NT * H1].unsqueeze(2).to_broadcast([P, NT * H1, P]), ALU.mult)
                dve.drain()
                V.tensor_tensor(o, o, diff_g[:].unsqueeze(1).to_broadcast([P, NT * H1, P]), ALU.mult)\
                    .then_inc(hb_ready, 1)
                low_T(l, places_x(), xTl, xTh)
                for c in range(16, 18):
                    split(2 * c + 4)
                    split(2 * c + 5)
                    p = c % 2
                    acc_wait(l, p)
                    g0, g1 = (bg[:, w, :, p * NC:(p + 1) * NC] for w in range(2))
                    V.scalar_tensor_tensor(g1, g1, 1.0, acc[:, p], ALU.add, ALU.mult).then_inc(acc_read[p], 1)
                    dve.drain()
                    V.tensor_tensor(g0, g0, g1, ALU.add).then_inc(m_ready, 1)
                low_T(l, places_x(), yTl, yTh)
                dve.drain().then_inc(small_free, 1)
                split(40)
                split(41)

            for s in [*slot_lo, *acc_read, *aux_read, ln_free, mix_free]:
                dve.sem_inc(s, 1)
            dve.wait_ge(x_in, 16)
            dve.sem_inc(x_ready, 2)
            dve.wait_ge(const_in, 8 * 16)
            pos_f = lam_t[:, 0:NT]
            V.tensor_copy(pos_f, pos_i[:])
            dve.drain()
            for t in range(NT):
                V.tensor_scalar(ang[:, 0, t, :], inv_freq, pos_f[:, t:t + 1], None, ALU.mult)
            dve.drain()
            big = 12582912.0
            parts = two_pi_parts()
            for k, turn, shift in ((2, 0.0, 0.0), (3, 0.25, PI / 2)):
                V.tensor_scalar(ang[:, 1], ang[:, 0], 1.0 / (2 * PI), turn, ALU.mult, ALU.add)
                dve.drain()
                V.tensor_scalar(ang[:, 1], ang[:, 1], big, None, ALU.add)
                dve.drain()
                V.tensor_scalar(ang[:, 1], ang[:, 1], big, None, ALU.subtract)
                dve.drain()
                src = ang[:, 0]
                for c in parts:
                    V.scalar_tensor_tensor(ang[:, k], ang[:, 1], -c, src, ALU.mult, ALU.add)
                    dve.drain()
                    src = ang[:, k]
                V.tensor_scalar(ang[:, k], ang[:, k], shift, None, ALU.add)
                dve.drain()
                V.tensor_scalar(ang[:, k], ang[:, k], PI32, -PI32, ALU.min, ALU.max)
                dve.drain()
            dve.drain().then_inc(angles, 1)
            dve.wait_ge(sines, 1)
            hr = ROPE2 // 2
            V.tensor_copy(rope2[:, 0, :, 0:hr], ang[:, 3])
            V.tensor_copy(rope2[:, 0, :, hr:ROPE2], ang[:, 3])
            V.tensor_scalar(rope2[:, 1, :, 0:hr], ang[:, 2], -1.0, None, ALU.mult)
            V.tensor_copy(rope2[:, 1, :, hr:ROPE2], ang[:, 2])
            dve.drain().then_inc(small_free, 1)

            for s in range(2):
                low(s, 0)
            with dve.Fori(0, DEPTH) as l:
                low_T(l, places_x(), xTl, xTh)
                for which in range(2):
                    feed_forward(l, lambda s: l * SLOT_LAYER[s] + (NF + CH // 2) * which, [0, 1, 2],
                                 (2 * l + which) * NT * NF, lambda t: aux[:, t, FB:2 * FB], FB, [2], NF)
                    add_norm(l, 2 * which)
                    if which == 0:
                        mixer(l)
                        add_norm(l, 1)
                        low_T(l, places_x(), xTl, xTh)
                for c in n_aux + n_acc + [n_hi]:
                    c.layer_ends()
            if stop == 1:
                return

            l = L2
            n_norm = [0]

            def low_unit(u):
                g = job_of_unit(u)
                if g["units"] is None:
                    s = (g["s0"] + u - g["u0"]) % RING
                    low(s, slot_n2(s, g["n0"][s]))
                else:
                    s, n = g["slots"][u - g["u0"]]
                    k0, k1, cols = g["units"][u - g["u0"]][:3]
                    low(s, slot_n2(s, n), (k1 - k0) * cols)

            def split_after(name):
                for u in units_after(JOB[name]):
                    low_unit(u)

            def in_sbuf(name):
                p, n = JOB[name]["acc"][0]
                dve.wait_ge(acc_read[p], acc_n2(p, n) + 2)

            def norm_x():
                n = n_norm[0]
                n_norm[0] += 1
                dve.wait_ge(sumsq, n + 1)
                V.tensor_scalar(nv[:, 0:NT], ssq[:, :, 0], 1.0 / D, EPS, ALU.mult, ALU.add)
                newton(NT)
                dve.wait_ge(ln_in, 96 * DEPTH + 32 * (n + 1))
                for t in range(NT):
                    last = V.scalar_tensor_tensor(bv[:, t, :], x[:, t, :], ny[:, t:t + 1], ln_par[:, 0, :],
                                                  ALU.mult, ALU.mult)
                last.then_inc(xn_ready, 1)
                dve.drain().then_inc(ln_free, 1)
                low_T(l, places_x(), xTl, xTh)

            def group_norm(src, dst, gain, n, tmp, scale=1.0, signal=None):
                groups = src.shape[1]
                V.tensor_tensor(tmp, src, src, ALU.mult)
                dve.drain()
                V.tensor_reduce(nv[:, 0:groups], tmp, AX_X, ALU.add)
                dve.drain()
                V.tensor_scalar(nv[:, 0:groups], nv[:, 0:groups], 1.0 / n, EPS, ALU.mult, ALU.add)
                newton(groups)
                if scale != 1.0:
                    V.tensor_scalar(ny[:, 0:groups], ny[:, 0:groups], scale, None, ALU.mult)
                    dve.drain()
                V.tensor_tensor(tmp, src, ny[:, 0:groups].unsqueeze(2).to_broadcast([P, groups, n]), ALU.mult)
                dve.drain()
                last = V.tensor_tensor(dst, tmp, gain.unsqueeze(1).to_broadcast([P, groups, n]), ALU.mult)
                if signal is not None:
                    last.then_inc(signal, 1)
                else:
                    dve.drain()

            def rotate2(v, tmp, heads, signal=None):
                hr = ROPE2 // 2
                a_, b_ = tmp
                for t in range(NT):
                    g = slice(t * heads, (t + 1) * heads)

                    def table(k, c0, c1):
                        return rope2[:, k, t, c0:c1].unsqueeze(1).to_broadcast([P, heads, c1 - c0])

                    V.tensor_tensor(a_[:, g], v[:, g], table(0, 0, ROPE2), ALU.mult)
                    V.tensor_tensor(b_[:, g, 0:hr], v[:, g, hr:ROPE2], table(1, 0, hr), ALU.mult)
                    V.tensor_tensor(b_[:, g, hr:ROPE2], v[:, g, 0:hr], table(1, hr, ROPE2), ALU.mult)
                dve.drain()
                last = V.tensor_tensor(v, a_, b_, ALU.add)
                if signal is not None:
                    last.then_inc(signal, 1)
                else:
                    dve.drain()

            n_s = [DEPTH * H1]

            def heads2(n_heads, score, width0, count=None):
                n0 = n_s[0]
                n_s[0] += n_heads

                def scores(h):
                    b = h % 2
                    dve.wait_ge(aux_full[b], n_aux[b].take(l) + 1)
                    score(SE[:, b, 0, :], aux[:, b, 0:3 * P], h).then_inc(aux_read[b], 1)
                    dve.drain()
                    V.tensor_reduce(rmax[:, b, 0:1], SE[:, b, 0, 0:P], AX_X, ALU.max, negate=True)
                    V.tensor_reduce(rmax[:, b, 1:2], SE[:, b, 0, P:3 * P], AX_X, ALU.max, negate=True)\
                        .then_inc(s_ready, 1)

                scores(0)
                scores(1)
                for h in range(n_heads):
                    b = h % 2
                    dve.wait_ge(e_ready, n0 + h + 1)
                    if count is not None:
                        for t, c in ((0, slice(0, P)), (1, slice(P, 3 * P))):
                            last = V.scalar_tensor_tensor(SE[:, b, 0, c], SE[:, b, 0, c], 1.0, count[:, c],
                                                          ALU.mult, ALU.mult, accum_out=rsum[:, b, t:t + 1])
                        last.then_inc(a_ready, 1)
                        dve.drain()
                    V.reciprocal(rinv[:, b, 0:2], rsum[:, b, 0:2])
                    if h + 2 < n_heads:
                        scores(h + 2)
                    dve.wait_ge(aux_full[3], n_aux[3].take(l) + 1)
                    dve.drain()
                    for t in range(NT):
                        last = V.tensor_scalar(bu[:, t, width0 + h * HD:width0 + (h + 1) * HD],
                                               aux[:, 3, t * HD:(t + 1) * HD], rinv[:, b, t:t + 1], None, ALU.mult)
                    last.then_inc(aux_read[3], 1)
                n_aux[2].k += n_heads

            def add_out(name):
                for k in range(2):
                    p, n = JOB[f"{name}{k}"]["acc"][0]
                    split_after(f"{name}{k}")
                    dve.wait_ge(acc_full[p], acc_n2(p, n) + 1)
                    col = slice(k * NC, (k + 1) * NC)
                    V.tensor_tensor(x[:, :, col], x[:, :, col], acc[:, p], ALU.add).then_inc(acc_read[p], 1)
                dve.drain().then_inc(x_ready, 1)

            def ff_and_side(i):
                norm_x()
                g = JOB[f"ff{i}"]
                feed_forward(l, lambda s: slot_n2(s, g["n0"][s]), [(g["s0"] + j) % RING for j in range(RING)],
                             2 * DEPTH * NT * NF + i * NT * NF2, lambda t: aux[:, t, :], NC, [2, 3], NF2)
                for p, n in g["acc"]:
                    dve.wait_ge(acc_full[p], acc_n2(p, n) + 1)
                    col = slice(p * NC, (p + 1) * NC)
                    V.tensor_tensor(x[:, :, col], x[:, :, col], acc[:, p], ALU.add).then_inc(acc_read[p], 1)
                dve.drain().then_inc(x_ready, 1)
                split_after(f"ff{i}")
                norm_x()
                low_T(l, [place_pair(2, 0)], yTl, yTh)
                for k in range(2):
                    split_after(f"g{i}{k}")
                split_after(f"side{i}")
                in_sbuf(f"g{i}0")
                in_sbuf(f"g{i}1")
                for p, n in JOB[f"side{i}"]["acc"]:
                    dve.wait_ge(acc_full[p], acc_n2(p, n) + 1)
                    col = slice(p * NC, (p + 1) * NC)
                    gate = bg[:, 0, :, col]
                    V.scalar_tensor_tensor(gate, gate, 1.0, acc[:, p], ALU.add, ALU.mult).then_inc(acc_read[p], 1)
                    dve.drain()
                    V.scalar_tensor_tensor(x[:, :, col], gate, 0.5, x[:, :, col], ALU.mult, ALU.add)
                dve.drain().then_inc(x_ready, 1)

            norm_x()
            for u in (2, 3):
                low_unit(u)
            mixf, bkf = flat(mix_par), flat(bk)
            gain, c0 = {}, 0
            for name, w in EVEN_GAINS:
                gain[name] = ln_par[:, 1, c0:c0 + w]
                c0 += w

            def tmp(groups, n, at=0):
                return bkf[:, at:at + groups * n].rearrange("p (g c) -> p g c", c=n)

            split_after("cq")
            in_sbuf("cq")
            dve.wait_ge(gains_in, 16 * len(EVEN_GAINS))
            V.tensor_scalar(nv[:, 0:NT], ssq[:, :, 1], 1.0 / Q_LORA, EPS, ALU.mult, ALU.add)
            newton(NT)
            for t in range(NT):
                v = mixf[:, t * Q_LORA:(t + 1) * Q_LORA]
                last = V.scalar_tensor_tensor(v, v, ny[:, t:t + 1], gain["e_cq_norm_2"], ALU.mult, ALU.mult)
            last.then_inc(low_ready, 1)
            split_after("ckv")
            in_sbuf("ckv")
            V.tensor_scalar(nv[:, 0:NT], ssq[:, :, 2], 1.0 / KV_LORA, EPS, ALU.mult, ALU.add)
            newton(NT)
            kv = mixf[:, NT * Q_LORA:NT * (Q_LORA + KV_LORA + ROPE2)].rearrange("p (t c) -> p t c", t=NT)
            for t in range(NT):
                v = kv[:, t, 0:KV_LORA]
                last = V.scalar_tensor_tensor(v, v, ny[:, t:t + 1], gain["e_ckv_norm_2"], ALU.mult, ALU.mult)
            last.then_inc(low_ready, 1)
            group_norm(kv[:, :, KV_LORA:], k_rope[:, :, :], gain["e_kn_rope_2"], ROPE2, tmp(NT, ROPE2))
            rotate2(k_rope[:, :, :], (tmp(NT, ROPE2), tmp(NT, ROPE2, 1024)), 1)
            split_after("qb")
            in_sbuf("qb")
            v = bg_flat[:, 0:D].rearrange("p (g c) -> p g c", c=HD)
            group_norm(v, v, gain["e_dil_qn_2"], HD, tmp(16, HD), scale=HD ** -0.5, signal=heads_ready)
            low_T(l, places_cq(), yTl, yTh)
            split_after("kb")
            in_sbuf("kb")
            dve.drain()
            v = bg_flat[:, D:2 * D].rearrange("p (g c) -> p g c", c=HD)
            group_norm(v, v, gain["e_dil_kn_2"], HD, tmp(16, HD), signal=heads_ready)
            low_T(l, [place_pair(2, 3)], yTl, yTh)
            split_after("vb")
            for k in range(2):
                split_after(f"uq{k}")
            in_sbuf("uq0")
            in_sbuf("uq1")
            dve.drain()
            qa = flat(bu)[:, 0:16 * MLA_D].rearrange("p (g c) -> p g c", c=MLA_D)
            group_norm(qa[:, :, 0:MLA_N], qa[:, :, 0:MLA_N], gain["e_qn_nope_2"], MLA_N, tmp(16, MLA_N))
            group_norm(qa[:, :, MLA_N:], qa[:, :, MLA_N:], gain["e_qn_rope_2"], ROPE2, tmp(16, ROPE2))
            rotate2(qa[:, :, MLA_N:], (tmp(16, ROPE2), tmp(16, ROPE2, 1024)), MLA_H, signal=heads_ready)
            for k in range(2):
                split_after(f"ukv{k}")
            in_sbuf("ukv0")
            in_sbuf("ukv1")
            dve.drain()
            kva = flat(bval).rearrange("p (g c) -> p g c", c=P)
            ka = mixf[:, 0:16 * MLA_D].rearrange("p (g c) -> p g c", c=MLA_D)
            group_norm(kva[:, :, 0:MLA_N], ka[:, :, 0:MLA_N], gain["e_kn_nope_2"], MLA_N, tmp(16, MLA_N))
            for t in range(NT):
                last = V.tensor_copy(ka[:, t * MLA_H:(t + 1) * MLA_H, MLA_N:],
                                     k_rope[:, t:t + 1, :].to_broadcast([P, MLA_H, ROPE2]))
            last.then_inc(heads_ready, 1)
            dve.drain().then_inc(gains_free, 1)
            for b, k in ((0, 4), (1, 4), (2, 2), (3, 2)):
                n_aux[b].k += k
            heads2(MLA_H, lambda o, s, h: V.scalar_tensor_tensor(o, s, MLA_D ** -0.5, causal[:], ALU.mult, ALU.add), 0)
            heads2(DIL_H, lambda o, s, h: V.scalar_tensor_tensor(o, dist[:, 1, :], slope(h, DIL_H), s, ALU.mult,
                                                                 ALU.add), MLA_H * MLA_V, times)
            dve.drain().then_inc(o_ready, 1)
            low_T(l, places_x(), yTl, yTh)
            add_out("eout")
            ff_and_side(0)
            norm_x()
            og = [ln_par[:, 1, k * HD:(k + 1) * HD] for k in range(2)]
            for k in range(6):
                split_after(f"z{k}")
                if k in (1, 3):
                    in_sbuf(f"z{k - 1}")
                    in_sbuf(f"z{k}")
                    if k == 1:
                        dve.wait_ge(gains_in, 16 * (len(EVEN_GAINS) + len(ODD_GAINS)))
                    v = flat(bq if k == 1 else bu).rearrange("p (g c) -> p g c", c=HD)
                    dve.drain()
                    group_norm(v, v, og[k // 2], HD, tmp(32, HD), scale=HD ** -0.5 if k == 1 else 1.0,
                               signal=heads_ready)
            for b in range(4):
                n_aux[b].k += 2
            heads2(MOBA_H, lambda o, s, h: V.scalar_tensor_tensor(o, dist[:, 0, :], slope(h, MOBA_H), s, ALU.mult,
                                                                  ALU.add), 0)
            dve.drain().then_inc(o_ready, 1)
            low_T(l, places_x(), yTl, yTh)
            add_out("oout")
            ff_and_side(1)


PI32 = float(np.float32(3.1415925))


def two_pi_parts():
    parts, rest = [], 2 * np.pi
    for _ in range(2):
        _, e = np.frexp(rest)
        step = 2.0 ** (e - 11)
        c = float(np.floor(rest / step) * step)
        parts.append(c)
        rest -= c
    return parts + [float(np.float32(rest))]


def constants():
    r = np.arange(P)
    q, k = r[:, None], r[None, :]
    tri = (q <= k).astype(np.float32)
    d = np.concatenate([q - k, q + P - k, q - k], axis=1)
    causal = np.where(d >= 0, 0.0, NEG).astype(np.float32)
    times = ((d >= 0) & (d <= 128)).astype(np.float32)
    for dil in (4, 16):
        times += ((d >= 0) & (d % dil == 0)).astype(np.float32)
    dist = np.stack([np.where(d >= 0, -d, NEG), np.where(times > 0, -d, NEG)], axis=1).astype(np.float32)
    pos = np.arange(S, dtype=np.float32)
    inv = (np.float32(10000.0) ** (-np.arange(0, HD, 2, dtype=np.float32) / np.float32(HD))).astype(np.float32)
    ang = (pos[:, None] * inv[None, :]).astype(np.float32).astype(np.float64)
    cos, sin = np.cos(ang), np.sin(ang)
    rope = np.stack([np.concatenate([cos, cos], 1), np.concatenate([-sin, sin], 1)])
    rope = rope.reshape(2, NT, P, HD).transpose(2, 0, 1, 3).astype(np.float32)
    lam = 0.8 - 0.6 * np.exp(-0.3 * np.arange(DEPTH))
    half = ROPE2 // 2
    inv2 = (np.float32(10000.0) ** (-np.arange(half, dtype=np.float32) / np.float32(half))).astype(np.float32)
    return {
        "c_ident": np.eye(P, dtype=np.float32),
        "c_tri": tri,
        "c_causal": causal,
        "c_rope": np.ascontiguousarray(rope),
        "c_lam": np.stack([lam, 1.0 - lam], axis=1).astype(np.float32),
        "c_dist": np.ascontiguousarray(dist),
        "c_times": times,
        "c_inv_freq": np.broadcast_to(inv2, (P, half)).copy(),
    }


SHAPES = {
    "w_in": (DEPTH * D, -1), "gate_b": (DEPTH * 2, D), "sgu_w": (DEPTH * 8, P, P), "sgu_b": (DEPTH * 8, P),
    "lam": (DEPTH, 4 * HD), "w_branch": (DEPTH * 2 * D, D), "w_out": (DEPTH * D, D),
    "ffn_w1": (DEPTH * 2 * D, F1), "ffn_w3": (DEPTH * 2 * D, F1), "ffn_w2": (DEPTH * 2 * F1, D),
    "ln_g": (DEPTH * 3, D), "ln_b": (DEPTH * 3, D),
    "p_2": (DEPTH * S, 256), "e_w_in_2": (D, -1), "e_w_uq_2": (Q_LORA, -1), "e_w_ukv_2": (KV_LORA, -1),
    "e_w_out_2": (D, D), "o_w_in_2": (D, -1), "o_w_out_2": (D, D), "w_ff1_2": (DEPTH * D, F2),
    "w_ff2_2": (DEPTH * F2, D), "w_ple_gate_2": (DEPTH * D, D), "w_ple_proj_2": (DEPTH * 256, D),
}


def kernel(**inputs):
    from concourse.bacc import Bacc
    from concourse.bass_utils import run_bass_kernel_spmd

    nc = Bacc("TRN2", target_bir_lowering=False, num_devices=1, dynamic_dma_scratch_size=4096)
    arrays, args = {}, {}
    for name, value in {**inputs, **constants()}.items():
        v = np.ascontiguousarray(value)
        if name in SHAPES:
            v = v.reshape(SHAPES[name])
        arrays[name] = v
        args[name] = nc.dram_tensor(name, v.shape, mybir.dt.from_np(v.dtype), kind="ExternalInput").ap()
    out = nc.dram_tensor("out", (1, S, D), F32, kind="ExternalOutput").ap()
    build(nc, args, out)
    return run_bass_kernel_spmd(nc, [arrays], core_ids=[0]).results[0]["out"]
```

```python
from contextlib import ExitStack

import numpy as np

import concourse.bass as bass
from concourse import mybir

F32 = mybir.dt.float32
F32R = mybir.dt.float32r
I32 = mybir.dt.int32
ALU = mybir.AluOpType
ACT = mybir.ActivationFunctionType
AX_X = mybir.AxisListType.X

P = 128
S = 256
NT = S // P
D = 1024
KT = D // P
DEPTH = 2
RING = 4
UNIT = 2048
NC = 512
NEG = -1.0e30

F1 = 2816
FB = 256
NF = F1 // FB
H1 = 8
HD = 64
ALPHA = (2.0 * DEPTH) ** 0.25
LN_EPS = 1e-5
CH = 20
IN_COLS = [1024, 1536, 0, 512, 2048, 2560, 3072, 3584, 4096, 4608, 5120, 5632, 6144, 6656]
HEAD_UNITS = [[20, 21], [22, 23], [24, 25], [26, 27], [28], [29], [30], [31]]

ACC_LAYER = 2 + CH // 2
USED_LAYER = 2 * (NF + NF - 1) + 3 * 3
SLOT_LAYER = tuple((2 * NF if s < 3 else 0) + CH // 2 for s in range(RING))
AUX_LAYER = tuple((2 * NF if b < 3 else 0) + 6 + 2 + 1 + (1 if b < 2 else 0) + H1 for b in range(4))

EPS = 1e-6
F2 = 4096
FB2 = 512
NF2 = F2 // FB2
Q_LORA, KV_LORA, ROPE2 = 384, 256, 32
MLA_H, MLA_N, MLA_V = 8, 64, 64
MLA_D = MLA_N + ROPE2
DIL_H = 8
MOBA_H = 16
EVEN_GAINS = [("e_cq_norm_2", Q_LORA), ("e_ckv_norm_2", KV_LORA), ("e_qn_nope_2", MLA_N),
              ("e_qn_rope_2", ROPE2), ("e_kn_nope_2", MLA_N), ("e_kn_rope_2", ROPE2),
              ("e_dil_qn_2", HD), ("e_dil_kn_2", HD)]
ODD_GAINS = [("o_qn_2", HD), ("o_kn_2", HD)]
PI = float(np.pi)


def jobs_of_block2():
    jobs = []

    def chunk(name, w, row0, col0, cols, kts, split):
        units = [(k0, k1, cols, w, row0 + k0 * P, col0) for k0, k1 in split]
        jobs.append(dict(name=name, units=units, wide=False, cols=cols, kts=kts))

    def quad(name, w, row0, cols):
        c0 = (0, cols[0])
        units = [(k0, k0 + 4, cols[h], w, row0 + k0 * P, c0[h]) for h in range(2) for k0 in (0, 4)]
        jobs.append(dict(name=name, units=units, wide=True, cols=cols))

    full = [(0, 4), (4, 8)]
    quad("c", "e_w_in_2", 0, (Q_LORA, KV_LORA + ROPE2))
    for k, name in enumerate(("qb", "kb", "vb")):
        chunk(name, "e_w_in_2", 0, Q_LORA + KV_LORA + ROPE2 + k * NC, NC, KT, full)
    for k in range(2):
        chunk(f"uq{k}", "e_w_uq_2", 0, k * 384, 384, 3, [(0, 3)])
    for k in range(2):
        chunk(f"ukv{k}", "e_w_ukv_2", 0, k * NC, NC, 2, [(0, 2)])
    quad("eout", "e_w_out_2", 0, (NC, NC))

    def ff_and_side(i):
        jobs.append(dict(name=f"ff{i}", units=None, wide=True, i=i))
        jobs.append(dict(name=f"side{i}", units=[(0, 2, D, "w_ple_proj_2", i * 256, 0)], wide=True))
        quad(f"g{i}", "w_ple_gate_2", i * D, (NC, NC))

    ff_and_side(0)
    quad("z01", "o_w_in_2", 0, (NC, NC))
    for k in range(2, 6):
        chunk(f"z{k}", "o_w_in_2", 0, k * NC, NC, KT, full)
    quad("oout", "o_w_out_2", 0, (NC, NC))
    ff_and_side(1)
    u, acc, par, slots, used = 0, [0, 0], 0, [0] * RING, 0
    after_wide = True
    for g in jobs:
        g["u0"], g["used"], g["after_wide"] = u, used, after_wide
        after_wide = g["wide"]
        used += 2 * (NF2 - 1) + NF2 + 1 if g["units"] is None else len(g["units"]) - 1 if g["wide"] else 0
        g["slots"] = []
        if g["units"] is None:
            s0 = u % RING
            g["s0"], g["n0"] = s0, list(slots)
            for s in range(RING):
                slots[s] += NF2
            g["nu"] = NF2 * RING
            u += RING * NF2
        else:
            for _ in g["units"]:
                g["slots"].append((u % RING, slots[u % RING]))
                slots[u % RING] += 1
                u += 1
            g["nu"] = len(g["units"])
        if g["wide"]:
            g["acc"] = [(0, acc[0]), (1, acc[1])]
            acc = [acc[0] + 1, acc[1] + 1]
        else:
            g["acc"] = [(par, acc[par])]
            acc[par] += 1
            par = 1 - par
    return jobs


JOBS = jobs_of_block2()
JOB = {g["name"]: g for g in JOBS}


def job_of_unit(u):
    return next(g for g in JOBS if g["u0"] <= u < g["u0"] + g["nu"])


N_UNITS = JOBS[-1]["u0"] + JOBS[-1]["nu"]


def units_after(g):
    end = g["u0"] + g["nu"]
    return [u for u in range(g["u0"] + RING, min(end + RING, N_UNITS)) if not in_ff(u)]


def in_ff(u):
    g = job_of_unit(u)
    return g["units"] is None and u - g["u0"] >= 2


class Uses:

    def __init__(self, per):
        self.per = per
        self.k = 0

    def at(self, layer):
        return layer * self.per + self.k

    def take(self, layer):
        n = self.at(layer)
        self.k += 1
        return n

    def layer_ends(self):
        assert self.k == self.per, (self.k, self.per)
        self.k = 0


def rows(ap, row0, n, col0, nc):
    r = ap[row0:row0 + n, :] if isinstance(row0, int) else ap[bass.ds(row0, n), :]
    r = r[:, col0:col0 + nc] if isinstance(col0, int) else r[:, bass.ds(col0, nc)]
    return r.rearrange("(k p) n -> p k n", p=P)


def slope(h, n):
    return float(np.float32(2.0) ** np.float32(-8.0 * (h + 1) / n))


def build(nc, a, out, stop=None):
    ctx = ExitStack()
    with ctx:
        def sb(name, shape, dt=F32):
            return ctx.enter_context(nc.sbuf_tensor(name, shape, dt))

        def sem(name):
            return ctx.enter_context(nc.semaphore(name))

        raw = sb("w_raw", [P, RING, UNIT])
        whi = sb("w_high", [P, RING, UNIT], F32R)
        wlo = sb("w_low", [P, RING, UNIT], F32R)
        x = sb("x_res", [P, NT, D])
        xTh = sb("xT_high", [P, KT, S], F32R)
        xTl = sb("xT_low", [P, KT, S], F32R)
        yTh = sb("yT_high", [P, KT, S], F32R)
        yTl = sb("yT_low", [P, KT, S], F32R)
        bv = sb("buf_v", [P, NT, D])
        bu = sb("buf_u", [P, NT, D])
        bq = sb("buf_q", [P, NT, D])
        bk = sb("buf_k", [P, NT, D])
        bval = sb("buf_val", [P, NT, D])
        bg = sb("buf_gates", [P, 2, NT, D])
        ln_par = sb("ln_param", [P, 2, D])
        mix_par = sb("mix_param", [P, 2, D])
        ident = sb("ident", [P, P])
        tri = sb("tri", [P, P])
        causal = sb("causal", [P, 3 * P])
        rope = sb("rope_tab", [P, 2, NT, HD])
        lam_init = sb("lam_init", [P, 2])
        diff_g = sb("diff_g", [P, 2 * HD])
        sgu_bT = sb("sgu_bT", [P, 8])
        aT = sb("probs_T", [P, 3 * P])
        junk = sb("junk", [P, 4])
        stat = sb("stat", [P, NT, 2, 6])
        mv = sb("mean_var", [P, NT, 2])
        nv = sb("group_var", [P, 32])
        ny = sb("inverse_root", [P, 32])
        EPS1 = (4 * LN_EPS, LN_EPS, 2.0 * HD * LN_EPS)
        eps_tile = sb("epsilons", [P, 2 * len(EPS1)])
        minus_half = sb("minus_half", [P, 32])
        nx = sb("inverse_root_x", [P, 2 * NT])
        lam_t = sb("lam_t", [P, 4])
        neg_lam = sb("neg_lam", [P, 1])
        rmax = sb("row_max", [P, 2, 4])
        rsum = sb("row_sum", [P, 2, 4])
        rinv = sb("row_inv", [P, 2, 4])
        ssq = sb("sum_sq", [P, NT, H1])
        dist = sb("neg_distance", [P, 2, 3 * P])
        times = sb("pattern_count", [P, 3 * P])
        pos_i = sb("pos_i", [P, NT], I32)
        rope2 = sb("rope2", [P, 2, NT, ROPE2])
        k_rope = sb("k_rope", [P, NT, ROPE2])

        def flat(t):
            return t[:, :, :].rearrange("p t d -> p (t d)")

        bg_flat = bg[:, :, :, :].rearrange("p a t d -> p (a t d)")
        ang = flat(bval)[:, 0:P].rearrange("p (k t c) -> p k t c", k=4, t=NT)
        inv_freq = flat(bval)[:, P:P + ROPE2 // 2]
        lam_w = bg_flat[:, 2 * D:2 * D + 4 * HD]
        act_b = flat(bk)[:, 0:NT * NC].rearrange("p (t f) -> p t f", t=NT)
        gate_b = flat(bk)[:, NT * NC:2 * NT * NC].rearrange("p (t f) -> p t f", t=NT)
        sgu_raw = bval[:, 0, :].rearrange("p (g r) -> p g r", g=8)
        wT = bg_flat[:, 0:D].rearrange("p (g r) -> p g r", g=8)
        qT = flat(bv).rearrange("p (h s) -> p h s", s=S)
        kT = flat(bq).rearrange("p (h s) -> p h s", s=S)
        SE = flat(bk)[:, 0:4 * 3 * P].rearrange("p (b m c) -> p b m c", b=2, m=2)
        pa = flat(bk)[:, 4 * 3 * P:5 * 3 * P]

        acc = ctx.enter_context(nc.psum_tensor("acc", [P, 2, NT, NC], F32))
        aux = ctx.enter_context(nc.psum_tensor("aux", [P, 4, NC], F32))

        slot_full = [sem(f"slot_full{s}") for s in range(RING)]
        slot_hi = [sem(f"slot_hi{s}") for s in range(RING)]
        slot_lo = [sem(f"slot_lo{s}") for s in range(RING)]
        acc_full = [sem("acc_full0"), sem("acc_full1")]
        acc_read = [sem("acc_read0"), sem("acc_read1")]
        aux_full = [sem(f"aux_full{b}") for b in range(4)]
        aux_read = [sem(f"aux_read{b}") for b in range(4)]
        unit_used = sem("unit_used")
        var_ready = sem("var_ready")
        rstd_ready = sem("rstd_ready")
        t_hi = sem("t_hi")
        act_done = sem("act_done")
        x_ready = sem("x_ready")
        tanh_done = sem("tanh_done")
        vn_ready = sem("vn_ready")
        roped = sem("roped")
        s_ready = sem("s_ready")
        e_ready = sem("e_ready")
        a_ready = sem("a_ready")
        m_ready = sem("m_ready")
        lam_dot = sem("lam_dot")
        lam_exp = sem("lam_exp")
        const_in = sem("const_in")
        x_in = sem("x_in")
        ln_in = sem("ln_in")
        ln_free = sem("ln_free")
        mix_in = sem("mix_in")
        mix_free = sem("mix_free")
        small_in = sem("small_in")
        small_free = sem("small_free")
        gains_in = sem("gains_in")
        side_in = sem("side_in")
        sq_ready = sem("sq_ready")
        sumsq = sem("sumsq")
        xn_ready = sem("xn_ready")
        low_ready = sem("low_ready")
        heads_ready = sem("heads_ready")
        angles = sem("angles")
        sines = sem("sines")
        o_ready = sem("o_ready")
        out_done = sem("out_done")

        block = ctx.enter_context(nc.Block())
        L2 = DEPTH

        def cast(ap):
            return ap.bitcast(F32)

        def slot_n2(s, n):
            return L2 * SLOT_LAYER[s] + n

        def acc_n2(p, n):
            return L2 * ACC_LAYER + n

        def used_n2(n):
            return L2 * USED_LAYER + n

        RSTD_V, RSTD_HEADS, RSTD_NORM = 2, 4, (0, 4 + H1, 6 + H1)
        RSTD_LAYER = 8 + H1
        X_LAYER = 12
        X_LAST = 4 + X_LAYER * DEPTH

        def mixer_n(l, u):
            s = u % RING
            return l * SLOT_LAYER[s] + (NF if s < 3 else 0) + u // RING

        @block.sync
        def _(sp):
            sp.dma_start(x[:], a["x"].rearrange("b (t p) d -> p (b t) d", p=P)).then_inc(x_in, 16)

            def load(s, n, parts):
                sp.wait_ge(slot_lo[s], n + 1)
                for dst, src in parts:
                    sp.dma_start(dst, src).then_inc(slot_full[s], 32 // len(parts))

            def hidden1(l, which, i):
                for j in range(2):
                    dst = raw[:, j, :].rearrange("p (m k n) -> p m k n", m=2, k=4)
                    r0 = (l * 2 + which) * D + j * 4 * P
                    load(j, l * SLOT_LAYER[0] + (NF + CH // 2) * which + i,
                         [(dst[:, 0], rows(a["ffn_w1"], r0, 4 * P, i * FB, FB)),
                          (dst[:, 1], rows(a["ffn_w3"], r0, 4 * P, i * FB, FB))])

            def down1(l, which, i):
                dst = raw[:, 2, :].rearrange("p (k n) -> p k n", k=2)
                load(2, l * SLOT_LAYER[2] + (NF + CH // 2) * which + i,
                     [(dst, rows(a["ffn_w2"], (l * 2 + which) * F1 + i * FB, FB, 0, D))])

            def ffn1(l, which):
                with sp.Fori(0, NF - 1) as i:
                    hidden1(l, which, i + 1)
                    down1(l, which, i)

            def mixer_unit(l, u):
                c, j = divmod(u, 2)
                if u in (4, 5, 36, 37):
                    w = a["w_in" if c == 2 else "w_out"]
                    src = tuple(rows(w, l * D + (4 * j + k) * P, 2 * P, 0, NC) for k in (2, 0))
                elif c < 14:
                    src = rows(a["w_in"], l * D + j * 4 * P, 4 * P, IN_COLS[c], NC)
                elif c < 18:
                    src = rows(a["w_branch"], (l * 2 + (c - 14) // 2) * D + j * 4 * P, 4 * P,
                               (c % 2) * NC, NC)
                else:
                    src = rows(a["w_out"], l * D + j * 4 * P, 4 * P, (c % 2) * NC, NC)
                dst = raw[:, u % RING, :].rearrange("p (k n) -> p k n", k=4)
                if isinstance(src, tuple):
                    parts = [(dst[:, 2:4], src[0]), (dst[:, 0:2], src[1])]
                else:
                    parts = [(dst, src)]
                load(u % RING, mixer_n(l, u), parts)

            with sp.Fori(0, DEPTH) as l:
                hidden1(l, 0, 0)
                ffn1(l, 0)
                for u in (0, 1, 3):
                    mixer_unit(l, u)
                down1(l, 0, NF - 1)
                for u in (2, *range(4, 2 * CH)):
                    mixer_unit(l, u)
                hidden1(l, 1, 0)
                ffn1(l, 1)
                down1(l, 1, NF - 1)

            def load_unit(u):
                if u >= N_UNITS:
                    return
                g = job_of_unit(u)
                if g["units"] is None:
                    ff_unit(g, u - g["u0"], 0)
                else:
                    s, n = g["slots"][u - g["u0"]]
                    k0, k1, cols, w, r0, c0 = g["units"][u - g["u0"]]
                    dst = raw[:, s, 0:(k1 - k0) * cols].rearrange("p (k n) -> p k n", k=k1 - k0)
                    load(s, slot_n2(s, n), [(dst, rows(a[w], r0, (k1 - k0) * P, c0, cols))])

            def ff_unit(g, j, i):
                s = (g["s0"] + j) % RING
                dst = raw[:, s, :].rearrange("p (k n) -> p k n", k=4 if j < 2 else 2)
                if j < 2:
                    src = rows(a["w_ff1_2"], g["i"] * D + j * 4 * P, 4 * P, i * FB2, FB2)
                else:
                    src = rows(a["w_ff2_2"], g["i"] * F2 + i * FB2 + (j - 2) * 2 * P, 2 * P, 0, D)
                load(s, slot_n2(s, g["n0"][s]) + i, [(dst, src)])

            u = 0
            while u < (N_UNITS if stop is None else 2):
                g = job_of_unit(u)
                if g["units"] is None and u == g["u0"] + 2:
                    with sp.Fori(0, NF2 - 1) as i:
                        ff_unit(g, 0, i + 1)
                        ff_unit(g, 1, i + 1)
                        ff_unit(g, 2, i)
                        ff_unit(g, 3, i)
                    end = g["u0"] + g["nu"]
                    load_unit(end)
                    load_unit(end + 1)
                    ff_unit(g, 2, NF2 - 1)
                    ff_unit(g, 3, NF2 - 1)
                    u = end + 2
                else:
                    load_unit(u)
                    u += 1
            for t in range(NT):
                sp.wait_ge(x_ready, X_LAST + (10 + t + 1 if stop is None else 0))
                sp.dma_start(out.rearrange("b (t p) d -> p (b t) d", p=P)[:, t, :], x[:, t, :])\
                    .then_inc(out_done, 16)
            sp.wait_ge(out_done, 16 * NT)

        @block.gpsimd
        def _(pool):
            consts = ((ident[:], a["c_ident"]), (tri[:], a["c_tri"]), (causal[:], a["c_causal"]),
                      (rope[:], a["c_rope"]), (dist[:], a["c_dist"]),
                      (times[:], a["c_times"]), (inv_freq, a["c_inv_freq"]))
            for dst, src in consts:
                pool.dma_start(dst, src).then_inc(const_in, 16)
            with nc.allow_non_contiguous_dma(reason="256 positions onto partitions"):
                pool.dma_start(pos_i[:], a["positions_2"].rearrange("b (t p) -> p (b t)", p=P))\
                    .then_inc(const_in, 16)

            def norm_params(l, k):
                n = l * 3 + k
                pool.wait_ge(ln_free, n + 1)
                for w, name in enumerate(("ln_g", "ln_b")):
                    pool.dma_start(ln_par[:, w, :], a[name][bass.ds(n, 1), :].partition_broadcast(P))\
                        .then_inc(ln_in, 16)

            nc.gpsimd.memset(minus_half[:], -0.5)
            for k, eps in enumerate(EPS1):
                nc.gpsimd.memset(eps_tile[:, 2 * k:2 * k + 2], eps)
            pool.drain()

            def inverse_root(dst, src, eps):
                if eps in EPS1:
                    k = EPS1.index(eps)
                    nc.gpsimd.tensor_tensor(dst, src, eps_tile[:, 2 * k:2 * k + dst.shape[1]], ALU.add)
                else:
                    nc.gpsimd.tensor_scalar(dst, src, eps, None, ALU.add)
                pool.drain()
                nc.gpsimd.tensor_tensor(dst, dst, minus_half[:, 0:dst.shape[1]], ALU.pow).then_inc(rstd_ready, 1)

            def tile_roots(l, n, col, eps):
                for t in range(NT):
                    pool.wait_ge(var_ready, 8 * l + 2 * n + t + 1)
                    inverse_root(nx[:, col + t:col + t + 1], mv[:, t, 1:2], eps)

            with pool.Fori(0, DEPTH) as l:
                norm_params(l, 0)
                pool.wait_ge(small_free, l + 1)
                pool.dma_start(sgu_raw, a["sgu_w"][bass.ds(l * 8, 8), :, :].rearrange("g t r -> t g r"))\
                    .then_inc(small_in, 16)
                with nc.allow_non_contiguous_dma(reason="1024 biases onto partitions"):
                    pool.dma_start(sgu_bT[:], a["sgu_b"][bass.ds(l * 8, 8), :].rearrange("g t -> t g"))\
                        .then_inc(small_in, 16)
                pool.dma_start(diff_g[:], a["diff_ln_g"][bass.ds(l, 1), :].partition_broadcast(P))\
                    .then_inc(small_in, 16)
                pool.dma_start(lam_w, a["lam"][bass.ds(l, 1), :].partition_broadcast(P))\
                    .then_inc(small_in, 16)
                pool.dma_start(lam_init[:], a["c_lam"][bass.ds(l, 1), :].partition_broadcast(P))\
                    .then_inc(small_in, 16)
                pool.wait_ge(mix_free, 2 * l + 1)
                for w, name in enumerate(("sgu_ln_g", "sgu_ln_b")):
                    pool.dma_start(mix_par[:, w, :], a[name][bass.ds(l, 1), :].partition_broadcast(P))\
                        .then_inc(mix_in, 16)
                tile_roots(l, 0, 0, 4 * LN_EPS)
                norm_params(l, 1)
                tile_roots(l, 1, NT, LN_EPS)
                pool.wait_ge(mix_free, 2 * l + 2)
                for w in range(2):
                    pool.dma_start(mix_par[:, w, :], a["gate_b"][bass.ds(l * 2 + w, 1), :].partition_broadcast(P))\
                        .then_inc(mix_in, 16)
                for h in range(H1):
                    pool.wait_ge(sq_ready, H1 * l + h + 1)
                    inverse_root(ny[:, NT * h:NT * h + NT], ssq[:, :, h], 2.0 * HD * LN_EPS)
                tile_roots(l, 2, 0, 4 * LN_EPS)
                norm_params(l, 2)
                tile_roots(l, 3, 0, 4 * LN_EPS)
            if stop == 1:
                return
            pool.wait_ge(ln_free, 3 * DEPTH + 1)
            n = 0
            n_var = [8 * DEPTH]

            def group_roots(groups, eps):
                n_var[0] += 1
                pool.wait_ge(var_ready, n_var[0])
                inverse_root(ny[:, 0:groups], nv[:, 0:groups], eps)

            for i in range(2):
                for name, n_rms in (("mix_norm_2", 0), ("ff_norm_2", 1), ("ple_norm_2", 2)):
                    pool.wait_ge(ln_free, 3 * DEPTH + 1 + n)
                    pool.dma_start(ln_par[:, 0, :], a[name][i:i + 1, :].partition_broadcast(P))\
                        .then_inc(ln_in, 32)
                    if n_rms == 0:
                        c0 = 0
                        gains = EVEN_GAINS if i == 0 else ODD_GAINS
                        for gname, w in gains:
                            pool.dma_start(ln_par[:, 1, c0:c0 + w], a[gname].partition_broadcast(P))\
                                .then_inc(gains_in, 16)
                            c0 += w
                    for t in range(NT):
                        pool.wait_ge(sumsq, 2 * n + t + 1)
                        inverse_root(nx[:, t:t + 1], ssq[:, t, 0:1], EPS)
                    if n_rms == 0 and i == 0:
                        group_roots(2 * NT, EPS)
                        for groups, width in ((NT, ROPE2), (16, HD), (16, HD), (16, MLA_N), (16, ROPE2),
                                              (16, MLA_N)):
                            group_roots(groups, EPS * width)
                    elif n_rms == 0:
                        group_roots(32, EPS * HD)
                        group_roots(32, EPS * HD)
                    n += 1
                    if n_rms == 1:
                        pool.wait_ge(ln_free, 3 * DEPTH + 1 + n)
                        pool.dma_start(bq[:, :, 0:256],
                                       a["p_2"][i * S:(i + 1) * S, :].rearrange("(t p) n -> p t n", p=P))\
                            .then_inc(side_in, 16)

        @block.tensor
        def _(pe):
            n_acc = [Uses(ACC_LAYER), Uses(ACC_LAYER)]
            n_aux = [Uses(k) for k in AUX_LAYER]

            pe.wait_ge(const_in, 8 * 16)

            def aux_wait(l, b):
                pe.wait_ge(aux_read[b], n_aux[b].at(l) + 1)

            def aux_all(l, banks=range(4)):
                for b in banks:
                    aux_wait(l, b)

            def aux_end(b, last):
                last.then_inc(aux_full[b], 1)
                n_aux[b].k += 1

            def products(dst, tiles, k_first, k_last, lh, ll, t, rh, rl):
                tok = slice(t * P, (t + 1) * P)
                for kt, j in tiles:
                    for q, (lhs, rhs) in enumerate(((lh, rh), (lh, rl), (ll, rh))):
                        last = nc.tensor.matmul(dst, lhs[:, kt, tok], rhs(j),
                                                start=(kt == k_first and q == 0),
                                                stop=(kt == k_last and q == 2))
                return last

            def transpose_tile(l, src, t, ready=None):
                for half in range(2):
                    b = 2 * t + half
                    if ready is not None:
                        ready(half)
                    aux_wait(l, b)
                    for k in range(4):
                        kt = half * 4 + k
                        last = nc.tensor.transpose(aux[:, b, k * P:(k + 1) * P],
                                                   src[:, t, kt * P:(kt + 1) * P], ident[:])
                    aux_end(b, last)

            def tile_split(l, t):
                for b in (2 * t, 2 * t + 1):
                    aux_wait(l, b)

            def acc_wait(l, t, after_wide):
                if after_wide:
                    pe.wait_ge(acc_read[t], n_acc[t].at(l) + 1)
                elif t == 0:
                    for p in range(2):
                        pe.wait_ge(acc_read[p], n_acc[p].at(l) + 1)

            def quad(l, units, lh, ll, after_wide, tile1=None, ahead=None):
                for t in range(NT):
                    acc_wait(l, t, after_wide)
                    tile_split(l, t)
                    for j, (s, n, cols) in enumerate(units):
                        if t == 0 and j == 3 and tile1 is not None:
                            tile1()
                        if t == 1 and j == 3 and ahead is not None:
                            ahead()
                        if t == 0:
                            pe.wait_ge(slot_lo[s], n + 2)
                        half, k0 = j // 2, 4 * (j % 2)
                        vh, vl = (w[:, s, 0:4 * cols].rearrange("p (k n) -> p k n", k=4) for w in (whi, wlo))
                        last = products(acc[:, half, t, 0:cols], [(k0 + k, k) for k in range(4)], 0, KT - 1,
                                        lh, ll, t, lambda k: vh[:, k, :], lambda k: vl[:, k, :])
                        if j == 3:
                            last.then_inc(acc_full[t], 1)
                        elif t == 1:
                            last.then_inc(unit_used, 1)
                for p in range(2):
                    n_acc[p].k += 1

            def feed_forward(l, slot0, which_slots, hid_view, n_f, iters, tile1, before_last=None):
                aux0 = [n_aux[0].at(l), n_aux[1].at(l)]
                t_banks = [2] if n_f == 2 else [2, 3]
                down_slots = which_slots[2:]

                def hidden(i, t):
                    pe.wait_ge(aux_read[t], aux0[t] + i + 1)
                    for j in range(2):
                        s = which_slots[j]
                        if t == 0:
                            pe.wait_ge(slot_lo[s], slot0(s) + i + 2)
                        vh, vl = hid_view(whi[:, s, :]), hid_view(wlo[:, s, :])
                        dst = aux[:, t, :]
                        if n_f == 2:
                            dst = dst.rearrange("p (m n) -> p m n", m=2)
                        last = products(dst, [(4 * j + k, k) for k in range(4)], 0, KT - 1, xTh, xTl, t, vh, vl)
                        if j == 1:
                            last.then_inc(aux_full[t], 1)
                        elif t == 1:
                            last.then_inc(unit_used, 1)

                def transposes(i):
                    for t in range(NT):
                        pe.wait_ge(aux_read[t], aux0[t] + i + 2)
                    for b in t_banks:
                        pe.wait_ge(aux_read[b], aux0[b] + i + 1)
                        for f in range(2):
                            for t in range(NT):
                                f0 = ((b - 2) * 2 + f) * P
                                last = nc.tensor.transpose(aux[:, b, (2 * f + t) * P:(2 * f + t + 1) * P],
                                                           gate_b[:, t, f0:f0 + P], ident[:])
                        last.then_inc(aux_full[b], 1)

                def down_part(i, q, t, first, final):
                    s = down_slots[q]
                    if t == 0:
                        pe.wait_ge(slot_lo[s], slot0(s) + i + 2)
                        pe.wait_ge(aux_read[2 + q], aux0[2 + q] + i + 2)
                    vh, vl = (w[:, s, :].rearrange("p (k n) -> p k n", k=2) for w in (whi, wlo))
                    for half in range(2):
                        col = slice(half * NC, (half + 1) * NC)
                        last = products(acc[:, half, t, :], [(2 * q + k, k) for k in range(2)],
                                        0 if first else -1, n_f - 1 if final else -1, yTh, yTl, t,
                                        lambda k: vh[:, k, col], lambda k: vl[:, k, col])
                    return last

                def down(i, first=False):
                    for q in range(len(down_slots)):
                        for t in range(NT):
                            last = down_part(i, q, t, first, False)
                        last.then_inc(unit_used, 1)

                def last_down(i):
                    for t in range(NT):
                        for q in range(len(down_slots)):
                            last = down_part(i, q, t, False, True)
                            if q == len(down_slots) - 1:
                                last.then_inc(acc_full[t], 1)
                            elif t == 1:
                                last.then_inc(unit_used, 1)

                tile_split(l, 0)
                hidden(0, 0)
                tile1()
                tile_split(l, 1)
                aux0 += [n_aux[2].at(l), n_aux[3].at(l)]
                hidden(0, 1)
                hidden(1, 0)
                transposes(0)
                hidden(1, 1)
                for p in range(2):
                    pe.wait_ge(acc_read[p], n_acc[p].at(l) + 1)
                down(0, first=True)
                with pe.Fori(2, iters) as i:
                    hidden(i, 0)
                    transposes(i - 1)
                    hidden(i, 1)
                    down(i - 1)
                transposes(iters - 1)
                for b in [0, 1, *t_banks]:
                    n_aux[b].k += iters
                if before_last is not None:
                    before_last()
                last_down(iters - 1)
                for p in range(2):
                    n_acc[p].k += 1

            def ffn1(l, which):
                def view(w):
                    v = w.rearrange("p (m k n) -> p m k n", m=2, k=4)
                    return lambda k: v[:, :, k, :]

                feed_forward(l, lambda s: l * SLOT_LAYER[s] + (NF + CH // 2) * which, [0, 1, 2], view, 2, NF,
                             lambda: x_T(l, 2 * which, 1))

            def x_T(l, k, t):
                transpose_tile(l, x, t, lambda half: pe.wait_ge(x_ready, X_LAYER * l + 4 * k + 2 * t + half + 1))

            def mixer_quad(l, u0, lh, ll, after_wide, tile1=None, ahead=None):
                quad(l, [(u % RING, mixer_n(l, u), NC) for u in range(u0, u0 + 4)], lh, ll, after_wide,
                     tile1, ahead)

            def chunk_unit(l, u, lh, ll):
                c, j = divmod(u, 2)
                s, p = u % RING, c % 2
                pe.wait_ge(slot_lo[s], mixer_n(l, u) + 2)
                if j == 0:
                    pe.wait_ge(acc_read[p], n_acc[p].take(l) + 1)
                vh, vl = (w[:, s, :].rearrange("p (k n) -> p k n", k=4) for w in (whi, wlo))
                for t in range(NT):
                    if c == 2 and j == 0 and t == 1:
                        pe.wait_ge(acc_read[1], n_acc[1].at(l) + 1)
                    last = products(acc[:, p, t, :], [(4 * j + k, k) for k in range(4)], 0, KT - 1, lh, ll, t,
                                    lambda k: vh[:, k, :], lambda k: vl[:, k, :])
                if j == 1:
                    last.then_inc(acc_full[p], 1)

            def chunk(l, c, lh=xTh, ll=xTl):
                chunk_unit(l, 2 * c, lh, ll)
                chunk_unit(l, 2 * c + 1, lh, ll)

            def transpose_heads(l, src, n, width=P, banks=range(4), heads=2):
                for q, b in enumerate(banks):
                    aux_wait(l, b)
                    for k in range(heads):
                        for t in range(NT):
                            h = heads * q + k
                            last = nc.tensor.transpose(aux[0:width, b, (2 * k + t) * P:(2 * k + t + 1) * P],
                                                       src(t, h), ident[:])
                    aux_end(b, last)

            def scores(l, h):
                for m in range(2):
                    aux_wait(l, m)
                    d = slice(m * HD, (m + 1) * HD)
                    nc.tensor.matmul(aux[:, m, 0:P], qT[d, h, 0:P], kT[d, h, 0:P], start=True, stop=True)
                    last = nc.tensor.matmul(aux[:, m, P:3 * P], qT[d, h, P:S], kT[d, h, 0:S],
                                            start=True, stop=True)
                    aux_end(m, last)

            def prob_transposes(l, src):
                aux_wait(l, 2)
                for k in range(3):
                    last = nc.tensor.transpose(aux[:, 2, k * P:(k + 1) * P], src[:, k * P:(k + 1) * P], ident[:])
                aux_end(2, last)

            def values(l, v, width):
                aux_wait(l, 2)
                aux_wait(l, 3)
                nc.tensor.matmul(aux[:, 3, 0:width], aT[:, 0:P], v[0], start=True, stop=True)
                o1 = aux[:, 3, width:2 * width]
                nc.tensor.matmul(o1, aT[:, P:2 * P], v[0], start=True, stop=False)
                last = nc.tensor.matmul(o1, aT[:, 2 * P:3 * P], v[1], start=False, stop=True)
                aux_end(3, last)

            def mixer(l):
                x_T(l, 1, 0)
                mixer_quad(l, 0, xTh, xTl, True, tile1=lambda: x_T(l, 1, 1))
                pe.wait_ge(small_in, 80 * l + 80)
                for b in range(2):
                    aux_wait(l, b)
                    for k in range(4):
                        last = nc.tensor.transpose(aux[:, b, k * P:(k + 1) * P], sgu_raw[:, 4 * b + k, :], ident[:])
                    aux_end(b, last)
                chunk(l, 2)
                chunk(l, 3)
                chunk(l, 4)
                aux_all(l)
                pe.wait_ge(vn_ready, 2 * l + 2)
                for b in range(4):
                    for k in range(2):
                        g = 2 * b + k
                        last = nc.tensor.matmul(aux[:, b, k * S:(k + 1) * S].rearrange("p (t c) -> p t c", t=NT),
                                                wT[:, g, :], bv[:, :, g * P:(g + 1) * P], start=True, stop=True)
                    aux_end(b, last)
                chunk(l, 5)
                aux_all(l)
                for t in range(NT):
                    transpose_tile(l, bu, t)
                chunk(l, 6)
                pe.wait_ge(roped, 4 * l + 2)
                transpose_heads(l, lambda t, h: bq[:, t, h * P:(h + 1) * P], 8)
                chunk(l, 7)
                chunk(l, 8)
                pe.wait_ge(roped, 4 * l + 4)
                transpose_heads(l, lambda t, h: bk[:, t, h * P:(h + 1) * P], 8)
                chunk(l, 9)
                aux_all(l)
                scores(l, 0)
                for h in range(H1):
                    for u in HEAD_UNITS[h]:
                        chunk_unit(l, u, *((xTh, xTl) if u < 28 else (yTh, yTl)))
                    pe.wait_ge(a_ready, l * H1 + h + 1)
                    prob_transposes(l, pa)
                    if h + 1 < H1:
                        scores(l, h + 1)
                    if h == 0:
                        for p in range(2):
                            pe.wait_ge(acc_read[p], l * ACC_LAYER + 7)
                    values(l, [bval[:, t, h * P:(h + 1) * P] for t in range(NT)], P)
                aux_wait(l, 3)
                for t in range(NT):
                    transpose_tile(l, bu, t)

                def m_T(t):
                    transpose_tile(l, bg[:, 0], t, lambda half: pe.wait_ge(m_ready, 2 * l + t + 1))

                mixer_quad(l, 32, xTh, xTl, False, ahead=lambda: m_T(0))
                mixer_quad(l, 36, yTh, yTl, True, tile1=lambda: m_T(1), ahead=lambda: x_T(l, 2, 0))

            with pe.Fori(0, DEPTH) as l:
                x_T(l, 0, 0)
                ffn1(l, 0)
                mixer(l)
                ffn1(l, 1)
                for c in n_aux + n_acc:
                    c.layer_ends()
            if stop == 1:
                return

            l = L2

            def job(name, lh=xTh, ll=xTl, kt0=0):
                g = JOB[name]
                p, n = g["acc"][0]
                pe.wait_ge(acc_read[p], acc_n2(p, n) + 1)
                for (s, n), (k0, k1, cols, *_) in zip(g["slots"], g["units"]):
                    pe.wait_ge(slot_lo[s], slot_n2(s, n) + 2)
                    vh, vl = (w[:, s, 0:(k1 - k0) * cols].rearrange("p (k n) -> p k n", k=k1 - k0)
                              for w in (whi, wlo))
                    for t in range(NT):
                        if g["after_wide"] and k0 == 0:
                            pe.wait_ge(acc_read[t], n_acc[t].at(l) + 1)
                        last = products(acc[:, p, t, 0:cols],
                                        [(kt0 + k, k - k0) for k in range(k0, k1)], kt0, kt0 + g["kts"] - 1,
                                        lh, ll, t, lambda k: vh[:, k, :], lambda k: vl[:, k, :])
                last.then_inc(acc_full[p], 1)
                n_acc[p].k += 1

            def quad2(name, lh, ll, tile1=None, ahead=None):
                g = JOB[name]
                quad(l, [(s, slot_n2(s, n), unit[2]) for (s, n), unit in zip(g["slots"], g["units"])], lh, ll,
                     g["after_wide"], tile1, ahead)

            n_norm = [0]

            def norm_T(t):
                if t == 0:
                    n_norm[0] += 1
                n = n_norm[0] - 1
                transpose_tile(l, bv, t, lambda half: pe.wait_ge(xn_ready, 4 * n + 2 * t + half + 1))

            def norm_T0():
                norm_T(0)

            def norm_T1():
                norm_T(1)

            def heads2(n_heads, q, k, v, ready, n0):
                def score(h):
                    b = h % 2
                    aux_wait(l, b)
                    nc.tensor.matmul(aux[:, b, 0:P], q(h, 0), k(h, 0, P), start=True, stop=True)
                    last = nc.tensor.matmul(aux[:, b, P:3 * P], q(h, 1), k(h, 0, S), start=True, stop=True)
                    aux_end(b, last)

                score(0)
                score(1)
                for h in range(n_heads):
                    pe.wait_ge(ready, n0 + h + 1)
                    prob_transposes(l, SE[:, h % 2, 0, :])
                    if h + 2 < n_heads:
                        score(h + 2)
                    values(l, v(h), HD)

            def feed_forward2(i):
                g = JOB[f"ff{i}"]

                def view(w):
                    v = w.rearrange("p (k n) -> p k n", k=4)
                    return lambda k: v[:, k, :]

                def side_T():
                    pe.wait_ge(side_in, 16 * (i + 1))
                    aux_wait(l, 0)
                    for f in range(2):
                        for t in range(NT):
                            last = nc.tensor.transpose(aux[:, 0, (2 * f + t) * P:(2 * f + t + 1) * P],
                                                       bq[:, t, f * P:(f + 1) * P], ident[:])
                    aux_end(0, last)

                feed_forward(l, lambda s: slot_n2(s, g["n0"][s]),
                             [(g["s0"] + j) % RING for j in range(RING)], view, 4, NF2, norm_T1, side_T)

            def ff_and_side(i):
                feed_forward2(i)
                (s, n), = JOB[f"side{i}"]["slots"]
                pe.wait_ge(slot_lo[s], slot_n2(s, n) + 2)
                aux_wait(l, 0)
                vh, vl = (w[:, s, :].rearrange("p (k n) -> p k n", k=2) for w in (whi, wlo))
                for t in range(NT):
                    acc_wait(l, t, True)
                    for half in range(2):
                        col = slice(half * NC, (half + 1) * NC)
                        last = products(acc[:, half, t, :], [(4 + k, k) for k in range(2)], 4, 5, yTh, yTl, t,
                                        lambda k: vh[:, k, col], lambda k: vl[:, k, col])
                    last.then_inc(acc_full[t], 1)
                    if t == 0:
                        norm_T0()
                for p in range(2):
                    n_acc[p].k += 1
                quad2(f"g{i}", xTh, xTl, tile1=norm_T1, ahead=norm_T0 if i == 0 else None)

            norm_T0()
            quad2("c", xTh, xTl, tile1=norm_T1)
            job("qb")
            pe.wait_ge(low_ready, 1)
            for t in range(NT):
                aux_wait(l, t)
                for k in range(3):
                    c0 = t * Q_LORA + k * P
                    last = nc.tensor.transpose(aux[:, t, k * P:(k + 1) * P], flat(mix_par)[:, c0:c0 + P],
                                               ident[:])
                aux_end(t, last)
            job("kb")
            pe.wait_ge(low_ready, 2)
            aux_wait(l, 2)
            for k in range(2):
                for t in range(NT):
                    c0 = 2 * Q_LORA + t * (KV_LORA + ROPE2) + k * P
                    last = nc.tensor.transpose(aux[:, 2, (2 * k + t) * P:(2 * k + t + 1) * P],
                                               flat(mix_par)[:, c0:c0 + P], ident[:])
            aux_end(2, last)
            job("vb")
            aux_all(l)
            job("uq0", yTh, yTl, 0)
            job("uq1", yTh, yTl, 0)
            job("ukv0", yTh, yTl, 3)
            job("ukv1", yTh, yTl, 3)
            qb, kb, vb, qbT = (bg_flat[:, k * D:(k + 1) * D] for k in range(4))
            kbT = qb
            for q, src in enumerate((qb, kb)):
                pe.wait_ge(heads_ready, q + 1)
                aux_all(l)
                transpose_heads(l, lambda t, h: src[:, t * NC + h * P:t * NC + (h + 1) * P], 4, banks=[0, 1])
            pe.wait_ge(heads_ready, 3)
            transpose_heads(l, lambda t, h: flat(bu)[:, t * 768 + h * MLA_D:t * 768 + (h + 1) * MLA_D], 8,
                            width=MLA_D)
            pe.wait_ge(heads_ready, 4)
            transpose_heads(l, lambda t, h: flat(mix_par)[:, t * 768 + h * MLA_D:t * 768 + (h + 1) * MLA_D], 8,
                            width=MLA_D)
            aux_all(l)
            heads2(MLA_H, lambda h, t: qT[0:MLA_D, h, t * P:(t + 1) * P], lambda h, k0, k1: kT[0:MLA_D, h, k0:k1],
                   lambda h: [bval[:, t, h * P + MLA_N:(h + 1) * P] for t in range(NT)], e_ready, DEPTH * H1)

            def half(t_, h, c0, c1):
                return t_[(h % 2) * HD:(h % 2 + 1) * HD, (h // 2) * S + c0:(h // 2) * S + c1]

            heads2(DIL_H, lambda h, t: half(qbT, h, t * P, (t + 1) * P), lambda h, k0, k1: half(kbT, h, k0, k1),
                   lambda h: [vb[:, t * NC + h * HD:t * NC + (h + 1) * HD] for t in range(NT)], a_ready,
                   DEPTH * H1)
            pe.wait_ge(o_ready, 1)
            for t in range(NT):
                transpose_tile(l, bu, t)
            quad2("eout", yTh, yTl, ahead=norm_T0)
            ff_and_side(0)
            quad2("z01", xTh, xTl, tile1=norm_T1)
            for k in range(2, 4):
                job(f"z{k}")
            pe.wait_ge(heads_ready, 5)
            transpose_heads(l, lambda t, h: bq[:, t, h * P:(h + 1) * P], 8)
            job("z4")
            job("z5")
            pe.wait_ge(heads_ready, 6)
            transpose_heads(l, lambda t, h: bu[:, t, h * P:(h + 1) * P], 8)
            aux_all(l)
            for name in ("z4", "z5"):
                p, n = JOB[name]["acc"][0]
                pe.wait_ge(acc_read[p], acc_n2(p, n) + 2)
            heads2(MOBA_H, lambda h, t: half(flat(bv), h, t * P, (t + 1) * P),
                   lambda h, k0, k1: half(flat(bq), h, k0, k1),
                   lambda h: [bval[:, t, h * HD:(h + 1) * HD] for t in range(NT)], e_ready,
                   DEPTH * H1 + MLA_H + DIL_H)
            pe.wait_ge(o_ready, 2)
            for t in range(NT):
                transpose_tile(l, bu, t)
            quad2("oout", yTh, yTl, ahead=norm_T0)
            ff_and_side(1)

        def places_x(tiles=range(NT)):
            for t in tiles:
                for half in range(2):
                    yield (2 * t + half, aux[:, 2 * t + half, :].rearrange("p (k c) -> p k c", k=4),
                           (slice(4 * half, 4 * half + 4), slice(t * P, (t + 1) * P)))

        def place_pair(b, k0):
            return b, aux[:, b, :].rearrange("p (k c) -> p k c", k=2), (slice(k0, k0 + 2), slice(0, S))

        def places_cq():
            for t in range(NT):
                yield t, aux[:, t, 0:3 * P].rearrange("p (k c) -> p k c", k=3), (slice(0, 3), slice(t * P, (t + 1) * P))

        @block.scalar
        def _(act):
            n_acc = [Uses(ACC_LAYER), Uses(ACC_LAYER)]
            n_aux = [Uses(k) for k in AUX_LAYER]
            n_used = Uses(USED_LAYER)

            def high(s, n, size=UNIT):
                act.wait_ge(slot_full[s], 32 * n + 32)
                nc.scalar.copy(whi[:, s, 0:size], raw[:, s, 0:size]).then_inc(slot_hi[s], 1)

            def high_T(l, places, dst):
                for b, src, (k, tok) in places:
                    act.wait_ge(aux_full[b], n_aux[b].take(l) + 1)
                    nc.scalar.copy(dst[:, k, tok], src).then_inc(t_hi, 1)

            def acc_done(l, p):
                act.wait_ge(acc_full[p], n_acc[p].take(l) + 1)

            def copy_banks(l, dst, banks=range(4), parts=P):
                for q, b in enumerate(banks):
                    act.wait_ge(aux_full[b], n_aux[b].take(l) + 1)
                    nc.scalar.copy(dst[0:parts, q * NC:(q + 1) * NC], aux[0:parts, b, :])\
                        .then_inc(aux_read[b], 1)

            def used_wait(l):
                act.wait_ge(unit_used, n_used.take(l) + 1)

            def wide_read(t, dst, func=ACT.Copy, scale=1.0):
                for half in range(2):
                    last = nc.scalar.activation(dst[:, half * NC:(half + 1) * NC], acc[:, half, t, :], func,
                                                scale=scale)
                last.then_inc(acc_read[t], 1)

            def feed_forward(l, slot0, which_slots, func, cols, t_banks, iters, tile1, before_last=None):
                aux0 = [n_aux[0].at(l), n_aux[1].at(l)]
                down_slots = which_slots[2:]
                nd = len(down_slots)
                used0 = n_used.at(l)

                def activate(i, t):
                    act.wait_ge(aux_full[t], aux0[t] + i + 1)
                    nc.scalar.activation(act_b[:, t, 0:cols], aux[:, t, 0:cols], func).then_inc(act_done, 1)

                def transposed(i):
                    for b in t_banks:
                        act.wait_ge(aux_full[b], aux0[b] + i + 1)
                        _, src, (k, tok) = place_pair(b, 2 * (b - 2))
                        nc.scalar.copy(yTh[:, k, tok], src).then_inc(t_hi, 1)

                activate(0, 0)
                tile1()
                aux0 += [n_aux[2].at(l), n_aux[3].at(l)]
                act.wait_ge(unit_used, used0 + 1)
                high(which_slots[0], slot0(which_slots[0]) + 1)
                activate(0, 1)
                high(which_slots[1], slot0(which_slots[1]) + 1)
                for s in down_slots:
                    high(s, slot0(s))
                with act.Fori(1, iters) as i:
                    activate(i, 0)
                    transposed(i - 1)
                    used = used0 + 1 + (i - 1) * (1 + nd)
                    act.wait_ge(unit_used, used + 1)
                    high(which_slots[0], slot0(which_slots[0]) + i + 1)
                    activate(i, 1)
                    high(which_slots[1], slot0(which_slots[1]) + i + 1)
                    for q, s in enumerate(down_slots):
                        act.wait_ge(unit_used, used + 2 + q)
                        high(s, slot0(s) + i)
                transposed(iters - 1)
                for b in [0, 1, *t_banks]:
                    n_aux[b].k += iters
                if before_last is not None:
                    before_last()
                n_used.k += iters + (iters - 1) * nd

            def mixer(l):
                high(3, mixer_n(l, 3))
                high_T(l, places_x([0]), xTh)
                for p in range(2):
                    acc_done(l, p)
                high(2, mixer_n(l, 2))
                high_T(l, places_x([1]), xTh)

                def split(u):
                    if u < 2 * CH + 2:
                        high(u % RING, mixer_n(l, u))

                def to_sbuf(c, dst, func):
                    p = c % 2
                    col = slice(p * NC, (p + 1) * NC)
                    nc.scalar.activation(dst[:, :, col], acc[:, p], func).then_inc(acc_read[p], 1)

                def head_exp(h):
                    act.wait_ge(s_ready, l * H1 + h + 1)
                    for m in range(2):
                        for t, c in ((0, slice(0, P)), (1, slice(P, 3 * P))):
                            last = nc.scalar.activation(SE[:, h % 2, m, c], SE[:, h % 2, m, c], ACT.Exp,
                                                        bias=rmax[:, h % 2, 2 * m + t:2 * m + t + 1],
                                                        scale=HD ** -0.5,
                                                        accum_out=rsum[:, h % 2, 2 * m + t:2 * m + t + 1])
                    last.then_inc(e_ready, 1)

                def probs_T(h):
                    act.wait_ge(aux_full[2], n_aux[2].take(l) + 1)
                    nc.scalar.copy(aT[:], aux[:, 2, 0:3 * P]).then_inc(aux_read[2], 1)

                def head_out(h):
                    act.wait_ge(aux_full[3], n_aux[3].take(l) + 1)
                    for t in range(NT):
                        last = nc.scalar.activation(bu[:, t, h * P:(h + 1) * P], aux[:, 3, t * P:(t + 1) * P],
                                                    ACT.Square, accum_out=ssq[:, t, h:h + 1])
                    last.then_inc(sq_ready, 1)

                acc_done(l, 0)
                wide_read(0, bv[:, 0, :], ACT.Gelu)
                for j in range(3):
                    used_wait(l)
                    split(4 + j)
                acc_done(l, 1)
                wide_read(1, bv[:, 1, :], ACT.Gelu)
                split(7)
                for b in range(2):
                    n_aux[b].k += 1
                for c in range(2, 10):
                    acc_done(l, c % 2)
                    split(2 * c + 4)
                    split(2 * c + 5)
                    if c < 4:
                        to_sbuf(c, bu, ACT.Gelu)
                    elif c >= 8:
                        to_sbuf(c, bval, ACT.Copy)
                    if c == 4:
                        for b in range(4):
                            n_aux[b].k += 1
                    if c == 5:
                        high_T(l, places_x(), yTh)
                    if c == 6:
                        copy_banks(l, flat(bv))
                    if c == 8:
                        copy_banks(l, flat(bq))
                act.wait_ge(lam_dot, l + 1)
                nc.scalar.activation(lam_t[:, 2:4], lam_t[:, 0:2], ACT.Exp).then_inc(lam_exp, 1)
                for m in range(2):
                    n_aux[m].k += H1
                head_exp(0)
                for h in range(H1):
                    probs_T(h)
                    ends = [u // 2 for u in HEAD_UNITS[h] if u % 2]
                    for c in ends:
                        acc_done(l, c % 2)
                        split(2 * c + 4)
                    if h + 1 < H1:
                        head_exp(h + 1)
                    for c in ends:
                        split(2 * c + 5)
                        if c < 14:
                            w, p = divmod(c - 10, 2)
                            act.wait_ge(acc_read[p], l * ACC_LAYER + 1 + c // 2 + 2)
                            g = bg[:, w, :, p * NC:(p + 1) * NC]
                            nc.scalar.activation(g, g, ACT.Tanh, scale=0.5).then_inc(tanh_done, 1)
                    head_out(h)
                high_T(l, places_x(), xTh)
                for u0, dst in ((32, yTh), (36, xTh)):
                    for j in range(2):
                        used_wait(l)
                        split(u0 + 4 + j)
                    high_T(l, places_x([0]), dst)
                    used_wait(l)
                    split(u0 + 6)
                    acc_done(l, 0)
                    acc_done(l, 1)
                    split(u0 + 7)
                    if u0 == 32:
                        high_T(l, places_x([1]), dst)

            act.wait_ge(angles, 1)
            nc.scalar.activation(ang[:, 2:4], ang[:, 2:4], ACT.Sin).then_inc(sines, 1)
            for s in range(2):
                high(s, 0)
            with act.Fori(0, DEPTH) as l:
                high_T(l, places_x([0]), xTh)
                for which in range(2):
                    feed_forward(l, lambda s: l * SLOT_LAYER[s] + (NF + CH // 2) * which, [0, 1, 2],
                                 ACT.Silu, FB, [2], NF, lambda: high_T(l, places_x([1]), xTh))
                    if which == 0:
                        mixer(l)
                for p in range(2):
                    acc_done(l, p)
                for c in n_aux + n_acc + [n_used]:
                    c.layer_ends()
            if stop == 1:
                return

            l = L2
            n_norm = [0]

            def split_after(name):
                g = JOB[name]
                for u in units_after(g):
                    high_unit(u)

            def high_unit(u):
                g = job_of_unit(u)
                if g["units"] is None:
                    s = (g["s0"] + u - g["u0"]) % RING
                    high(s, slot_n2(s, g["n0"][s]))
                else:
                    s, n = g["slots"][u - g["u0"]]
                    k0, k1, cols = g["units"][u - g["u0"]][:3]
                    high(s, slot_n2(s, n), (k1 - k0) * cols)

            def acc_full2(name, t):
                act.wait_ge(acc_full[t], acc_n2(*JOB[name]["acc"][t]) + 1)

            def split_unit(name, j):
                g = JOB[name]
                if j < 3:
                    act.wait_ge(unit_used, used_n2(g["used"]) + j + 1)
                else:
                    acc_full2(name, 1)
                u = g["u0"] + RING + j
                if u < N_UNITS and not in_ff(u):
                    high_unit(u)

            def done(name):
                p, n = JOB[name]["acc"][0]
                act.wait_ge(acc_full[p], acc_n2(p, n) + 1)
                split_after(name)

            def to_sbuf(name, dst, func=ACT.Copy, scale=1.0):
                g = JOB[name]
                p = g["acc"][0][0]
                nc.scalar.activation(dst, acc[:, p, :, 0:g["cols"]], func, scale=scale).then_inc(acc_read[p], 1)

            def squares(t):
                if t == 0:
                    n_norm[0] += 1
                n = n_norm[0] - 1
                act.wait_ge(x_ready, X_LAST - 4 + 2 * (t + 1) if n == 0 else X_LAST + 2 * (n - 1) + t + 1)
                nc.scalar.activation(bv[:, t, :], x[:, t, :], ACT.Square, scale=D ** -0.5,
                                     accum_out=ssq[:, t, 0:1])\
                    .then_inc(sumsq, 1)

            def heads2(n_heads, n0):
                def exps(h):
                    act.wait_ge(s_ready, n0 + h + 1)
                    b = h % 2
                    for t, c in ((0, slice(0, P)), (1, slice(P, 3 * P))):
                        last = nc.scalar.activation(SE[:, b, 0, c], SE[:, b, 0, c], ACT.Exp,
                                                    bias=rmax[:, b, t:t + 1], accum_out=rsum[:, b, t:t + 1])
                    last.then_inc(e_ready, 1)

                exps(0)
                for h in range(n_heads):
                    if h + 1 < n_heads:
                        exps(h + 1)
                    act.wait_ge(aux_full[2], n_aux[2].take(l) + 1)
                    if h > 0:
                        act.wait_ge(aux_full[3], n_aux[3].at(l) + h)
                    nc.scalar.copy(aT[:], aux[:, 2, 0:3 * P]).then_inc(aux_read[2], 1)
                for b in range(2):
                    n_aux[b].k += n_heads // 2
                n_aux[3].k += n_heads

            def ff_and_side(i):
                g = JOB[f"ff{i}"]
                end = g["u0"] + g["nu"]
                n_used.k = g["used"]
                feed_forward(l, lambda s: slot_n2(s, g["n0"][s]), [(g["s0"] + j) % RING for j in range(RING)],
                             ACT.Relu, NC, [2, 3], NF2, lambda: high_T(l, places_x([1]), xTh),
                             lambda: high_T(l, [place_pair(0, 4)], yTh))
                squares(0)
                act.wait_ge(unit_used, used_n2(g["used"]) + 3 * NF2 - 1)
                high_unit(end + 2)
                squares(1)
                acc_full2(f"side{i}", 0)
                wide_read(0, bg[:, 1, 0, :])
                high_T(l, places_x([0]), xTh)
                high_unit(end + 3)
                acc_full2(f"side{i}", 1)
                wide_read(1, bg[:, 1, 1, :])
                high_unit(end + 4)
                high_T(l, places_x([1]), xTh)
                name = f"g{i}"
                acc_full2(name, 0)
                wide_read(0, bg[:, 0, 0, :], ACT.Tanh, 0.5)
                if i == 0:
                    squares(0)
                    for j in range(2):
                        split_unit(name, j)
                    high_T(l, places_x([0]), xTh)
                    split_unit(name, 2)
                    split_unit(name, 3)
                acc_full2(name, 1)
                wide_read(1, bg[:, 0, 1, :], ACT.Tanh, 0.5)
                if i == 0:
                    squares(1)
                    high_T(l, places_x([1]), xTh)

            def out_norm(name):
                high_T(l, places_x(), yTh)
                squares(0)
                for j in range(2):
                    split_unit(name, j)
                high_T(l, places_x([0]), xTh)
                squares(1)

            squares(0)
            squares(1)
            for u in (2, 3):
                high_unit(u)
            high_T(l, places_x(), xTh)
            mixf = flat(mix_par)
            for t in range(NT):
                acc_full2("c", t)
                nc.scalar.activation(aT[:], acc[:, 0, t, 0:Q_LORA], ACT.Square, accum_out=ssq[:, t, 1:2])
                act.drain()
                nc.scalar.activation(aT[:, 0:KV_LORA], acc[:, 1, t, 0:KV_LORA], ACT.Square,
                                     accum_out=ssq[:, t, 2:3])
                act.drain()
                nc.scalar.copy(mixf[:, t * Q_LORA:(t + 1) * Q_LORA], acc[:, 0, t, 0:Q_LORA])
                w = KV_LORA + ROPE2
                c0 = NT * Q_LORA + t * w
                nc.scalar.copy(mixf[:, c0:c0 + w], acc[:, 1, t, 0:w])
                act.drain().then_inc(acc_read[t], 1)
                if t == 0:
                    for j in range(3):
                        split_unit("c", j)
            split_unit("c", 3)
            done("qb")
            to_sbuf("qb", bg_flat[:, 0:D].rearrange("p (t c) -> p t c", t=NT))
            high_T(l, places_cq(), yTh)
            done("kb")
            to_sbuf("kb", bg_flat[:, D:2 * D].rearrange("p (t c) -> p t c", t=NT))
            high_T(l, [place_pair(2, 3)], yTh)
            done("vb")
            to_sbuf("vb", bg_flat[:, 2 * D:3 * D].rearrange("p (t c) -> p t c", t=NT))
            qa = flat(bu)[:, 0:NT * MLA_H * MLA_D].rearrange("p (t c) -> p t c", t=NT)
            for k in range(2):
                done(f"uq{k}")
                to_sbuf(f"uq{k}", qa[:, :, k * 384:(k + 1) * 384])
            for k in range(2):
                done(f"ukv{k}")
                to_sbuf(f"ukv{k}", bval[:, :, k * NC:(k + 1) * NC])
            copy_banks(l, bg_flat[:, 3 * D:4 * D], banks=[0, 1])
            copy_banks(l, bg_flat[:, 0:D], banks=[0, 1])
            copy_banks(l, flat(bv), parts=MLA_D)
            copy_banks(l, flat(bq), parts=MLA_D)
            heads2(MLA_H, DEPTH * H1)
            heads2(DIL_H, DEPTH * H1 + MLA_H)
            out_norm("eout")
            ff_and_side(0)
            acc_full2("z01", 0)
            wide_read(0, bq[:, 0, :])
            for j in range(3):
                split_unit("z01", j)
            acc_full2("z01", 1)
            wide_read(1, bq[:, 1, :])
            split_unit("z01", 3)
            for k in range(2, 6):
                done(f"z{k}")
                dst = (bq, bu, bval)[k // 2]
                to_sbuf(f"z{k}", dst[:, :, (k % 2) * NC:(k % 2 + 1) * NC])
                if k == 3:
                    copy_banks(l, flat(bv))
            copy_banks(l, flat(bq))
            heads2(MOBA_H, DEPTH * H1 + MLA_H + DIL_H)
            out_norm("oout")
            ff_and_side(1)

        @block.vector
        def _(dve):
            n_acc = [Uses(ACC_LAYER), Uses(ACC_LAYER)]
            n_aux = [Uses(k) for k in AUX_LAYER]
            n_hi = Uses(2 * NF + 6 * 4)
            V = nc.vector

            def low(s, n, size=UNIT):
                dve.wait_ge(slot_hi[s], n + 1)
                V.tensor_tensor(wlo[:, s, 0:size], raw[:, s, 0:size], cast(whi[:, s, 0:size]), ALU.subtract)\
                    .then_inc(slot_lo[s], 1)

            def low_T(l, places, dst_l, dst_h):
                for b, src, (k, tok) in places:
                    dve.wait_ge(t_hi, n_hi.take(l) + 1)
                    V.tensor_tensor(dst_l[:, k, tok], src, cast(dst_h[:, k, tok]), ALU.subtract)\
                        .then_inc(aux_read[b], 1)
                    n_aux[b].k += 1

            def mean_and_var(src, t):
                for half in range(2):
                    V.bn_stats(stat[:, t, half, :], src[:, t, half * NC:(half + 1) * NC])
                dve.drain()
                V.bn_aggr(mv[:, t, :], stat[:, t, :, :].rearrange("p a b -> p (a b)")).then_inc(var_ready, 1)
                dve.drain()

            def scale_shift(l, n, src, t, col, par, ready):
                halves = [slice(half * NC, (half + 1) * NC) for half in range(2)]
                for c in halves:
                    V.scalar_tensor_tensor(src[:, t, c], src[:, t, c], mv[:, t, 0:1], par[:, 0, c],
                                           ALU.subtract, ALU.mult)
                dve.drain()
                dve.wait_ge(rstd_ready, RSTD_LAYER * l + n + t + 1)
                for c in halves:
                    last = V.scalar_tensor_tensor(src[:, t, c], src[:, t, c], nx[:, col + t:col + t + 1],
                                                  par[:, 1, c], ALU.mult, ALU.add)
                    if ready is x_ready or c is halves[1]:
                        last.then_inc(ready, 1)

            def acc_wait(l, p):
                dve.wait_ge(acc_full[p], n_acc[p].take(l) + 1)

            def add_tile(l, t):
                acc_wait(l, t)
                for half in range(2):
                    c = slice(half * NC, (half + 1) * NC)
                    last = V.scalar_tensor_tensor(x[:, t, c], x[:, t, c], 2 * ALPHA, acc[:, half, t, :],
                                                  ALU.mult, ALU.add)
                last.then_inc(acc_read[t], 1)

            def norm_tile(l, k, t):
                dve.drain()
                mean_and_var(x, t)
                dve.wait_ge(ln_in, 32 * (3 * l + k) + 32)
                scale_shift(l, RSTD_NORM[k], x, t, 0, ln_par, x_ready)
                if t == NT - 1:
                    dve.drain().then_inc(ln_free, 1)

            def feed_forward(l, slot0, which_slots, act0, other, cols, t_banks, iters, tile1, before_last=None):
                down_slots = which_slots[2:]
                aux0 = []

                def multiply(i, t):
                    dve.wait_ge(act_done, act0 + 2 * i + t + 1)
                    V.tensor_tensor(gate_b[:, t, 0:cols], act_b[:, t, 0:cols], other(t), ALU.mult)\
                        .then_inc(aux_read[t], 1)

                def transposed(i):
                    for q, b in enumerate(t_banks):
                        dve.wait_ge(t_hi, h0 + len(t_banks) * i + q + 1)
                        _, src, (k, tok) = place_pair(b, 2 * (b - 2))
                        V.tensor_tensor(yTl[:, k, tok], src, cast(yTh[:, k, tok]), ALU.subtract)\
                            .then_inc(aux_read[b], 1)

                multiply(0, 0)
                tile1()
                h0 = n_hi.at(l)
                aux0 = [n_aux[b].at(l) for b in range(4)]
                low(which_slots[0], slot0(which_slots[0]) + 1)
                multiply(0, 1)
                low(which_slots[1], slot0(which_slots[1]) + 1)
                for s in down_slots:
                    low(s, slot0(s))
                with dve.Fori(1, iters) as i:
                    for b in t_banks:
                        dve.wait_ge(aux_full[b], aux0[b] + i)
                    multiply(i, 0)
                    transposed(i - 1)
                    low(which_slots[0], slot0(which_slots[0]) + i + 1)
                    multiply(i, 1)
                    low(which_slots[1], slot0(which_slots[1]) + i + 1)
                    for s in down_slots:
                        low(s, slot0(s) + i)
                transposed(iters - 1)
                for b in [0, 1, *t_banks]:
                    n_aux[b].k += iters
                n_hi.k += len(t_banks) * iters
                if before_last is not None:
                    before_last()

            def rotate(l, c, dst):
                p = c % 2
                dve.drain()
                acc_wait(l, p)
                src = acc[:, p].rearrange("p t (h d) -> p t h d", d=HD)
                out_ = dst[:, :, p * NC:(p + 1) * NC].rearrange("p t (h d) -> p t h d", d=HD)
                tmp = bg_flat[:, D:2 * D].rearrange("p (t h d) -> p t h d", t=NT, d=HD)
                half = HD // 2

                def table(k, c0, c1):
                    return rope[:, k, :, c0:c1].unsqueeze(2).to_broadcast([P, NT, NC // HD, c1 - c0])

                V.tensor_tensor(out_, src, table(0, 0, HD), ALU.mult)
                V.tensor_tensor(tmp[:, :, :, 0:half], src[:, :, :, half:HD], table(1, 0, half), ALU.mult)
                dve.drain()
                V.tensor_tensor(tmp[:, :, :, half:HD], src[:, :, :, 0:half], table(1, half, HD), ALU.mult)\
                    .then_inc(acc_read[p], 1)
                dve.drain()
                V.tensor_tensor(out_, out_, tmp, ALU.add).then_inc(roped, 1)

            def mixer(l):
                low(3, mixer_n(l, 3))
                add_tile(l, 0)
                norm_tile(l, 0, 0)
                add_tile(l, 1)
                low_T(l, places_x([0]), xTl, xTh)
                low(2, mixer_n(l, 2))
                norm_tile(l, 0, 1)
                low_T(l, places_x([1]), xTl, xTh)

                def split(u):
                    if u < 2 * CH + 2:
                        low(u % RING, mixer_n(l, u))

                def head_scores(h):
                    for m in range(2):
                        dve.wait_ge(aux_full[m], n_aux[m].take(l) + 1)
                        V.tensor_tensor(SE[:, h % 2, m, :], aux[:, m, 0:3 * P], causal[:], ALU.add)\
                            .then_inc(aux_read[m], 1)
                    dve.drain()
                    rm = rmax[:, h % 2, :].rearrange("p (m t) -> p m t", m=2)
                    V.tensor_reduce(rm[:, :, 0], SE[:, h % 2, :, 0:P], AX_X, ALU.max)
                    V.tensor_reduce(rm[:, :, 1], SE[:, h % 2, :, P:3 * P], AX_X, ALU.max)
                    dve.drain()
                    V.tensor_scalar(rmax[:, h % 2, :], rmax[:, h % 2, :], -(HD ** -0.5), None, ALU.mult)\
                        .then_inc(s_ready, 1)

                def head_probs(h):
                    dve.wait_ge(e_ready, l * H1 + h + 1)
                    r = rinv[:, h % 2, :]
                    V.reciprocal(r, rsum[:, h % 2, :])
                    dve.drain()
                    V.tensor_scalar(r[:, 2:4], r[:, 2:4], neg_lam[:], None, ALU.mult)
                    for t, c in ((0, slice(0, P)), (1, slice(P, 3 * P))):
                        V.tensor_scalar(pa[:, c], SE[:, h % 2, 0, c], r[:, t:t + 1], None, ALU.mult)
                    dve.drain()
                    for t, c in ((0, slice(0, P)), (1, slice(P, 3 * P))):
                        last = V.scalar_tensor_tensor(pa[:, c], SE[:, h % 2, 1, c], r[:, 2 + t:3 + t], pa[:, c],
                                                      ALU.mult, ALU.add)
                        if t == 0:
                            dve.drain()
                    last.then_inc(a_ready, 1)

                for j in range(3):
                    split(4 + j)
                for b in range(2):
                    dve.wait_ge(aux_full[b], n_aux[b].take(l) + 1)
                    V.tensor_tensor(wT[:, 4 * b:4 * b + 4, :], aux[:, b, :].rearrange("p (g t) -> p g t", g=4),
                                    tri[:].unsqueeze(1).to_broadcast([P, 4, P]), ALU.mult)\
                        .then_inc(aux_read[b], 1)
                split(7)
                for t in range(NT):
                    dve.wait_ge(acc_read[t], n_acc[t].take(l) + 2)
                    mean_and_var(bv, t)
                    dve.wait_ge(mix_in, 64 * l + 32)
                    scale_shift(l, RSTD_V, bv, t, NT, mix_par, vn_ready)
                dve.drain().then_inc(mix_free, 1)
                for c in range(2, 10):
                    split(2 * c + 4)
                    split(2 * c + 5)
                    if 4 <= c < 8:
                        rotate(l, c, bq if c < 6 else bk)
                    else:
                        n_acc[c % 2].k += 1
                    if c == 4:
                        for p in range(2):
                            dve.wait_ge(acc_read[p], l * ACC_LAYER + 1 + 2 + 1)
                        for b in range(4):
                            dve.wait_ge(aux_full[b], n_aux[b].take(l) + 1)
                            for k in range(2):
                                g = 2 * b + k
                                u = bu[:, :, g * P:(g + 1) * P]
                                last = V.scalar_tensor_tensor(
                                    u, aux[:, b, k * S:(k + 1) * S].rearrange("p (t c) -> p t c", t=NT),
                                    sgu_bT[:, g:g + 1], u, ALU.add, ALU.mult)
                            last.then_inc(aux_read[b], 1)
                    if c == 5:
                        low_T(l, places_x(), yTl, yTh)
                    if c in (6, 8):
                        for b in range(4):
                            n_aux[b].k += 1
                lw = lam_w.rearrange("p (a b d) -> p a b d", a=2, b=2)
                V.tensor_tensor(pa[:, 0:2 * HD].rearrange("p (a d) -> p a d", a=2), lw[:, :, 0], lw[:, :, 1],
                                ALU.mult)
                dve.drain()
                V.tensor_reduce(lam_t[:, 0:2], pa[:, 0:2 * HD].rearrange("p (a d) -> p a d", a=2), AX_X, ALU.add)\
                    .then_inc(lam_dot, 1)
                dve.wait_ge(lam_exp, l + 1)
                V.tensor_tensor(lam_t[:, 0:1], lam_t[:, 3:4], lam_t[:, 2:3], ALU.subtract)
                dve.drain()
                V.tensor_tensor(neg_lam[:], lam_t[:, 0:1], lam_init[:, 0:1], ALU.subtract)
                dve.drain()
                V.tensor_scalar(diff_g[:], diff_g[:], lam_init[:, 1:2], (2.0 * HD) ** 0.5, ALU.mult, ALU.mult)

                def normalise(h):
                    dve.wait_ge(aux_full[3], n_aux[3].take(l) + 1)
                    dve.wait_ge(rstd_ready, RSTD_LAYER * l + RSTD_HEADS + h + 1)
                    for t in range(NT):
                        last = V.scalar_tensor_tensor(bu[:, t, h * P:(h + 1) * P], aux[:, 3, t * P:(t + 1) * P],
                                                      ny[:, NT * h + t:NT * h + t + 1], diff_g[:],
                                                      ALU.mult, ALU.mult)
                    last.then_inc(aux_read[3], 1)

                head_scores(0)
                head_probs(0)
                for h in range(H1):
                    if h > 0:
                        normalise(h - 1)
                    ends = [u // 2 for u in HEAD_UNITS[h] if u % 2]
                    if h + 1 < H1:
                        head_scores(h + 1)
                    for c in ends:
                        split(2 * c + 4)
                    if h + 1 < H1:
                        head_probs(h + 1)
                    for c in ends:
                        split(2 * c + 5)
                        w, p = divmod(c - 10, 2)
                        acc_wait(l, p)
                        g = bg[:, w % 2, :, p * NC:(p + 1) * NC]
                        if c < 14:
                            if c == 10:
                                dve.wait_ge(mix_in, 64 * l + 64)
                            V.tensor_tensor(g, acc[:, p], mix_par[:, w, p * NC:(p + 1) * NC].unsqueeze(1)
                                            .to_broadcast([P, NT, NC]), ALU.add).then_inc(acc_read[p], 1)
                            if c == 13:
                                dve.drain().then_inc(mix_free, 1)
                        else:
                            dve.wait_ge(tanh_done, 4 * l + 4)
                            V.scalar_tensor_tensor(g, g, 1.0, acc[:, p], ALU.add, ALU.mult)\
                                .then_inc(acc_read[p], 1)
                n_aux[2].k += H1
                normalise(H1 - 1)
                low_T(l, places_x(), xTl, xTh)
                for t in range(NT):
                    acc_wait(l, t)
                    for half in range(2):
                        g1 = bg[:, 1, t, half * NC:(half + 1) * NC]
                        last = V.scalar_tensor_tensor(g1, g1, 1.0, acc[:, half, t, :], ALU.add, ALU.mult)
                    last.then_inc(acc_read[t], 1)
                    dve.drain()
                    g0 = bg[:, 0, t, :]
                    V.tensor_tensor(g0, g0, bg[:, 1, t, :], ALU.add).then_inc(m_ready, 1)
                    if t == 0:
                        split(36)
                        split(37)
                        low_T(l, places_x([0]), yTl, yTh)
                        split(38)
                dve.drain().then_inc(small_free, 1)
                split(39)
                low_T(l, places_x([1]), yTl, yTh)
                add_tile(l, 0)
                norm_tile(l, 1, 0)
                split(40)
                split(41)
                low_T(l, places_x([0]), xTl, xTh)
                add_tile(l, 1)
                norm_tile(l, 1, 1)

            for s in [*slot_lo, *acc_read, *aux_read, ln_free, mix_free]:
                dve.sem_inc(s, 1)
            dve.wait_ge(x_in, 16)
            dve.sem_inc(x_ready, 4)
            dve.wait_ge(const_in, 8 * 16)
            pos_f = lam_t[:, 0:NT]
            V.tensor_copy(pos_f, pos_i[:])
            dve.drain()
            for t in range(NT):
                V.tensor_scalar(ang[:, 0, t, :], inv_freq, pos_f[:, t:t + 1], None, ALU.mult)
            dve.drain()
            big = 12582912.0
            parts = two_pi_parts()
            for k, turn, shift in ((2, 0.0, 0.0), (3, 0.25, PI / 2)):
                V.tensor_scalar(ang[:, 1], ang[:, 0], 1.0 / (2 * PI), turn, ALU.mult, ALU.add)
                dve.drain()
                V.tensor_scalar(ang[:, 1], ang[:, 1], big, None, ALU.add)
                dve.drain()
                V.tensor_scalar(ang[:, 1], ang[:, 1], big, None, ALU.subtract)
                dve.drain()
                src = ang[:, 0]
                for c in parts:
                    V.scalar_tensor_tensor(ang[:, k], ang[:, 1], -c, src, ALU.mult, ALU.add)
                    dve.drain()
                    src = ang[:, k]
                V.tensor_scalar(ang[:, k], ang[:, k], shift, None, ALU.add)
                dve.drain()
                V.tensor_scalar(ang[:, k], ang[:, k], PI32, -PI32, ALU.min, ALU.max)
                dve.drain()
            dve.drain().then_inc(angles, 1)
            dve.wait_ge(sines, 1)
            hr = ROPE2 // 2
            V.tensor_copy(rope2[:, 0, :, 0:hr], ang[:, 3])
            V.tensor_copy(rope2[:, 0, :, hr:ROPE2], ang[:, 3])
            V.tensor_scalar(rope2[:, 1, :, 0:hr], ang[:, 2], -1.0, None, ALU.mult)
            V.tensor_copy(rope2[:, 1, :, hr:ROPE2], ang[:, 2])
            dve.drain().then_inc(small_free, 1)

            for s in range(2):
                low(s, 0)
            with dve.Fori(0, DEPTH) as l:
                low_T(l, places_x([0]), xTl, xTh)
                for which in range(2):
                    feed_forward(l, lambda s: l * SLOT_LAYER[s] + (NF + CH // 2) * which, [0, 1, 2],
                                 (2 * l + which) * NT * NF, lambda t: aux[:, t, FB:2 * FB], FB, [2], NF,
                                 lambda: low_T(l, places_x([1]), xTl, xTh))
                    if which == 0:
                        mixer(l)
                for t in range(NT):
                    add_tile(l, t)
                    norm_tile(l, 2, t)
                for c in n_aux + n_acc + [n_hi]:
                    c.layer_ends()
            if stop == 1:
                return

            l = L2
            n_norm = [0]
            n_root = [RSTD_LAYER * DEPTH]

            def low_unit(u):
                g = job_of_unit(u)
                if g["units"] is None:
                    s = (g["s0"] + u - g["u0"]) % RING
                    low(s, slot_n2(s, g["n0"][s]))
                else:
                    s, n = g["slots"][u - g["u0"]]
                    k0, k1, cols = g["units"][u - g["u0"]][:3]
                    low(s, slot_n2(s, n), (k1 - k0) * cols)

            def split_after(name):
                for u in units_after(JOB[name]):
                    low_unit(u)

            def split_unit(name, j):
                u = JOB[name]["u0"] + RING + j
                if u < N_UNITS and not in_ff(u):
                    low_unit(u)

            def in_sbuf(name, t=0):
                p, n = JOB[name]["acc"][t]
                dve.wait_ge(acc_read[p], acc_n2(p, n) + 2)

            def add_x(name, t):
                dve.wait_ge(acc_full[t], acc_n2(*JOB[name]["acc"][t]) + 1)
                for half in range(2):
                    c = slice(half * NC, (half + 1) * NC)
                    last = V.tensor_tensor(x[:, t, c], x[:, t, c], acc[:, half, t, :], ALU.add)
                last.then_inc(acc_read[t], 1)
                dve.drain().then_inc(x_ready, 1)

            def norm_x(t):
                if t == 0:
                    n_norm[0] += 1
                n = n_norm[0] - 1
                dve.wait_ge(sumsq, 2 * n + t + 1)
                n_root[0] += 1
                dve.wait_ge(rstd_ready, n_root[0])
                dve.wait_ge(ln_in, 96 * DEPTH + 32 * (n + 1))
                for half in range(2):
                    c = slice(half * NC, (half + 1) * NC)
                    V.scalar_tensor_tensor(bv[:, t, c], x[:, t, c], nx[:, t:t + 1], ln_par[:, 0, c],
                                           ALU.mult, ALU.mult).then_inc(xn_ready, 1)
                if t == NT - 1:
                    dve.drain().then_inc(ln_free, 1)

            def group_norm(src, dst, gain, n, tmp, scale=1.0, signal=None):
                groups = src.shape[1]
                V.tensor_tensor(tmp, src, src, ALU.mult)
                dve.drain()
                V.tensor_reduce(nv[:, 0:groups], tmp, AX_X, ALU.add).then_inc(var_ready, 1)
                dve.drain()
                n_root[0] += 1
                dve.wait_ge(rstd_ready, n_root[0])
                V.tensor_scalar(ny[:, 0:groups], ny[:, 0:groups], scale * n ** 0.5, None, ALU.mult)
                dve.drain()
                V.tensor_tensor(tmp, src, ny[:, 0:groups].unsqueeze(2).to_broadcast([P, groups, n]), ALU.mult)
                dve.drain()
                last = V.tensor_tensor(dst, tmp, gain.unsqueeze(1).to_broadcast([P, groups, n]), ALU.mult)
                if signal is not None:
                    last.then_inc(signal, 1)
                else:
                    dve.drain()

            def rotate2(v, tmp, heads, signal=None):
                hr = ROPE2 // 2
                a_, b_ = tmp
                for t in range(NT):
                    g = slice(t * heads, (t + 1) * heads)

                    def table(k, c0, c1):
                        return rope2[:, k, t, c0:c1].unsqueeze(1).to_broadcast([P, heads, c1 - c0])

                    V.tensor_tensor(a_[:, g], v[:, g], table(0, 0, ROPE2), ALU.mult)
                    V.tensor_tensor(b_[:, g, 0:hr], v[:, g, hr:ROPE2], table(1, 0, hr), ALU.mult)
                    V.tensor_tensor(b_[:, g, hr:ROPE2], v[:, g, 0:hr], table(1, hr, ROPE2), ALU.mult)
                dve.drain()
                last = V.tensor_tensor(v, a_, b_, ALU.add)
                if signal is not None:
                    last.then_inc(signal, 1)
                else:
                    dve.drain()

            n_s = [DEPTH * H1]

            def heads2(n_heads, score, width0, count=None):
                n0 = n_s[0]
                n_s[0] += n_heads

                def scores(h):
                    b = h % 2
                    dve.wait_ge(aux_full[b], n_aux[b].take(l) + 1)
                    score(SE[:, b, 0, :], aux[:, b, 0:3 * P], h).then_inc(aux_read[b], 1)
                    dve.drain()
                    V.tensor_reduce(rmax[:, b, 0:1], SE[:, b, 0, 0:P], AX_X, ALU.max, negate=True)
                    V.tensor_reduce(rmax[:, b, 1:2], SE[:, b, 0, P:3 * P], AX_X, ALU.max, negate=True)\
                        .then_inc(s_ready, 1)

                scores(0)
                scores(1)
                for h in range(n_heads):
                    b = h % 2
                    dve.wait_ge(e_ready, n0 + h + 1)
                    if count is not None:
                        for t, c in ((0, slice(0, P)), (1, slice(P, 3 * P))):
                            last = V.scalar_tensor_tensor(SE[:, b, 0, c], SE[:, b, 0, c], 1.0, count[:, c],
                                                          ALU.mult, ALU.mult, accum_out=rsum[:, b, t:t + 1])
                        last.then_inc(a_ready, 1)
                        dve.drain()
                    V.reciprocal(rinv[:, b, 0:2], rsum[:, b, 0:2])
                    if h + 2 < n_heads:
                        scores(h + 2)
                    dve.wait_ge(aux_full[3], n_aux[3].take(l) + 1)
                    dve.drain()
                    for t in range(NT):
                        last = V.tensor_scalar(bu[:, t, width0 + h * HD:width0 + (h + 1) * HD],
                                               aux[:, 3, t * HD:(t + 1) * HD], rinv[:, b, t:t + 1], None, ALU.mult)
                    last.then_inc(aux_read[3], 1)
                n_aux[2].k += n_heads

            def ff_and_side(i):
                g = JOB[f"ff{i}"]
                end = g["u0"] + g["nu"]
                feed_forward(l, lambda s: slot_n2(s, g["n0"][s]), [(g["s0"] + j) % RING for j in range(RING)],
                             2 * DEPTH * NT * NF + i * NT * NF2, lambda t: aux[:, t, :], NC, [2, 3], NF2,
                             lambda: low_T(l, places_x([1]), xTl, xTh),
                             lambda: low_T(l, [place_pair(0, 4)], yTl, yTh))
                add_x(f"ff{i}", 0)
                norm_x(0)
                add_x(f"ff{i}", 1)
                low_unit(end + 2)
                low_T(l, places_x([0]), xTl, xTh)
                norm_x(1)
                low_unit(end + 3)
                low_unit(end + 4)
                low_T(l, places_x([1]), xTl, xTh)
                name = f"g{i}"
                for t in range(NT):
                    in_sbuf(name, t)
                    gate = bg[:, 0, t, :]
                    V.scalar_tensor_tensor(gate, gate, 1.0, bg[:, 1, t, :], ALU.add, ALU.mult)
                    dve.drain()
                    V.scalar_tensor_tensor(x[:, t, :], gate, 0.5, x[:, t, :], ALU.mult, ALU.add)\
                        .then_inc(x_ready, 1)
                    if i == 0:
                        norm_x(t)
                        if t == 0:
                            split_unit(name, 0)
                            split_unit(name, 1)
                        low_T(l, places_x([t]), xTl, xTh)
                        if t == 0:
                            split_unit(name, 2)
                            split_unit(name, 3)

            def out_norm(name):
                low_T(l, places_x(), yTl, yTh)
                add_x(name, 0)
                norm_x(0)
                for j in range(2):
                    split_unit(name, j)
                low_T(l, places_x([0]), xTl, xTh)
                add_x(name, 1)
                norm_x(1)

            norm_x(0)
            norm_x(1)
            for u in (2, 3):
                low_unit(u)
            low_T(l, places_x(), xTl, xTh)
            mixf, bkf = flat(mix_par), flat(bk)
            gain, c0 = {}, 0
            for name, w in EVEN_GAINS:
                gain[name] = ln_par[:, 1, c0:c0 + w]
                c0 += w

            def tmp(groups, n, at=0):
                return bkf[:, at:at + groups * n].rearrange("p (g c) -> p g c", c=n)

            for j in range(3):
                split_unit("c", j)
            for t in range(NT):
                in_sbuf("c", t)
            dve.wait_ge(gains_in, 16 * len(EVEN_GAINS))
            V.tensor_scalar(nv[:, 0:NT], ssq[:, :, 1], 1.0 / Q_LORA, None, ALU.mult)
            V.tensor_scalar(nv[:, NT:2 * NT], ssq[:, :, 2], 1.0 / KV_LORA, None, ALU.mult).then_inc(var_ready, 1)
            n_root[0] += 1
            dve.wait_ge(rstd_ready, n_root[0])
            for t in range(NT):
                v = mixf[:, t * Q_LORA:(t + 1) * Q_LORA]
                last = V.scalar_tensor_tensor(v, v, ny[:, t:t + 1], gain["e_cq_norm_2"], ALU.mult, ALU.mult)
            last.then_inc(low_ready, 1)
            split_unit("c", 3)
            kv = mixf[:, NT * Q_LORA:NT * (Q_LORA + KV_LORA + ROPE2)].rearrange("p (t c) -> p t c", t=NT)
            for t in range(NT):
                v = kv[:, t, 0:KV_LORA]
                last = V.scalar_tensor_tensor(v, v, ny[:, NT + t:NT + t + 1], gain["e_ckv_norm_2"], ALU.mult, ALU.mult)
            last.then_inc(low_ready, 1)
            group_norm(kv[:, :, KV_LORA:], k_rope[:, :, :], gain["e_kn_rope_2"], ROPE2, tmp(NT, ROPE2))
            rotate2(k_rope[:, :, :], (tmp(NT, ROPE2), tmp(NT, ROPE2, 1024)), 1)
            split_after("qb")
            in_sbuf("qb")
            v = bg_flat[:, 0:D].rearrange("p (g c) -> p g c", c=HD)
            group_norm(v, v, gain["e_dil_qn_2"], HD, tmp(16, HD), scale=HD ** -0.5, signal=heads_ready)
            low_T(l, places_cq(), yTl, yTh)
            split_after("kb")
            in_sbuf("kb")
            dve.drain()
            v = bg_flat[:, D:2 * D].rearrange("p (g c) -> p g c", c=HD)
            group_norm(v, v, gain["e_dil_kn_2"], HD, tmp(16, HD), signal=heads_ready)
            low_T(l, [place_pair(2, 3)], yTl, yTh)
            split_after("vb")
            for k in range(2):
                split_after(f"uq{k}")
            in_sbuf("uq0")
            in_sbuf("uq1")
            dve.drain()
            qa = flat(bu)[:, 0:16 * MLA_D].rearrange("p (g c) -> p g c", c=MLA_D)
            group_norm(qa[:, :, 0:MLA_N], qa[:, :, 0:MLA_N], gain["e_qn_nope_2"], MLA_N, tmp(16, MLA_N))
            group_norm(qa[:, :, MLA_N:], qa[:, :, MLA_N:], gain["e_qn_rope_2"], ROPE2, tmp(16, ROPE2))
            rotate2(qa[:, :, MLA_N:], (tmp(16, ROPE2), tmp(16, ROPE2, 1024)), MLA_H, signal=heads_ready)
            for k in range(2):
                split_after(f"ukv{k}")
            in_sbuf("ukv0")
            in_sbuf("ukv1")
            dve.drain()
            kva = flat(bval).rearrange("p (g c) -> p g c", c=P)
            ka = mixf[:, 0:16 * MLA_D].rearrange("p (g c) -> p g c", c=MLA_D)
            group_norm(kva[:, :, 0:MLA_N], ka[:, :, 0:MLA_N], gain["e_kn_nope_2"], MLA_N, tmp(16, MLA_N))
            for t in range(NT):
                last = V.tensor_copy(ka[:, t * MLA_H:(t + 1) * MLA_H, MLA_N:],
                                     k_rope[:, t:t + 1, :].to_broadcast([P, MLA_H, ROPE2]))
            last.then_inc(heads_ready, 1)
            for b, k in ((0, 4), (1, 4), (2, 2), (3, 2)):
                n_aux[b].k += k
            heads2(MLA_H, lambda o, s, h: V.scalar_tensor_tensor(o, s, MLA_D ** -0.5, causal[:], ALU.mult, ALU.add), 0)
            heads2(DIL_H, lambda o, s, h: V.scalar_tensor_tensor(o, dist[:, 1, :], slope(h, DIL_H), s, ALU.mult,
                                                                 ALU.add), MLA_H * MLA_V, times)
            dve.drain().then_inc(o_ready, 1)
            out_norm("eout")
            ff_and_side(0)
            og = [ln_par[:, 1, k * HD:(k + 1) * HD] for k in range(2)]
            for k in range(1, 6):
                if k == 1:
                    for j in range(RING):
                        split_unit("z01", j)
                else:
                    split_after(f"z{k}")
                if k in (1, 3):
                    if k == 1:
                        for t in range(NT):
                            in_sbuf("z01", t)
                    else:
                        in_sbuf("z2")
                        in_sbuf("z3")
                    if k == 1:
                        dve.wait_ge(gains_in, 16 * (len(EVEN_GAINS) + len(ODD_GAINS)))
                    v = flat(bq if k == 1 else bu).rearrange("p (g c) -> p g c", c=HD)
                    dve.drain()
                    group_norm(v, v, og[k // 2], HD, tmp(32, HD), scale=HD ** -0.5 if k == 1 else 1.0,
                               signal=heads_ready)
            for b in range(4):
                n_aux[b].k += 2
            heads2(MOBA_H, lambda o, s, h: V.scalar_tensor_tensor(o, dist[:, 0, :], slope(h, MOBA_H), s, ALU.mult,
                                                                  ALU.add), 0)
            dve.drain().then_inc(o_ready, 1)
            out_norm("oout")
            ff_and_side(1)


PI32 = float(np.float32(3.1415925))


def two_pi_parts():
    parts, rest = [], 2 * np.pi
    for _ in range(2):
        _, e = np.frexp(rest)
        step = 2.0 ** (e - 11)
        c = float(np.floor(rest / step) * step)
        parts.append(c)
        rest -= c
    return parts + [float(np.float32(rest))]


def constants():
    r = np.arange(P)
    q, k = r[:, None], r[None, :]
    tri = (q <= k).astype(np.float32)
    d = np.concatenate([q - k, q + P - k, q - k], axis=1)
    causal = np.where(d >= 0, 0.0, NEG).astype(np.float32)
    times = ((d >= 0) & (d <= 128)).astype(np.float32)
    for dil in (4, 16):
        times += ((d >= 0) & (d % dil == 0)).astype(np.float32)
    dist = np.stack([np.where(d >= 0, -d, NEG), np.where(times > 0, -d, NEG)], axis=1).astype(np.float32)
    pos = np.arange(S, dtype=np.float32)
    inv = (np.float32(10000.0) ** (-np.arange(0, HD, 2, dtype=np.float32) / np.float32(HD))).astype(np.float32)
    ang = (pos[:, None] * inv[None, :]).astype(np.float32).astype(np.float64)
    cos, sin = np.cos(ang), np.sin(ang)
    rope = np.stack([np.concatenate([cos, cos], 1), np.concatenate([-sin, sin], 1)])
    rope = rope.reshape(2, NT, P, HD).transpose(2, 0, 1, 3).astype(np.float32)
    lam = 0.8 - 0.6 * np.exp(-0.3 * np.arange(DEPTH))
    half = ROPE2 // 2
    inv2 = (np.float32(10000.0) ** (-np.arange(half, dtype=np.float32) / np.float32(half))).astype(np.float32)
    return {
        "c_ident": np.eye(P, dtype=np.float32),
        "c_tri": tri,
        "c_causal": causal,
        "c_rope": np.ascontiguousarray(rope),
        "c_lam": np.stack([lam, 1.0 - lam], axis=1).astype(np.float32),
        "c_dist": np.ascontiguousarray(dist),
        "c_times": times,
        "c_inv_freq": np.broadcast_to(inv2, (P, half)).copy(),
    }


SHAPES = {
    "w_in": (DEPTH * D, -1), "gate_b": (DEPTH * 2, D), "sgu_w": (DEPTH * 8, P, P), "sgu_b": (DEPTH * 8, P),
    "lam": (DEPTH, 4 * HD), "w_branch": (DEPTH * 2 * D, D), "w_out": (DEPTH * D, D),
    "ffn_w1": (DEPTH * 2 * D, F1), "ffn_w3": (DEPTH * 2 * D, F1), "ffn_w2": (DEPTH * 2 * F1, D),
    "ln_g": (DEPTH * 3, D), "ln_b": (DEPTH * 3, D),
    "p_2": (DEPTH * S, 256), "e_w_in_2": (D, -1), "e_w_uq_2": (Q_LORA, -1), "e_w_ukv_2": (KV_LORA, -1),
    "e_w_out_2": (D, D), "o_w_in_2": (D, -1), "o_w_out_2": (D, D), "w_ff1_2": (DEPTH * D, F2),
    "w_ff2_2": (DEPTH * F2, D), "w_ple_gate_2": (DEPTH * D, D), "w_ple_proj_2": (DEPTH * 256, D),
}


def kernel(**inputs):
    from concourse.bacc import Bacc
    from concourse.bass_utils import run_bass_kernel_spmd

    nc = Bacc("TRN2", target_bir_lowering=False, num_devices=1, dynamic_dma_scratch_size=4096)
    arrays, args = {}, {}
    for name, value in {**inputs, **constants()}.items():
        v = np.ascontiguousarray(value)
        if name in SHAPES:
            v = v.reshape(SHAPES[name])
        arrays[name] = v
        args[name] = nc.dram_tensor(name, v.shape, mybir.dt.from_np(v.dtype), kind="ExternalInput").ap()
    out = nc.dram_tensor("out", (1, S, D), F32, kind="ExternalOutput").ap()
    build(nc, args, out)
    return run_bass_kernel_spmd(nc, [arrays], core_ids=[0]).results[0]["out"]
```

```python
from contextlib import ExitStack

import numpy as np

import concourse.bass as bass
from concourse import mybir

F32 = mybir.dt.float32
F32R = mybir.dt.float32r
I32 = mybir.dt.int32
ALU = mybir.AluOpType
ACT = mybir.ActivationFunctionType
AX_X = mybir.AxisListType.X

P = 128
S = 256
NT = S // P
D = 1024
KT = D // P
DEPTH = 2
RING = 4
UNIT = 2048
NC = 512
NEG = -1.0e30

F1 = 2816
FB = 256
NF = F1 // FB
H1 = 8
HD = 64
ALPHA = (2.0 * DEPTH) ** 0.25
LN_EPS = 1e-5
CH = 20
IN_COLS = [1024, 1536, 0, 512, 2048, 2560, 3072, 3584, 4096, 4608, 5120, 5632, 6144, 6656]
HEAD_UNITS = [[20, 21], [22, 23], [24, 25], [26, 27], [28], [29], [30], [31]]

ACC_LAYER = 2 + CH // 2
USED_LAYER = 2 * (NF + NF - 1) + 3 * 3
FFN_USES = (NF, NF, NF - 1, 1)
SLOT_LAYER = tuple(2 * n + CH // 2 for n in FFN_USES)
AUX_LAYER = tuple((2 * NF if b < 3 else 0) + 6 + 2 + 1 + (1 if b < 2 else 0) + H1 for b in range(4))

EPS = 1e-6
F2 = 4096
FB2 = 512
NF2 = F2 // FB2
Q_LORA, KV_LORA, ROPE2 = 384, 256, 32
MLA_H, MLA_N, MLA_V = 8, 64, 64
MLA_D = MLA_N + ROPE2
DIL_H = 8
MOBA_H = 16
EVEN_GAINS = [("e_cq_norm_2", Q_LORA), ("e_ckv_norm_2", KV_LORA), ("e_qn_nope_2", MLA_N),
              ("e_qn_rope_2", ROPE2), ("e_kn_nope_2", MLA_N), ("e_kn_rope_2", ROPE2),
              ("e_dil_qn_2", HD), ("e_dil_kn_2", HD)]
ODD_GAINS = [("o_qn_2", HD), ("o_kn_2", HD)]
PI = float(np.pi)
RSQRT_MAGIC = float(0x5F3759DF)


def jobs_of_block2():
    jobs = []

    def chunk(name, w, row0, col0, cols, kts, split):
        units = [(k0, k1, cols, w, row0 + k0 * P, col0) for k0, k1 in split]
        jobs.append(dict(name=name, units=units, wide=False, cols=cols, kts=kts))

    def quad(name, w, row0, cols):
        c0 = (0, cols[0])
        units = [(k0, k0 + 4, cols[h], w, row0 + k0 * P, c0[h]) for h in range(2) for k0 in (0, 4)]
        jobs.append(dict(name=name, units=units, wide=True, cols=cols))

    full = [(0, 4), (4, 8)]
    quad("c", "e_w_in_2", 0, (Q_LORA, KV_LORA + ROPE2))
    for k, name in enumerate(("qb", "kb", "vb")):
        chunk(name, "e_w_in_2", 0, Q_LORA + KV_LORA + ROPE2 + k * NC, NC, KT, full)
    for k in range(2):
        chunk(f"uq{k}", "e_w_uq_2", 0, k * 384, 384, 3, [(0, 3)])
    for k in range(2):
        chunk(f"ukv{k}", "e_w_ukv_2", 0, k * NC, NC, 2, [(0, 2)])
    quad("eout", "e_w_out_2", 0, (NC, NC))

    def ff_and_side(i):
        jobs.append(dict(name=f"ff{i}", units=None, wide=True, i=i))
        jobs.append(dict(name=f"side{i}", units=[(0, 2, D, "w_ple_proj_2", i * 256, 0)], wide=True))
        quad(f"g{i}", "w_ple_gate_2", i * D, (NC, NC))

    ff_and_side(0)
    quad("z01", "o_w_in_2", 0, (NC, NC))
    for k in range(2, 6):
        chunk(f"z{k}", "o_w_in_2", 0, k * NC, NC, KT, full)
    quad("oout", "o_w_out_2", 0, (NC, NC))
    ff_and_side(1)
    u, acc, par, slots, used = 0, [0, 0], 0, [0] * RING, 0
    after_wide = True
    for g in jobs:
        g["u0"], g["used"], g["after_wide"] = u, used, after_wide
        after_wide = g["wide"]
        used += 2 * (NF2 - 1) + NF2 + 1 if g["units"] is None else len(g["units"]) - 1 if g["wide"] else 0
        g["slots"] = []
        if g["units"] is None:
            s0 = u % RING
            g["s0"], g["n0"] = s0, list(slots)
            for s in range(RING):
                slots[s] += NF2
            g["nu"] = NF2 * RING
            u += RING * NF2
        else:
            for _ in g["units"]:
                g["slots"].append((u % RING, slots[u % RING]))
                slots[u % RING] += 1
                u += 1
            g["nu"] = len(g["units"])
        if g["wide"]:
            g["acc"] = [(0, acc[0]), (1, acc[1])]
            acc = [acc[0] + 1, acc[1] + 1]
        else:
            g["acc"] = [(par, acc[par])]
            acc[par] += 1
            par = 1 - par
    return jobs


JOBS = jobs_of_block2()
JOB = {g["name"]: g for g in JOBS}


def job_of_unit(u):
    return next(g for g in JOBS if g["u0"] <= u < g["u0"] + g["nu"])


N_UNITS = JOBS[-1]["u0"] + JOBS[-1]["nu"]


def units_after(g):
    end = g["u0"] + g["nu"]
    return [u for u in range(g["u0"] + RING, min(end + RING, N_UNITS)) if not in_ff(u)]


def in_ff(u):
    g = job_of_unit(u)
    return g["units"] is None and u - g["u0"] >= 2


class Uses:

    def __init__(self, per):
        self.per = per
        self.k = 0

    def at(self, layer):
        return layer * self.per + self.k

    def take(self, layer):
        n = self.at(layer)
        self.k += 1
        return n

    def layer_ends(self):
        assert self.k == self.per, (self.k, self.per)
        self.k = 0


def rows(ap, row0, n, col0, nc):
    r = ap[row0:row0 + n, :] if isinstance(row0, int) else ap[bass.ds(row0, n), :]
    r = r[:, col0:col0 + nc] if isinstance(col0, int) else r[:, bass.ds(col0, nc)]
    return r.rearrange("(k p) n -> p k n", p=P)


def slope(h, n):
    return float(np.float32(2.0) ** np.float32(-8.0 * (h + 1) / n))


def build(nc, a, out):
    ctx = ExitStack()
    with ctx:
        def sb(name, shape, dt=F32):
            return ctx.enter_context(nc.sbuf_tensor(name, shape, dt))

        def sem(name):
            return ctx.enter_context(nc.semaphore(name))

        raw = sb("w_raw", [P, RING, UNIT])
        whi = sb("w_high", [P, RING, UNIT], F32R)
        wlo = sb("w_low", [P, RING, UNIT], F32R)
        x = sb("x_res", [P, NT, D])
        xTh = sb("xT_high", [P, KT, S], F32R)
        xTl = sb("xT_low", [P, KT, S], F32R)
        yTh = sb("yT_high", [P, KT, S], F32R)
        yTl = sb("yT_low", [P, KT, S], F32R)
        bv = sb("buf_v", [P, NT, D])
        bu = sb("buf_u", [P, NT, D])
        bq = sb("buf_q", [P, NT, D])
        bk = sb("buf_k", [P, NT, D])
        bval = sb("buf_val", [P, NT, D])
        bg = sb("buf_gates", [P, 2, NT, D])
        ln_par = sb("ln_param", [P, 2, D])
        mix_par = sb("mix_param", [P, 2, D])
        ident = sb("ident", [P, P])
        tri = sb("tri", [P, P])
        causal = sb("causal", [P, 3 * P])
        rope = sb("rope_tab", [P, 2, NT, HD])
        lam_init = sb("lam_init", [P, 2])
        diff_g = sb("diff_g", [P, 2 * HD])
        sgu_bT = sb("sgu_bT", [P, 8])
        aT = sb("probs_T", [P, 3 * P])[:]
        stat = sb("stat", [P, NT, 2, 6])
        mv = sb("mean_var", [P, NT, 2])
        nv = sb("group_var", [P, 48])
        ny = sb("inverse_root", [P, 48])
        nz = sb("newton_t", [P, 48])
        EPS1 = (4 * LN_EPS, LN_EPS, 2.0 * HD * LN_EPS)
        eps_tile = sb("epsilons", [P, 2 * len(EPS1)])
        minus_half = sb("minus_half", [P, 32])
        nx = sb("inverse_root_x", [P, 2 * NT])
        lam_t = sb("lam_t", [P, 4])
        neg_lam = sb("neg_lam", [P, 1])
        rmax = sb("row_max", [P, 2, 4])
        rsum = sb("row_sum", [P, 2, 4])
        rinv = sb("row_inv", [P, 2, 4])
        ssq = sb("sum_sq", [P, NT, H1])
        dist = sb("neg_distance", [P, 2, 3 * P])
        times = sb("pattern_count", [P, 3 * P])
        pos_i = sb("pos_i", [P, NT], I32)
        rope2 = sb("rope2", [P, 2, NT, ROPE2])
        k_rope = rope[:, 0, :, 0:ROPE2]

        def flat(t):
            return t[:, :, :].rearrange("p t d -> p (t d)")

        bg_flat = bg[:, :, :, :].rearrange("p a t d -> p (a t d)")
        ang = flat(bval)[:, 0:P].rearrange("p (k t c) -> p k t c", k=4, t=NT)
        inv_freq = flat(bval)[:, P:P + ROPE2 // 2]
        turns = flat(bval)[:, 2 * P:2 * P + NT * ROPE2].rearrange("p (k t c) -> p k t c", k=2, t=NT)
        lam_w = bg_flat[:, 2 * D:2 * D + 4 * HD]
        act_b = flat(bk)[:, 0:NT * NC].rearrange("p (t f) -> p t f", t=NT)
        gate_b = flat(bk)[:, NT * NC:2 * NT * NC].rearrange("p (t f) -> p t f", t=NT)
        sgu_raw = bval[:, 0, :].rearrange("p (g r) -> p g r", g=8)
        wT = bg_flat[:, 0:D].rearrange("p (g r) -> p g r", g=8)
        qT = flat(bv).rearrange("p (h s) -> p h s", s=S)
        kT = flat(bq).rearrange("p (h s) -> p h s", s=S)
        SE = flat(bk)[:, 0:4 * 3 * P].rearrange("p (b m c) -> p b m c", b=2, m=2)
        pa = flat(bk)[:, 4 * 3 * P:5 * 3 * P]

        acc = ctx.enter_context(nc.psum_tensor("acc", [P, 2, NT, NC], F32))
        aux = ctx.enter_context(nc.psum_tensor("aux", [P, 4, NC], F32))

        slot_full = [sem(f"slot_full{s}") for s in range(RING)]
        slot_hi = [sem(f"slot_hi{s}") for s in range(RING)]
        slot_lo = [sem(f"slot_lo{s}") for s in range(RING)]
        acc_full = [sem("acc_full0"), sem("acc_full1")]
        acc_read = [sem("acc_read0"), sem("acc_read1")]
        aux_full = [sem(f"aux_full{b}") for b in range(4)]
        aux_read = [sem(f"aux_read{b}") for b in range(4)]
        unit_used = sem("unit_used")
        var_ready = sem("var_ready")
        rstd_ready = sem("rstd_ready")
        t_hi = sem("t_hi")
        act_done = sem("act_done")
        x_ready = sem("x_ready")
        tanh_done = sem("tanh_done")
        vn_ready = sem("vn_ready")
        roped = sem("roped")
        s_ready = sem("s_ready")
        e_ready = sem("e_ready")
        a_ready = sem("a_ready")
        m_ready = sem("m_ready")
        lam_dot = sem("lam_dot")
        lam_exp = sem("lam_exp")
        const_in = sem("const_in")
        ident_in = sem("ident_in")
        angle_in = sem("angle_in")
        gain0_in = sem("gain0_in")
        x_in = sem("x_in")
        ln_in = sem("ln_in")
        ln_free = sem("ln_free")
        mix_in = sem("mix_in")
        mix_free = sem("mix_free")
        small_in = sem("small_in")
        small_free = sem("small_free")
        gains_in = sem("gains_in")
        side_in = sem("side_in")
        sq_ready = sem("sq_ready")
        sumsq = sem("sumsq")
        xn_ready = sem("xn_ready")
        low_ready = sem("low_ready")
        heads_ready = sem("heads_ready")
        angles = sem("angles")
        sines = sem("sines")
        score_full = sem("score_full")
        o_full = sem("o_full")
        o_read = sem("o_read")
        out_done = sem("out_done")

        block = ctx.enter_context(nc.Block())
        L2 = DEPTH

        def cast(ap):
            return ap.bitcast(F32)

        def slot_n2(s, n):
            return L2 * SLOT_LAYER[s] + n

        def acc_n2(p, n):
            return L2 * ACC_LAYER + n

        def used_n2(n):
            return L2 * USED_LAYER + n

        def o_pair(g):
            return acc[:, g % 2, 1, 0:S]

        def score_bank(h):
            return (aux[:, 0, :], aux[:, 1, :], acc[:, 0, 0, :])[h % 3][:, 0:3 * P]

        def row(stat_, h, t):
            return stat_[:, :, :].rearrange("p a b -> p (a b)")[:, 2 * (h % 3) + t:2 * (h % 3) + t + 1]

        def probs(h):
            return flat(bk)[:, (h % 3) * 3 * P:(h % 3 + 1) * 3 * P]

        def probs_T(h):
            return flat(bk)[:, (3 + h % 2) * 3 * P:(4 + h % 2) * 3 * P]

        RSTD_V, RSTD_HEADS, RSTD_NORM = 2, 4, (0, 4 + H1, 6 + H1)
        RSTD_LAYER = 8 + H1
        X_LAYER = 12
        X_LAST = 4 + X_LAYER * DEPTH

        def mixer_n(l, u):
            s = u % RING
            return l * SLOT_LAYER[s] + FFN_USES[s] + u // RING

        def ffn_n(l, which, s):
            return l * SLOT_LAYER[s] + (FFN_USES[s] + CH // 2) * which

        @block.sync
        def _(sp):
            sp.dma_start(ident[:], a["c_ident"]).then_inc(ident_in, 16)
            sp.dma_start(x[:], a["x"].rearrange("b (t p) d -> p (b t) d", p=P)).then_inc(x_in, 16)

            def load(s, n, parts):
                sp.wait_ge(slot_lo[s], n + 1)
                for dst, src in parts:
                    sp.dma_start(dst, src).then_inc(slot_full[s], 32 // len(parts))

            def hidden1(l, which, i):
                for j in range(2):
                    dst = raw[:, j, :].rearrange("p (m k n) -> p m k n", m=2, k=4)
                    r0 = (l * 2 + which) * D + j * 4 * P
                    load(j, ffn_n(l, which, j) + i,
                         [(dst[:, 0], rows(a["ffn_w1"], r0, 4 * P, i * FB, FB)),
                          (dst[:, 1], rows(a["ffn_w3"], r0, 4 * P, i * FB, FB))])

            def down1(l, which, i, s, n):
                dst = raw[:, s, :].rearrange("p (k n) -> p k n", k=2)
                load(s, ffn_n(l, which, s) + n,
                     [(dst, rows(a["ffn_w2"], (l * 2 + which) * F1 + i * FB, FB, 0, D))])

            def ffn1(l, which):
                hidden1(l, which, 0)
                down1(l, which, NF - 1, 3, 0)
                with sp.Fori(0, NF - 1) as i:
                    hidden1(l, which, i + 1)
                    down1(l, which, i, 2, i)

            def mixer_unit(l, u):
                c, j = divmod(u, 2)
                if u in (4, 5, 36, 37):
                    w = a["w_in" if c == 2 else "w_out"]
                    src = tuple(rows(w, l * D + (4 * j + k) * P, 2 * P, 0, NC) for k in (2, 0))
                elif c < 14:
                    src = rows(a["w_in"], l * D + j * 4 * P, 4 * P, IN_COLS[c], NC)
                elif c < 18:
                    src = rows(a["w_branch"], (l * 2 + (c - 14) // 2) * D + j * 4 * P, 4 * P,
                               (c % 2) * NC, NC)
                else:
                    src = rows(a["w_out"], l * D + j * 4 * P, 4 * P, (c % 2) * NC, NC)
                dst = raw[:, u % RING, :].rearrange("p (k n) -> p k n", k=4)
                if isinstance(src, tuple):
                    parts = [(dst[:, 2:4], src[0]), (dst[:, 0:2], src[1])]
                else:
                    parts = [(dst, src)]
                load(u % RING, mixer_n(l, u), parts)

            with sp.Fori(0, DEPTH) as l:
                ffn1(l, 0)
                for u in range(2 * CH):
                    mixer_unit(l, u)
                ffn1(l, 1)

            def load_unit(u):
                if u >= N_UNITS:
                    return
                g = job_of_unit(u)
                if g["units"] is None:
                    ff_unit(g, u - g["u0"], 0)
                else:
                    s, n = g["slots"][u - g["u0"]]
                    k0, k1, cols, w, r0, c0 = g["units"][u - g["u0"]]
                    dst = raw[:, s, 0:(k1 - k0) * cols].rearrange("p (k n) -> p k n", k=k1 - k0)
                    load(s, slot_n2(s, n), [(dst, rows(a[w], r0, (k1 - k0) * P, c0, cols))])

            def ff_unit(g, j, i):
                s = (g["s0"] + j) % RING
                dst = raw[:, s, :].rearrange("p (k n) -> p k n", k=4 if j < 2 else 2)
                if j < 2:
                    src = rows(a["w_ff1_2"], g["i"] * D + j * 4 * P, 4 * P, i * FB2, FB2)
                else:
                    src = rows(a["w_ff2_2"], g["i"] * F2 + i * FB2 + (j - 2) * 2 * P, 2 * P, 0, D)
                load(s, slot_n2(s, g["n0"][s]) + i, [(dst, src)])

            sp.wait_ge(mix_free, 2 * DEPTH + 1)
            sp.dma_start(mix_par[:, 0, :], a["mix_norm_2"][0:1, :].partition_broadcast(P)).then_inc(gain0_in, 16)
            u = 0
            while u < N_UNITS:
                g = job_of_unit(u)
                if g["units"] is None and u == g["u0"] + 2:
                    with sp.Fori(0, NF2 - 1) as i:
                        ff_unit(g, 0, i + 1)
                        ff_unit(g, 1, i + 1)
                        ff_unit(g, 2, i)
                        ff_unit(g, 3, i)
                    end = g["u0"] + g["nu"]
                    load_unit(end)
                    load_unit(end + 1)
                    ff_unit(g, 2, NF2 - 1)
                    ff_unit(g, 3, NF2 - 1)
                    u = end + 2
                else:
                    load_unit(u)
                    u += 1
            for t in range(NT):
                sp.wait_ge(x_ready, X_LAST + 10 + t + 1)
                sp.dma_start(out.rearrange("b (t p) d -> p (b t) d", p=P)[:, t, :], x[:, t, :])\
                    .then_inc(out_done, 16)
            sp.wait_ge(out_done, 16 * NT)

        @block.gpsimd
        def _(pool):
            pool.dma_start(inv_freq, a["c_inv_freq"]).then_inc(angle_in, 16)
            with nc.allow_non_contiguous_dma(reason="256 positions onto partitions"):
                pool.dma_start(pos_i[:], a["positions_2"].rearrange("b (t p) -> p (b t)", p=P))\
                    .then_inc(angle_in, 16)
            consts = ((tri[:], a["c_tri"]), (causal[:], a["c_causal"]), (rope[:], a["c_rope"]),
                      (dist[:], a["c_dist"]), (times[:], a["c_times"]))
            for dst, src in consts:
                pool.dma_start(dst, src).then_inc(const_in, 16)

            def norm_params(l, k):
                n = l * 3 + k
                pool.wait_ge(ln_free, n + 1)
                for w, name in enumerate(("ln_g", "ln_b")):
                    pool.dma_start(ln_par[:, w, :], a[name][bass.ds(n, 1), :].partition_broadcast(P))\
                        .then_inc(ln_in, 16)

            nc.gpsimd.memset(minus_half[:], -0.5)
            for k, eps in enumerate(EPS1):
                nc.gpsimd.memset(eps_tile[:, 2 * k:2 * k + 2], eps)
            pool.drain()

            def inverse_root(dst, src, eps):
                if eps in EPS1:
                    k = EPS1.index(eps)
                    nc.gpsimd.tensor_tensor(dst, src, eps_tile[:, 2 * k:2 * k + dst.shape[1]], ALU.add)
                else:
                    nc.gpsimd.tensor_scalar(dst, src, eps, None, ALU.add)
                pool.drain()
                nc.gpsimd.tensor_tensor(dst, dst, minus_half[:, 0:dst.shape[1]], ALU.pow).then_inc(rstd_ready, 1)

            def tile_roots(l, n, col, eps):
                for t in range(NT):
                    pool.wait_ge(var_ready, 8 * l + 2 * n + t + 1)
                    inverse_root(nx[:, col + t:col + t + 1], mv[:, t, 1:2], eps)

            with pool.Fori(0, DEPTH) as l:
                norm_params(l, 0)
                pool.wait_ge(small_free, l + 1)
                pool.dma_start(sgu_raw, a["sgu_w"][bass.ds(l * 8, 8), :, :].rearrange("g t r -> t g r"))\
                    .then_inc(small_in, 16)
                with nc.allow_non_contiguous_dma(reason="1024 biases onto partitions"):
                    pool.dma_start(sgu_bT[:], a["sgu_b"][bass.ds(l * 8, 8), :].rearrange("g t -> t g"))\
                        .then_inc(small_in, 16)
                pool.dma_start(diff_g[:], a["diff_ln_g"][bass.ds(l, 1), :].partition_broadcast(P))\
                    .then_inc(small_in, 16)
                pool.dma_start(lam_w, a["lam"][bass.ds(l, 1), :].partition_broadcast(P))\
                    .then_inc(small_in, 16)
                pool.dma_start(lam_init[:], a["c_lam"][bass.ds(l, 1), :].partition_broadcast(P))\
                    .then_inc(small_in, 16)
                pool.wait_ge(mix_free, 2 * l + 1)
                for w, name in enumerate(("sgu_ln_g", "sgu_ln_b")):
                    pool.dma_start(mix_par[:, w, :], a[name][bass.ds(l, 1), :].partition_broadcast(P))\
                        .then_inc(mix_in, 16)
                tile_roots(l, 0, 0, 4 * LN_EPS)
                norm_params(l, 1)
                tile_roots(l, 1, NT, LN_EPS)
                pool.wait_ge(mix_free, 2 * l + 2)
                for w in range(2):
                    pool.dma_start(mix_par[:, w, :], a["gate_b"][bass.ds(l * 2 + w, 1), :].partition_broadcast(P))\
                        .then_inc(mix_in, 16)
                for h in range(H1):
                    pool.wait_ge(sq_ready, H1 * l + h + 1)
                    inverse_root(ny[:, NT * h:NT * h + NT], ssq[:, :, h], 2.0 * HD * LN_EPS)
                tile_roots(l, 2, 0, 4 * LN_EPS)
                norm_params(l, 2)
                tile_roots(l, 3, 0, 4 * LN_EPS)
            pool.wait_ge(ln_free, 3 * DEPTH + 1)
            n = 0
            for i in range(2):
                for name, n_rms in (("mix_norm_2", 0), ("ff_norm_2", 1), ("ple_norm_2", 2)):
                    pool.wait_ge(ln_free, 3 * DEPTH + 1 + n)
                    if n > 0:
                        pool.dma_start(ln_par[:, 0, :], a[name][i:i + 1, :].partition_broadcast(P))\
                            .then_inc(ln_in, 32)
                    for t in range(NT):
                        pool.wait_ge(sumsq, 2 * n + t + 1)
                        inverse_root(nx[:, t:t + 1], ssq[:, t, 0:1], EPS)
                    if n_rms == 0:
                        c0 = 0
                        gains = EVEN_GAINS if i == 0 else ODD_GAINS
                        for gname, w in gains:
                            pool.dma_start(ln_par[:, 1, c0:c0 + w], a[gname].partition_broadcast(P))\
                                .then_inc(gains_in, 16)
                            c0 += w
                    if n_rms == 0 and i == 0:
                        pool.wait_ge(var_ready, 8 * DEPTH + 1)
                        inverse_root(ny[:, 0:2 * NT], nv[:, 0:2 * NT], EPS)
                    n += 1
                    if n_rms == 1:
                        pool.wait_ge(ln_free, 3 * DEPTH + 1 + n)
                        pool.dma_start(bq[:, :, 0:256],
                                       a["p_2"][i * S:(i + 1) * S, :].rearrange("(t p) n -> p t n", p=P))\
                            .then_inc(side_in, 16)

        @block.tensor
        def _(pe):
            n_acc = [Uses(ACC_LAYER), Uses(ACC_LAYER)]
            n_aux = [Uses(k) for k in AUX_LAYER]

            pe.wait_ge(ident_in, 16)

            def aux_wait(l, b):
                pe.wait_ge(aux_read[b], n_aux[b].at(l) + 1)

            def aux_all(l, banks=range(4)):
                for b in banks:
                    aux_wait(l, b)

            def aux_end(b, last):
                last.then_inc(aux_full[b], 1)
                n_aux[b].k += 1

            def products(dst, tiles, k_first, k_last, lh, ll, t, rh, rl):
                tok = slice(t * P, (t + 1) * P)
                for kt, j in tiles:
                    for q, (lhs, rhs) in enumerate(((lh, rh), (lh, rl), (ll, rh))):
                        last = nc.tensor.matmul(dst, lhs[:, kt, tok], rhs(j),
                                                start=(kt == k_first and q == 0),
                                                stop=(kt == k_last and q == 2))
                return last

            def transpose_tile(l, src, t, ready=None):
                for half in range(2):
                    b = 2 * t + half
                    if ready is not None:
                        ready(half)
                    aux_wait(l, b)
                    for k in range(4):
                        kt = half * 4 + k
                        last = nc.tensor.transpose(aux[:, b, k * P:(k + 1) * P],
                                                   src[:, t, kt * P:(kt + 1) * P], ident[:])
                    aux_end(b, last)

            def acc_wait(l, t, after_wide):
                if after_wide:
                    pe.wait_ge(acc_read[t], n_acc[t].at(l) + 1)
                elif t == 0:
                    for p in range(2):
                        pe.wait_ge(acc_read[p], n_acc[p].at(l) + 1)

            def quad(l, units, lh, ll, after_wide, tile1=None, ahead=None):
                for t in range(NT):
                    acc_wait(l, t, after_wide)
                    for j, (s, n, cols) in enumerate(units):
                        if t == 0 and j == 3 and tile1 is not None:
                            tile1()
                        if t == 1 and j == 3 and ahead is not None:
                            ahead()
                        if t == 0:
                            pe.wait_ge(slot_lo[s], n + 2)
                        if j < 2:
                            aux_wait(l, 2 * t + j)
                        half, k0 = j // 2, 4 * (j % 2)
                        vh, vl = (w[:, s, 0:4 * cols].rearrange("p (k n) -> p k n", k=4) for w in (whi, wlo))
                        last = products(acc[:, half, t, 0:cols], [(k0 + k, k) for k in range(4)], 0, KT - 1,
                                        lh, ll, t, lambda k: vh[:, k, :], lambda k: vl[:, k, :])
                        if j == 3:
                            last.then_inc(acc_full[t], 1)
                        elif t == 1:
                            last.then_inc(unit_used, 1)
                for p in range(2):
                    n_acc[p].k += 1

            def feed_forward(l, slot0, which_slots, hid_view, n_f, iters, tile1, before_last=None,
                             last_slot=None):
                aux0 = [n_aux[0].at(l), n_aux[1].at(l)]
                t_banks = [2] if n_f == 2 else [2, 3]
                down_slots = which_slots[2:]

                def hidden(i, t):
                    pe.wait_ge(aux_read[t], aux0[t] + i + 1)
                    for j in range(2):
                        s = which_slots[j]
                        if t == 0:
                            pe.wait_ge(slot_lo[s], slot0(s) + i + 2)
                        if isinstance(i, int) and i == 0:
                            aux_wait(l, 2 * t + j)
                        vh, vl = hid_view(whi[:, s, :]), hid_view(wlo[:, s, :])
                        dst = aux[:, t, :]
                        if n_f == 2:
                            dst = dst.rearrange("p (m n) -> p m n", m=2)
                        last = products(dst, [(4 * j + k, k) for k in range(4)], 0, KT - 1, xTh, xTl, t, vh, vl)
                        if j == 1:
                            last.then_inc(aux_full[t], 1)
                        elif t == 1:
                            last.then_inc(unit_used, 1)

                def transposes(i):
                    for t in range(NT):
                        pe.wait_ge(aux_read[t], aux0[t] + i + 2)
                    for b in t_banks:
                        pe.wait_ge(aux_read[b], aux0[b] + i + 1)
                        for f in range(2):
                            for t in range(NT):
                                f0 = ((b - 2) * 2 + f) * P
                                last = nc.tensor.transpose(aux[:, b, (2 * f + t) * P:(2 * f + t + 1) * P],
                                                           gate_b[:, t, f0:f0 + P], ident[:])
                        last.then_inc(aux_full[b], 1)

                def down_part(i, q, t, first, final):
                    s, n = down_slots[q], i
                    if final and last_slot is not None:
                        s, n = last_slot, 0
                    if t == 0:
                        pe.wait_ge(slot_lo[s], slot0(s) + n + 2)
                        pe.wait_ge(aux_read[2 + q], aux0[2 + q] + i + 2)
                    vh, vl = (w[:, s, :].rearrange("p (k n) -> p k n", k=2) for w in (whi, wlo))
                    k0 = 2 * q + (n_f if final else 0)
                    for half in range(2):
                        col = slice(half * NC, (half + 1) * NC)
                        last = products(acc[:, half, t, :], [(k0 + k, k) for k in range(2)],
                                        0 if first else -1, 2 * n_f - 1 if final else -1, yTh, yTl, t,
                                        lambda k: vh[:, k, col], lambda k: vl[:, k, col])
                    return last

                def down(i, first=False, midway=None):
                    for q in range(len(down_slots)):
                        for t in range(NT):
                            if 2 * q + t == len(down_slots) and midway is not None:
                                midway()
                            last = down_part(i, q, t, first, False)
                        last.then_inc(unit_used, 1)

                def last_down(i):
                    for t in range(NT):
                        for q in range(len(down_slots)):
                            last = down_part(i, q, t, False, True)
                            if q == len(down_slots) - 1:
                                last.then_inc(acc_full[t], 1)
                            elif t == 1:
                                last.then_inc(unit_used, 1)

                hidden(0, 0)
                tile1()
                aux0 += [n_aux[2].at(l), n_aux[3].at(l)]
                hidden(0, 1)
                hidden(1, 0)
                transposes(0)
                hidden(1, 1)
                for p in range(2):
                    pe.wait_ge(acc_read[p], n_acc[p].at(l) + 1)
                down(0, first=True)
                with pe.Fori(2, iters - 1) as i:
                    hidden(i, 0)
                    transposes(i - 1)
                    hidden(i, 1)
                    down(i - 1)
                i = iters - 1
                hidden(i, 0)
                transposes(i - 1)
                hidden(i, 1)
                down(i - 1, midway=lambda: transposes(i))
                for b in [0, 1, *t_banks]:
                    n_aux[b].k += iters
                if before_last is not None:
                    before_last()
                last_down(iters - 1)
                for p in range(2):
                    n_acc[p].k += 1

            def ffn1(l, which):
                def view(w):
                    v = w.rearrange("p (m k n) -> p m k n", m=2, k=4)
                    return lambda k: v[:, :, k, :]

                feed_forward(l, lambda s: ffn_n(l, which, s), [0, 1, 2], view, 2, NF,
                             lambda: x_T(l, 2 * which, 1), last_slot=3)

            def x_T(l, k, t):
                transpose_tile(l, x, t, lambda half: pe.wait_ge(x_ready, X_LAYER * l + 4 * k + 2 * t + half + 1))

            def mixer_quad(l, u0, lh, ll, after_wide, tile1=None, ahead=None):
                quad(l, [(u % RING, mixer_n(l, u), NC) for u in range(u0, u0 + 4)], lh, ll, after_wide,
                     tile1, ahead)

            def chunk_unit(l, u, lh, ll):
                c, j = divmod(u, 2)
                s, p = u % RING, c % 2
                pe.wait_ge(slot_lo[s], mixer_n(l, u) + 2)
                if j == 0:
                    pe.wait_ge(acc_read[p], n_acc[p].take(l) + 1)
                vh, vl = (w[:, s, :].rearrange("p (k n) -> p k n", k=4) for w in (whi, wlo))
                for t in range(NT):
                    if c == 2 and j == 0 and t == 1:
                        pe.wait_ge(acc_read[1], n_acc[1].at(l) + 1)
                    last = products(acc[:, p, t, :], [(4 * j + k, k) for k in range(4)], 0, KT - 1, lh, ll, t,
                                    lambda k: vh[:, k, :], lambda k: vl[:, k, :])
                if j == 1:
                    last.then_inc(acc_full[p], 1)

            def chunk(l, c, lh=xTh, ll=xTl):
                chunk_unit(l, 2 * c, lh, ll)
                chunk_unit(l, 2 * c + 1, lh, ll)

            def transpose_heads(l, src, n, width=P, banks=range(4), heads=2):
                for q, b in enumerate(banks):
                    aux_wait(l, b)
                    for k in range(heads):
                        for t in range(NT):
                            h = heads * q + k
                            last = nc.tensor.transpose(aux[0:width, b, (2 * k + t) * P:(2 * k + t + 1) * P],
                                                       src(t, h), ident[:])
                    aux_end(b, last)

            def scores(l, h):
                for m in range(2):
                    aux_wait(l, m)
                    d = slice(m * HD, (m + 1) * HD)
                    nc.tensor.matmul(aux[:, m, 0:P], qT[d, h, 0:P], kT[d, h, 0:P], start=True, stop=True)
                    last = nc.tensor.matmul(aux[:, m, P:3 * P], qT[d, h, P:S], kT[d, h, 0:S],
                                            start=True, stop=True)
                    aux_end(m, last)

            def prob_transposes(l, src):
                aux_wait(l, 2)
                for k in range(3):
                    last = nc.tensor.transpose(aux[:, 2, k * P:(k + 1) * P], src[:, k * P:(k + 1) * P], ident[:])
                aux_end(2, last)

            def values(l, v, width):
                aux_wait(l, 2)
                aux_wait(l, 3)
                nc.tensor.matmul(aux[:, 3, 0:width], aT[:, 0:P], v[0], start=True, stop=True)
                o1 = aux[:, 3, width:2 * width]
                nc.tensor.matmul(o1, aT[:, P:2 * P], v[0], start=True, stop=False)
                last = nc.tensor.matmul(o1, aT[:, 2 * P:3 * P], v[1], start=False, stop=True)
                aux_end(3, last)

            def mixer(l):
                x_T(l, 1, 0)
                mixer_quad(l, 0, xTh, xTl, True, tile1=lambda: x_T(l, 1, 1))
                pe.wait_ge(small_in, 80 * l + 80)
                for b in range(2):
                    aux_wait(l, b)
                    for k in range(4):
                        last = nc.tensor.transpose(aux[:, b, k * P:(k + 1) * P], sgu_raw[:, 4 * b + k, :], ident[:])
                    aux_end(b, last)
                chunk(l, 2)
                chunk(l, 3)
                chunk(l, 4)
                aux_all(l)
                pe.wait_ge(vn_ready, 2 * l + 2)
                for b in range(4):
                    for k in range(2):
                        g = 2 * b + k
                        last = nc.tensor.matmul(aux[:, b, k * S:(k + 1) * S].rearrange("p (t c) -> p t c", t=NT),
                                                wT[:, g, :], bv[:, :, g * P:(g + 1) * P], start=True, stop=True)
                    aux_end(b, last)
                chunk(l, 5)
                aux_all(l)
                for t in range(NT):
                    transpose_tile(l, bu, t)
                chunk(l, 6)
                pe.wait_ge(roped, 4 * l + 2)
                transpose_heads(l, lambda t, h: bq[:, t, h * P:(h + 1) * P], 8)
                chunk(l, 7)
                chunk(l, 8)
                pe.wait_ge(roped, 4 * l + 4)
                transpose_heads(l, lambda t, h: bk[:, t, h * P:(h + 1) * P], 8)
                chunk(l, 9)
                aux_all(l)
                scores(l, 0)
                for h in range(H1):
                    for u in HEAD_UNITS[h]:
                        chunk_unit(l, u, *((xTh, xTl) if u < 28 else (yTh, yTl)))
                    pe.wait_ge(a_ready, l * H1 + h + 1)
                    prob_transposes(l, pa)
                    if h + 1 < H1:
                        scores(l, h + 1)
                    if h == 0:
                        for p in range(2):
                            pe.wait_ge(acc_read[p], l * ACC_LAYER + 7)
                    values(l, [bval[:, t, h * P:(h + 1) * P] for t in range(NT)], P)
                aux_wait(l, 3)
                for t in range(NT):
                    transpose_tile(l, bu, t)

                def m_T(t):
                    transpose_tile(l, bg[:, 0], t, lambda half: pe.wait_ge(m_ready, 2 * l + t + 1))

                mixer_quad(l, 32, xTh, xTl, False, ahead=lambda: m_T(0))
                mixer_quad(l, 36, yTh, yTl, True, tile1=lambda: m_T(1), ahead=lambda: x_T(l, 2, 0))

            with pe.Fori(0, DEPTH) as l:
                x_T(l, 0, 0)
                ffn1(l, 0)
                mixer(l)
                ffn1(l, 1)
                for c in n_aux + n_acc:
                    c.layer_ends()

            l = L2

            def job(name, lh=xTh, ll=xTl, kt0=0):
                g = JOB[name]
                p, n = g["acc"][0]
                pe.wait_ge(acc_read[p], acc_n2(p, n) + 1)
                for (s, n), (k0, k1, cols, *_) in zip(g["slots"], g["units"]):
                    pe.wait_ge(slot_lo[s], slot_n2(s, n) + 2)
                    vh, vl = (w[:, s, 0:(k1 - k0) * cols].rearrange("p (k n) -> p k n", k=k1 - k0)
                              for w in (whi, wlo))
                    for t in range(NT):
                        if g["after_wide"] and k0 == 0:
                            pe.wait_ge(acc_read[t], n_acc[t].at(l) + 1)
                        last = products(acc[:, p, t, 0:cols],
                                        [(kt0 + k, k - k0) for k in range(k0, k1)], kt0, kt0 + g["kts"] - 1,
                                        lh, ll, t, lambda k: vh[:, k, :], lambda k: vl[:, k, :])
                last.then_inc(acc_full[p], 1)
                n_acc[p].k += 1

            def quad2(name, lh, ll, tile1=None, ahead=None):
                g = JOB[name]
                quad(l, [(s, slot_n2(s, n), unit[2]) for (s, n), unit in zip(g["slots"], g["units"])], lh, ll,
                     g["after_wide"], tile1, ahead)

            n_norm = [0]

            def norm_T(t):
                if t == 0:
                    n_norm[0] += 1
                n = n_norm[0] - 1
                transpose_tile(l, bv, t, lambda half: pe.wait_ge(xn_ready, 4 * n + 2 * t + half + 1))

            def norm_T0():
                norm_T(0)

            def norm_T1():
                norm_T(1)

            def heads2(n_heads, q, k, v, n0):
                def score(h):
                    if h >= 3:
                        pe.wait_ge(s_ready, DEPTH * H1 + n0 + h - 2)
                    sc = score_bank(h)
                    nc.tensor.matmul(sc[:, 0:P], q(h, 0), k(h, 0, P), start=True, stop=True)
                    nc.tensor.matmul(sc[:, P:3 * P], q(h, 1), k(h, 0, S), start=True, stop=True)\
                        .then_inc(score_full, 1)

                def transposes(h):
                    b = 2 + h % 2
                    aux_wait(l, b)
                    pe.wait_ge(a_ready, DEPTH * H1 + n0 + h + 1)
                    for c in range(3):
                        last = nc.tensor.transpose(aux[:, b, c * P:(c + 1) * P], probs(h)[:, c * P:(c + 1) * P],
                                                   ident[:])
                    aux_end(b, last)

                def values(h):
                    pe.wait_ge(aux_read[2 + h % 2], at_T[h])
                    g = (n0 + h) // 2
                    if h % 2 == 0 and g >= 2:
                        pe.wait_ge(o_read, g - 1)
                    o = o_pair(g)[(h % 2) * HD:(h % 2 + 1) * HD, :]
                    p = probs_T(h)
                    v0, v1 = v(h)
                    nc.tensor.matmul(o[:, 0:P], v0, p[:, 0:P], start=True, stop=True)
                    nc.tensor.matmul(o[:, P:S], v0, p[:, P:2 * P], start=True, stop=False)
                    nc.tensor.matmul(o[:, P:S], v1, p[:, 2 * P:3 * P], start=False, stop=True).then_inc(o_full, 1)

                at_T = {}
                aux_all(l)
                for h in range(3):
                    score(h)
                for h in range(n_heads):
                    transposes(h)
                    at_T[h] = n_aux[2 + h % 2].at(l) + 1
                    if h + 3 < n_heads:
                        score(h + 3)
                    if h > 0:
                        values(h - 1)
                values(n_heads - 1)

            def feed_forward2(i):
                g = JOB[f"ff{i}"]

                def view(w):
                    v = w.rearrange("p (k n) -> p k n", k=4)
                    return lambda k: v[:, k, :]

                def side_T():
                    pe.wait_ge(side_in, 16 * (i + 1))
                    aux_wait(l, 0)
                    for f in range(2):
                        for t in range(NT):
                            last = nc.tensor.transpose(aux[:, 0, (2 * f + t) * P:(2 * f + t + 1) * P],
                                                       bq[:, t, f * P:(f + 1) * P], ident[:])
                    aux_end(0, last)

                feed_forward(l, lambda s: slot_n2(s, g["n0"][s]),
                             [(g["s0"] + j) % RING for j in range(RING)], view, 4, NF2, norm_T1, side_T)

            def ff_and_side(i):
                feed_forward2(i)
                (s, n), = JOB[f"side{i}"]["slots"]
                pe.wait_ge(slot_lo[s], slot_n2(s, n) + 2)
                aux_wait(l, 0)
                vh, vl = (w[:, s, :].rearrange("p (k n) -> p k n", k=2) for w in (whi, wlo))
                for t in range(NT):
                    acc_wait(l, t, True)
                    for half in range(2):
                        col = slice(half * NC, (half + 1) * NC)
                        last = products(acc[:, half, t, :], [(k, k) for k in range(2)], 0, 1, yTh, yTl, t,
                                        lambda k: vh[:, k, col], lambda k: vl[:, k, col])
                    last.then_inc(acc_full[t], 1)
                    if t == 0:
                        norm_T0()
                for p in range(2):
                    n_acc[p].k += 1
                quad2(f"g{i}", xTh, xTl, tile1=norm_T1, ahead=norm_T0 if i == 0 else None)

            norm_T0()
            quad2("c", xTh, xTl, tile1=norm_T1)
            job("qb")
            pe.wait_ge(low_ready, 1)
            for t in range(NT):
                aux_wait(l, t)
                for k in range(3):
                    c0 = t * Q_LORA + k * P
                    last = nc.tensor.transpose(aux[:, t, k * P:(k + 1) * P], flat(mix_par)[:, c0:c0 + P],
                                               ident[:])
                aux_end(t, last)
            pe.wait_ge(low_ready, 2)
            aux_wait(l, 2)
            for k in range(2):
                for t in range(NT):
                    c0 = 2 * Q_LORA + t * (KV_LORA + ROPE2) + k * P
                    last = nc.tensor.transpose(aux[:, 2, (2 * k + t) * P:(2 * k + t + 1) * P],
                                               flat(mix_par)[:, c0:c0 + P], ident[:])
            aux_end(2, last)
            job("kb")
            job("vb")
            aux_all(l)
            job("uq0", yTh, yTl, 0)
            job("uq1", yTh, yTl, 0)
            job("ukv0", yTh, yTl, 3)
            job("ukv1", yTh, yTl, 3)
            qb, kb, vb, qbT = (bg_flat[:, k * D:(k + 1) * D] for k in range(4))
            kbT = qb
            for q, src in enumerate((qb, kb)):
                pe.wait_ge(heads_ready, q + 1)
                aux_all(l)
                transpose_heads(l, lambda t, h: src[:, t * NC + h * P:t * NC + (h + 1) * P], 4, banks=[0, 1])
            pe.wait_ge(heads_ready, 3)
            transpose_heads(l, lambda t, h: flat(bu)[:, t * 768 + h * MLA_D:t * 768 + (h + 1) * MLA_D], 8,
                            width=MLA_D)
            pe.wait_ge(heads_ready, 4)
            transpose_heads(l, lambda t, h: flat(mix_par)[:, t * 768 + h * MLA_D:t * 768 + (h + 1) * MLA_D], 8,
                            width=MLA_D)
            aux_all(l)
            for name in ("ukv0", "ukv1"):
                p, n = JOB[name]["acc"][0]
                pe.wait_ge(acc_read[p], acc_n2(p, n) + 2)
            heads2(MLA_H, lambda h, t: qT[0:MLA_D, h, t * P:(t + 1) * P], lambda h, k0, k1: kT[0:MLA_D, h, k0:k1],
                   lambda h: [bval[:, t, h * P + MLA_N:(h + 1) * P] for t in range(NT)], 0)

            def half(t_, h, c0, c1):
                return t_[(h % 2) * HD:(h % 2 + 1) * HD, (h // 2) * S + c0:(h // 2) * S + c1]

            heads2(DIL_H, lambda h, t: half(qbT, h, t * P, (t + 1) * P), lambda h, k0, k1: half(kbT, h, k0, k1),
                   lambda h: [vb[:, t * NC + h * HD:t * NC + (h + 1) * HD] for t in range(NT)], MLA_H)
            pe.wait_ge(o_read, (MLA_H + DIL_H) // 2)
            quad2("eout", yTh, yTl, ahead=norm_T0)
            ff_and_side(0)
            quad2("z01", xTh, xTl, tile1=norm_T1)
            for k in range(2, 4):
                job(f"z{k}")
            pe.wait_ge(heads_ready, 5)
            transpose_heads(l, lambda t, h: bq[:, t, h * P:(h + 1) * P], 8)
            job("z4")
            job("z5")
            pe.wait_ge(heads_ready, 6)
            transpose_heads(l, lambda t, h: bu[:, t, h * P:(h + 1) * P], 8)
            aux_all(l)
            for name in ("z4", "z5"):
                p, n = JOB[name]["acc"][0]
                pe.wait_ge(acc_read[p], acc_n2(p, n) + 2)
            heads2(MOBA_H, lambda h, t: half(flat(bv), h, t * P, (t + 1) * P),
                   lambda h, k0, k1: half(flat(bq), h, k0, k1),
                   lambda h: [bval[:, t, h * HD:(h + 1) * HD] for t in range(NT)], MLA_H + DIL_H)
            pe.wait_ge(o_read, (MLA_H + DIL_H + MOBA_H) // 2)
            quad2("oout", yTh, yTl, ahead=norm_T0)
            ff_and_side(1)

        def places_x(tiles=range(NT)):
            for t in tiles:
                for half in range(2):
                    yield (2 * t + half, aux[:, 2 * t + half, :].rearrange("p (k c) -> p k c", k=4),
                           (slice(4 * half, 4 * half + 4), slice(t * P, (t + 1) * P)))

        def place_pair(b, k0):
            return b, aux[:, b, :].rearrange("p (k c) -> p k c", k=2), (slice(k0, k0 + 2), slice(0, S))

        def places_cq():
            for t in range(NT):
                yield t, aux[:, t, 0:3 * P].rearrange("p (k c) -> p k c", k=3), (slice(0, 3), slice(t * P, (t + 1) * P))

        @block.scalar
        def _(act):
            n_acc = [Uses(ACC_LAYER), Uses(ACC_LAYER)]
            n_aux = [Uses(k) for k in AUX_LAYER]
            n_used = Uses(USED_LAYER)

            def high(s, n, size=UNIT):
                act.wait_ge(slot_full[s], 32 * n + 32)
                nc.scalar.copy(whi[:, s, 0:size], raw[:, s, 0:size]).then_inc(slot_hi[s], 1)

            def high_T(l, places, dst):
                for b, src, (k, tok) in places:
                    act.wait_ge(aux_full[b], n_aux[b].take(l) + 1)
                    nc.scalar.copy(dst[:, k, tok], src).then_inc(t_hi, 1)

            def acc_done(l, p):
                act.wait_ge(acc_full[p], n_acc[p].take(l) + 1)

            def copy_banks(l, dst, banks=range(4), parts=P):
                for q, b in enumerate(banks):
                    act.wait_ge(aux_full[b], n_aux[b].take(l) + 1)
                    nc.scalar.copy(dst[0:parts, q * NC:(q + 1) * NC], aux[0:parts, b, :])\
                        .then_inc(aux_read[b], 1)

            def used_wait(l):
                act.wait_ge(unit_used, n_used.take(l) + 1)

            def wide_read(t, dst, func=ACT.Copy, scale=1.0):
                for half in range(2):
                    last = nc.scalar.activation(dst[:, half * NC:(half + 1) * NC], acc[:, half, t, :], func,
                                                scale=scale)
                last.then_inc(acc_read[t], 1)

            def feed_forward(l, slot0, which_slots, func, cols, t_banks, iters, tile1, before_last=None,
                             last_slot=None):
                aux0 = [n_aux[0].at(l), n_aux[1].at(l)]
                down_slots = which_slots[2:]
                nd = len(down_slots)
                used0 = n_used.at(l)

                def activate(i, t):
                    act.wait_ge(aux_full[t], aux0[t] + i + 1)
                    nc.scalar.activation(act_b[:, t, 0:cols], aux[:, t, 0:cols], func).then_inc(act_done, 1)

                def transposed(i, k0=0):
                    for b in t_banks:
                        act.wait_ge(aux_full[b], aux0[b] + i + 1)
                        _, src, (k, tok) = place_pair(b, k0 + 2 * (b - 2))
                        nc.scalar.copy(yTh[:, k, tok], src).then_inc(t_hi, 1)

                activate(0, 0)
                tile1()
                aux0 += [n_aux[2].at(l), n_aux[3].at(l)]
                act.wait_ge(unit_used, used0 + 1)
                high(which_slots[0], slot0(which_slots[0]) + 1)
                activate(0, 1)
                high(which_slots[1], slot0(which_slots[1]) + 1)
                for s in down_slots + ([] if last_slot is None else [last_slot]):
                    high(s, slot0(s))

                def iteration(i, down_slots, last=False):
                    activate(i, 0)
                    transposed(i - 1)
                    used = used0 + 1 + (i - 1) * (1 + nd)
                    act.wait_ge(unit_used, used + 1)
                    high(which_slots[0], slot0(which_slots[0]) + i + 1)
                    activate(i, 1)
                    if last:
                        transposed(i, 2 * len(t_banks))
                    high(which_slots[1], slot0(which_slots[1]) + i + 1)
                    for q, s in enumerate(down_slots):
                        act.wait_ge(unit_used, used + 2 + q)
                        high(s, slot0(s) + i)

                with act.Fori(1, iters - 1) as i:
                    iteration(i, down_slots)
                iteration(iters - 1, down_slots if last_slot is None else [], last=True)
                for b in [0, 1, *t_banks]:
                    n_aux[b].k += iters
                if before_last is not None:
                    before_last()
                n_used.k += iters + (iters - 1) * nd

            def mixer(l):
                act.wait_ge(unit_used, n_used.at(l))
                high(2, mixer_n(l, 2))
                high_T(l, places_x([0]), xTh)
                for p in range(2):
                    acc_done(l, p)
                high(3, mixer_n(l, 3))
                high_T(l, places_x([1]), xTh)

                def split(u):
                    if u < 2 * CH + 2:
                        high(u % RING, mixer_n(l, u))

                def to_sbuf(c, dst, func):
                    p = c % 2
                    col = slice(p * NC, (p + 1) * NC)
                    nc.scalar.activation(dst[:, :, col], acc[:, p], func).then_inc(acc_read[p], 1)

                def head_exp(h):
                    act.wait_ge(s_ready, l * H1 + h + 1)
                    for m in range(2):
                        for t, c in ((0, slice(0, P)), (1, slice(P, 3 * P))):
                            last = nc.scalar.activation(SE[:, h % 2, m, c], SE[:, h % 2, m, c], ACT.Exp,
                                                        bias=rmax[:, h % 2, 2 * m + t:2 * m + t + 1],
                                                        scale=HD ** -0.5,
                                                        accum_out=rsum[:, h % 2, 2 * m + t:2 * m + t + 1])
                    last.then_inc(e_ready, 1)

                def probs_T(h):
                    act.wait_ge(aux_full[2], n_aux[2].take(l) + 1)
                    nc.scalar.copy(aT, aux[:, 2, 0:3 * P]).then_inc(aux_read[2], 1)

                def head_out(h):
                    act.wait_ge(aux_full[3], n_aux[3].take(l) + 1)
                    for t in range(NT):
                        last = nc.scalar.activation(bu[:, t, h * P:(h + 1) * P], aux[:, 3, t * P:(t + 1) * P],
                                                    ACT.Square, accum_out=ssq[:, t, h:h + 1])
                    last.then_inc(sq_ready, 1)

                acc_done(l, 0)
                wide_read(0, bv[:, 0, :], ACT.Gelu)
                for j in range(3):
                    used_wait(l)
                    split(4 + j)
                acc_done(l, 1)
                wide_read(1, bv[:, 1, :], ACT.Gelu)
                split(7)
                for b in range(2):
                    n_aux[b].k += 1
                for c in range(2, 10):
                    acc_done(l, c % 2)
                    split(2 * c + 4)
                    split(2 * c + 5)
                    if c < 4:
                        to_sbuf(c, bu, ACT.Gelu)
                    elif c >= 8:
                        to_sbuf(c, bval, ACT.Copy)
                    if c == 4:
                        for b in range(4):
                            n_aux[b].k += 1
                    if c == 5:
                        high_T(l, places_x(), yTh)
                    if c == 6:
                        copy_banks(l, flat(bv))
                    if c == 8:
                        copy_banks(l, flat(bq))
                act.wait_ge(lam_dot, l + 1)
                nc.scalar.activation(lam_t[:, 2:4], lam_t[:, 0:2], ACT.Exp).then_inc(lam_exp, 1)
                for m in range(2):
                    n_aux[m].k += H1
                head_exp(0)
                for h in range(H1):
                    probs_T(h)
                    ends = [u // 2 for u in HEAD_UNITS[h] if u % 2]
                    if h == H1 - 1:
                        head_out(h)
                        acc_done(l, 1)
                        split(34)
                        high_T(l, places_x([0]), xTh)
                        split(35)
                        high_T(l, places_x([1]), xTh)
                        break
                    for c in ends:
                        acc_done(l, c % 2)
                        split(2 * c + 4)
                    head_exp(h + 1)
                    for c in ends:
                        split(2 * c + 5)
                        if c < 14:
                            w, p = divmod(c - 10, 2)
                            act.wait_ge(acc_read[p], l * ACC_LAYER + 1 + c // 2 + 2)
                            g = bg[:, w, :, p * NC:(p + 1) * NC]
                            nc.scalar.activation(g, g, ACT.Tanh, scale=0.5).then_inc(tanh_done, 1)
                    head_out(h)
                for u0, dst in ((32, yTh), (36, xTh)):
                    for j in range(2):
                        used_wait(l)
                        split(u0 + 4 + j)
                    high_T(l, places_x([0]), dst)
                    used_wait(l)
                    split(u0 + 6)
                    acc_done(l, 0)
                    acc_done(l, 1)
                    split(u0 + 7)
                    if u0 == 32:
                        high_T(l, places_x([1]), dst)

            act.wait_ge(angles, 1)
            nc.scalar.activation(ang[:, 2:4], ang[:, 2:4], ACT.Sin).then_inc(sines, 1)
            for s in range(2):
                high(s, 0)
            with act.Fori(0, DEPTH) as l:
                high_T(l, places_x([0]), xTh)
                for which in range(2):
                    feed_forward(l, lambda s: ffn_n(l, which, s), [0, 1, 2],
                                 ACT.Silu, FB, [2], NF, lambda: high_T(l, places_x([1]), xTh), last_slot=3)
                    if which == 0:
                        mixer(l)
                for p in range(2):
                    acc_done(l, p)
                for c in n_aux + n_acc + [n_used]:
                    c.layer_ends()

            l = L2
            n_norm = [0]

            def split_after(name):
                g = JOB[name]
                for u in units_after(g):
                    high_unit(u)

            def high_unit(u):
                g = job_of_unit(u)
                if g["units"] is None:
                    s = (g["s0"] + u - g["u0"]) % RING
                    high(s, slot_n2(s, g["n0"][s]))
                else:
                    s, n = g["slots"][u - g["u0"]]
                    k0, k1, cols = g["units"][u - g["u0"]][:3]
                    high(s, slot_n2(s, n), (k1 - k0) * cols)

            def acc_full2(name, t):
                act.wait_ge(acc_full[t], acc_n2(*JOB[name]["acc"][t]) + 1)

            def split_unit(name, j):
                g = JOB[name]
                if j < 3:
                    act.wait_ge(unit_used, used_n2(g["used"]) + j + 1)
                else:
                    acc_full2(name, 1)
                u = g["u0"] + RING + j
                if u < N_UNITS and not in_ff(u):
                    high_unit(u)

            def full(name):
                p, n = JOB[name]["acc"][0]
                act.wait_ge(acc_full[p], acc_n2(p, n) + 1)

            def done(name):
                full(name)
                split_after(name)

            def to_sbuf(name, dst, func=ACT.Copy, scale=1.0):
                g = JOB[name]
                p = g["acc"][0][0]
                nc.scalar.activation(dst, acc[:, p, :, 0:g["cols"]], func, scale=scale).then_inc(acc_read[p], 1)

            def squares(t):
                if t == 0:
                    n_norm[0] += 1
                n = n_norm[0] - 1
                act.wait_ge(x_ready, X_LAST - 4 + 2 * (t + 1) if n == 0 else X_LAST + 2 * (n - 1) + t + 1)
                nc.scalar.activation(bv[:, t, :], x[:, t, :], ACT.Square, scale=D ** -0.5,
                                     accum_out=ssq[:, t, 0:1])\
                    .then_inc(sumsq, 1)

            def heads2(n_heads, n0):
                def exps(h):
                    act.wait_ge(s_ready, n0 + h + 1)
                    for t, c in ((0, slice(0, P)), (1, slice(P, 3 * P))):
                        last = nc.scalar.activation(probs(h)[:, c], probs(h)[:, c], ACT.Exp,
                                                    bias=row(rmax, h, t), accum_out=row(rsum, h, t))
                    last.then_inc(e_ready, 1)

                def outputs(g):
                    act.wait_ge(o_full, 2 * g + 2)
                    nc.scalar.copy(yTh[:, g % KT, :], o_pair(g)).then_inc(t_hi, 1)

                exps(0)
                h0 = n0 - DEPTH * H1
                for h in range(n_heads):
                    if h + 1 < n_heads:
                        exps(h + 1)
                    b = 2 + h % 2
                    act.wait_ge(aux_full[b], n_aux[b].take(l) + 1)
                    if h >= 2:
                        act.wait_ge(o_full, h0 + h - 1)
                    nc.scalar.copy(probs_T(h), aux[:, b, 0:3 * P]).then_inc(aux_read[b], 1)
                    if h % 2 and h > 1:
                        outputs((h0 + h - 3) // 2)
                outputs((h0 + n_heads) // 2 - 1)
            def ff_and_side(i):
                g = JOB[f"ff{i}"]
                end = g["u0"] + g["nu"]
                n_used.k = g["used"]
                feed_forward(l, lambda s: slot_n2(s, g["n0"][s]), [(g["s0"] + j) % RING for j in range(RING)],
                             ACT.Relu, NC, [2, 3], NF2, lambda: high_T(l, places_x([1]), xTh),
                             lambda: high_T(l, [place_pair(0, 0)], yTh))
                squares(0)
                act.wait_ge(unit_used, used_n2(g["used"]) + 3 * NF2 - 1)
                high_unit(end + 2)
                squares(1)
                acc_full2(f"side{i}", 0)
                wide_read(0, bg[:, 1, 0, :])
                high_T(l, places_x([0]), xTh)
                high_unit(end + 3)
                acc_full2(f"side{i}", 1)
                wide_read(1, bg[:, 1, 1, :])
                high_unit(end + 4)
                high_T(l, places_x([1]), xTh)
                name = f"g{i}"
                acc_full2(name, 0)
                wide_read(0, bg[:, 0, 0, :], ACT.Tanh, 0.5)
                if i == 0:
                    squares(0)
                    for j in range(2):
                        split_unit(name, j)
                    high_T(l, places_x([0]), xTh)
                    split_unit(name, 2)
                    split_unit(name, 3)
                acc_full2(name, 1)
                wide_read(1, bg[:, 0, 1, :], ACT.Tanh, 0.5)
                if i == 0:
                    squares(1)
                    high_T(l, places_x([1]), xTh)

            def out_norm(name):
                squares(0)
                for j in range(2):
                    split_unit(name, j)
                high_T(l, places_x([0]), xTh)
                squares(1)

            squares(0)
            squares(1)
            high_T(l, places_x([0]), xTh)
            for u in (2, 3):
                high_unit(u)
            high_T(l, places_x([1]), xTh)
            mixf = flat(mix_par)
            for t in range(NT):
                acc_full2("c", t)
                nc.scalar.activation(aT, acc[:, 0, t, 0:Q_LORA], ACT.Square, accum_out=ssq[:, t, 1:2])
                act.drain()
                nc.scalar.activation(aT[:, 0:KV_LORA], acc[:, 1, t, 0:KV_LORA], ACT.Square,
                                     accum_out=ssq[:, t, 2:3])
                act.drain()
                nc.scalar.copy(mixf[:, t * Q_LORA:(t + 1) * Q_LORA], acc[:, 0, t, 0:Q_LORA])
                w = KV_LORA + ROPE2
                c0 = NT * Q_LORA + t * w
                nc.scalar.copy(mixf[:, c0:c0 + w], acc[:, 1, t, 0:w])
                act.drain().then_inc(acc_read[t], 1)
                if t == 0:
                    for j in range(3):
                        split_unit("c", j)
            split_unit("c", 3)
            def two(ap):
                return ap.rearrange("p (t c) -> p t c", t=NT)

            def with_squares(name, sq, dst):
                g = JOB[name]
                p = g["acc"][0][0]
                for d, func in ((sq, ACT.Square), (dst, ACT.Copy)):
                    nc.scalar.activation(d, acc[:, p, :, 0:g["cols"]], func)
                act.drain().then_inc(acc_read[p], 1)

            bkf = flat(bk)
            done("qb")
            with_squares("qb", two(bkf[:, 0:D]), two(bg_flat[:, 0:D]))
            high_T(l, places_cq(), yTh)
            high_T(l, [place_pair(2, 3)], yTh)
            done("kb")
            with_squares("kb", two(bkf[:, D:2 * D]), two(bg_flat[:, D:2 * D]))
            done("vb")
            to_sbuf("vb", bg_flat[:, 2 * D:3 * D].rearrange("p (t c) -> p t c", t=NT))
            qa = flat(bu)[:, 0:NT * MLA_H * MLA_D].rearrange("p (t c) -> p t c", t=NT)
            for k in range(2):
                full(f"uq{k}")
                c = slice(k * 384, (k + 1) * 384)
                with_squares(f"uq{k}", two(flat(bq)[:, 0:NT * MLA_H * MLA_D])[:, :, c], qa[:, :, c])
            for k in range(2):
                full(f"ukv{k}")
                c = slice(k * NC, (k + 1) * NC)
                with_squares(f"ukv{k}", bv[:, :, c], bval[:, :, c])
            copy_banks(l, bg_flat[:, 3 * D:4 * D], banks=[0, 1])
            copy_banks(l, bg_flat[:, 0:D], banks=[0, 1])
            for name in ("uq0", "uq1", "ukv0", "ukv1"):
                split_after(name)
            copy_banks(l, flat(bv), parts=MLA_D)
            copy_banks(l, flat(bq), parts=MLA_D)
            heads2(MLA_H, DEPTH * H1)
            heads2(DIL_H, DEPTH * H1 + MLA_H)
            out_norm("eout")
            ff_and_side(0)
            for t in range(NT):
                acc_full2("z01", t)
                for half in range(2):
                    c = slice(half * NC, (half + 1) * NC)
                    for dst, func in ((bk, ACT.Square), (bq, ACT.Copy)):
                        nc.scalar.activation(dst[:, t, c], acc[:, half, t, :], func)
                act.drain().then_inc(acc_read[t], 1)
                for j in ((3,) if t else range(3)):
                    split_unit("z01", j)
            for k in range(2, 6):
                if k < 5:
                    done(f"z{k}")
                else:
                    full(f"z{k}")
                c = slice((k % 2) * NC, (k % 2 + 1) * NC)
                if k < 4:
                    act.wait_ge(heads_ready, 5)
                    with_squares(f"z{k}", bk[:, :, c], bu[:, :, c])
                else:
                    to_sbuf(f"z{k}", bval[:, :, c])
                if k == 3:
                    copy_banks(l, flat(bv))
            copy_banks(l, flat(bq))
            split_after("z5")
            heads2(MOBA_H, DEPTH * H1 + MLA_H + DIL_H)
            out_norm("oout")
            ff_and_side(1)

        @block.vector
        def _(dve):
            n_acc = [Uses(ACC_LAYER), Uses(ACC_LAYER)]
            n_aux = [Uses(k) for k in AUX_LAYER]
            n_hi = Uses(2 * NF + 6 * 4)
            V = nc.vector

            def low(s, n, size=UNIT):
                dve.wait_ge(slot_hi[s], n + 1)
                V.tensor_tensor(wlo[:, s, 0:size], raw[:, s, 0:size], cast(whi[:, s, 0:size]), ALU.subtract)\
                    .then_inc(slot_lo[s], 1)

            def low_T(l, places, dst_l, dst_h):
                for b, src, (k, tok) in places:
                    dve.wait_ge(t_hi, n_hi.take(l) + 1)
                    V.tensor_tensor(dst_l[:, k, tok], src, cast(dst_h[:, k, tok]), ALU.subtract)\
                        .then_inc(aux_read[b], 1)
                    n_aux[b].k += 1

            def mean_and_var(src, t):
                for half in range(2):
                    V.bn_stats(stat[:, t, half, :], src[:, t, half * NC:(half + 1) * NC])
                dve.drain()
                V.bn_aggr(mv[:, t, :], stat[:, t, :, :].rearrange("p a b -> p (a b)")).then_inc(var_ready, 1)
                dve.drain()

            def scale_shift(l, n, src, t, col, par, ready):
                halves = [slice(half * NC, (half + 1) * NC) for half in range(2)]
                for c in halves:
                    V.scalar_tensor_tensor(src[:, t, c], src[:, t, c], mv[:, t, 0:1], par[:, 0, c],
                                           ALU.subtract, ALU.mult)
                    dve.drain()
                    if c is halves[0]:
                        dve.wait_ge(rstd_ready, RSTD_LAYER * l + n + t + 1)
                    last = V.scalar_tensor_tensor(src[:, t, c], src[:, t, c], nx[:, col + t:col + t + 1],
                                                  par[:, 1, c], ALU.mult, ALU.add)
                    if ready is x_ready or c is halves[1]:
                        last.then_inc(ready, 1)

            def acc_wait(l, p):
                dve.wait_ge(acc_full[p], n_acc[p].take(l) + 1)

            def add_tile(l, t):
                acc_wait(l, t)
                for half in range(2):
                    c = slice(half * NC, (half + 1) * NC)
                    last = V.scalar_tensor_tensor(x[:, t, c], x[:, t, c], 2 * ALPHA, acc[:, half, t, :],
                                                  ALU.mult, ALU.add)
                last.then_inc(acc_read[t], 1)

            def norm_tile(l, k, t):
                dve.drain()
                mean_and_var(x, t)
                dve.wait_ge(ln_in, 32 * (3 * l + k) + 32)
                scale_shift(l, RSTD_NORM[k], x, t, 0, ln_par, x_ready)
                if t == NT - 1:
                    dve.drain().then_inc(ln_free, 1)

            def feed_forward(l, slot0, which_slots, act0, other, cols, t_banks, iters, tile1, before_last=None,
                             last_slot=None):
                down_slots = which_slots[2:]
                aux0 = []

                def multiply(i, t):
                    dve.wait_ge(act_done, act0 + 2 * i + t + 1)
                    V.tensor_tensor(gate_b[:, t, 0:cols], act_b[:, t, 0:cols], other(t), ALU.mult)\
                        .then_inc(aux_read[t], 1)

                def transposed(i, k0=0):
                    for q, b in enumerate(t_banks):
                        dve.wait_ge(t_hi, h0 + len(t_banks) * i + q + 1)
                        _, src, (k, tok) = place_pair(b, k0 + 2 * (b - 2))
                        V.tensor_tensor(yTl[:, k, tok], src, cast(yTh[:, k, tok]), ALU.subtract)\
                            .then_inc(aux_read[b], 1)

                multiply(0, 0)
                tile1()
                h0 = n_hi.at(l)
                aux0 = [n_aux[b].at(l) for b in range(4)]
                low(which_slots[0], slot0(which_slots[0]) + 1)
                multiply(0, 1)
                low(which_slots[1], slot0(which_slots[1]) + 1)
                for s in down_slots + ([] if last_slot is None else [last_slot]):
                    low(s, slot0(s))

                def iteration(i, down_slots, last=False):
                    for b in t_banks:
                        dve.wait_ge(aux_full[b], aux0[b] + i)
                    multiply(i, 0)
                    transposed(i - 1)
                    low(which_slots[0], slot0(which_slots[0]) + i + 1)
                    multiply(i, 1)
                    if last:
                        transposed(i, 2 * len(t_banks))
                    low(which_slots[1], slot0(which_slots[1]) + i + 1)
                    for s in down_slots:
                        low(s, slot0(s) + i)

                with dve.Fori(1, iters - 1) as i:
                    iteration(i, down_slots)
                iteration(iters - 1, down_slots if last_slot is None else [], last=True)
                for b in [0, 1, *t_banks]:
                    n_aux[b].k += iters
                n_hi.k += len(t_banks) * iters
                if before_last is not None:
                    before_last()

            def rotate(l, c, dst):
                p = c % 2
                dve.drain()
                acc_wait(l, p)
                src = acc[:, p].rearrange("p t (h d) -> p t h d", d=HD)
                out_ = dst[:, :, p * NC:(p + 1) * NC].rearrange("p t (h d) -> p t h d", d=HD)
                tmp = bg_flat[:, D:2 * D].rearrange("p (t h d) -> p t h d", t=NT, d=HD)
                half = HD // 2

                def table(k, c0, c1):
                    return rope[:, k, :, c0:c1].unsqueeze(2).to_broadcast([P, NT, NC // HD, c1 - c0])

                V.tensor_tensor(out_, src, table(0, 0, HD), ALU.mult)
                V.tensor_tensor(tmp[:, :, :, 0:half], src[:, :, :, half:HD], table(1, 0, half), ALU.mult)
                dve.drain()
                V.tensor_tensor(tmp[:, :, :, half:HD], src[:, :, :, 0:half], table(1, half, HD), ALU.mult)\
                    .then_inc(acc_read[p], 1)
                dve.drain()
                V.tensor_tensor(out_, out_, tmp, ALU.add).then_inc(roped, 1)

            def mixer(l):
                dve.wait_ge(const_in, 5 * 16)
                low(2, mixer_n(l, 2))
                add_tile(l, 0)
                norm_tile(l, 0, 0)
                low_T(l, places_x([0]), xTl, xTh)
                add_tile(l, 1)
                low(3, mixer_n(l, 3))
                norm_tile(l, 0, 1)
                low_T(l, places_x([1]), xTl, xTh)

                def split(u):
                    if u < 2 * CH + 2:
                        low(u % RING, mixer_n(l, u))

                def head_scores(h):
                    for m in range(2):
                        dve.wait_ge(aux_full[m], n_aux[m].take(l) + 1)
                        V.tensor_tensor(SE[:, h % 2, m, :], aux[:, m, 0:3 * P], causal[:], ALU.add)\
                            .then_inc(aux_read[m], 1)
                    dve.drain()
                    rm = rmax[:, h % 2, :].rearrange("p (m t) -> p m t", m=2)
                    V.tensor_reduce(rm[:, :, 0], SE[:, h % 2, :, 0:P], AX_X, ALU.max)
                    V.tensor_reduce(rm[:, :, 1], SE[:, h % 2, :, P:3 * P], AX_X, ALU.max)
                    dve.drain()
                    V.tensor_scalar(rmax[:, h % 2, :], rmax[:, h % 2, :], -(HD ** -0.5), None, ALU.mult)\
                        .then_inc(s_ready, 1)

                def head_probs(h):
                    dve.wait_ge(e_ready, l * H1 + h + 1)
                    r = rinv[:, h % 2, :]
                    V.reciprocal(r, rsum[:, h % 2, :])
                    dve.drain()
                    V.tensor_scalar(r[:, 2:4], r[:, 2:4], neg_lam[:], None, ALU.mult)
                    for t, c in ((0, slice(0, P)), (1, slice(P, 3 * P))):
                        V.tensor_scalar(pa[:, c], SE[:, h % 2, 0, c], r[:, t:t + 1], None, ALU.mult)
                    dve.drain()
                    for t, c in ((0, slice(0, P)), (1, slice(P, 3 * P))):
                        last = V.scalar_tensor_tensor(pa[:, c], SE[:, h % 2, 1, c], r[:, 2 + t:3 + t], pa[:, c],
                                                      ALU.mult, ALU.add)
                        if t == 0:
                            dve.drain()
                    last.then_inc(a_ready, 1)

                for j in range(3):
                    split(4 + j)
                for b in range(2):
                    dve.wait_ge(aux_full[b], n_aux[b].take(l) + 1)
                    V.tensor_tensor(wT[:, 4 * b:4 * b + 4, :], aux[:, b, :].rearrange("p (g t) -> p g t", g=4),
                                    tri[:].unsqueeze(1).to_broadcast([P, 4, P]), ALU.mult)\
                        .then_inc(aux_read[b], 1)
                split(7)
                for t in range(NT):
                    dve.wait_ge(acc_read[t], n_acc[t].take(l) + 2)
                    mean_and_var(bv, t)
                    dve.wait_ge(mix_in, 64 * l + 32)
                    scale_shift(l, RSTD_V, bv, t, NT, mix_par, vn_ready)
                dve.drain().then_inc(mix_free, 1)
                lw = lam_w.rearrange("p (a b d) -> p a b d", a=2, b=2)
                V.tensor_tensor(pa[:, 0:2 * HD].rearrange("p (a d) -> p a d", a=2), lw[:, :, 0], lw[:, :, 1],
                                ALU.mult)
                dve.drain()
                V.tensor_reduce(lam_t[:, 0:2], pa[:, 0:2 * HD].rearrange("p (a d) -> p a d", a=2), AX_X, ALU.add)\
                    .then_inc(lam_dot, 1)
                for c in range(2, 10):
                    split(2 * c + 4)
                    split(2 * c + 5)
                    if 4 <= c < 8:
                        rotate(l, c, bq if c < 6 else bk)
                    else:
                        n_acc[c % 2].k += 1
                    if c == 4:
                        for p in range(2):
                            dve.wait_ge(acc_read[p], l * ACC_LAYER + 1 + 2 + 1)
                        for b in range(4):
                            dve.wait_ge(aux_full[b], n_aux[b].take(l) + 1)
                            for k in range(2):
                                g = 2 * b + k
                                u = bu[:, :, g * P:(g + 1) * P]
                                last = V.scalar_tensor_tensor(
                                    u, aux[:, b, k * S:(k + 1) * S].rearrange("p (t c) -> p t c", t=NT),
                                    sgu_bT[:, g:g + 1], u, ALU.add, ALU.mult)
                            last.then_inc(aux_read[b], 1)
                    if c == 5:
                        low_T(l, places_x(), yTl, yTh)
                    if c in (6, 8):
                        for b in range(4):
                            n_aux[b].k += 1
                V.tensor_scalar(diff_g[:], diff_g[:], lam_init[:, 1:2], (2.0 * HD) ** 0.5, ALU.mult, ALU.mult)

                def normalise(h):
                    dve.wait_ge(aux_full[3], n_aux[3].take(l) + 1)
                    dve.wait_ge(rstd_ready, RSTD_LAYER * l + RSTD_HEADS + h + 1)
                    for t in range(NT):
                        last = V.scalar_tensor_tensor(bu[:, t, h * P:(h + 1) * P], aux[:, 3, t * P:(t + 1) * P],
                                                      ny[:, NT * h + t:NT * h + t + 1], diff_g[:],
                                                      ALU.mult, ALU.mult)
                    last.then_inc(aux_read[3], 1)

                def gate_branch0(c):
                    p = c % 2
                    acc_wait(l, p)
                    g = bg[:, 0, :, p * NC:(p + 1) * NC]
                    dve.wait_ge(tanh_done, 4 * l + 4)
                    V.scalar_tensor_tensor(g, g, 1.0, acc[:, p], ALU.add, ALU.mult).then_inc(acc_read[p], 1)

                head_scores(0)
                dve.wait_ge(lam_exp, l + 1)
                V.tensor_tensor(lam_t[:, 0:1], lam_t[:, 3:4], lam_t[:, 2:3], ALU.subtract)
                dve.drain()
                V.tensor_tensor(neg_lam[:], lam_t[:, 0:1], lam_init[:, 0:1], ALU.subtract)
                dve.drain()
                head_probs(0)
                for h in range(H1):
                    if h > 0:
                        normalise(h - 1)
                    if h == H1 - 1:
                        normalise(h)
                        gate_branch0(15)
                        low_T(l, places_x([0]), xTl, xTh)
                        split(34)
                        low_T(l, places_x([1]), xTl, xTh)
                        split(35)
                        break
                    ends = [u // 2 for u in HEAD_UNITS[h] if u % 2]
                    head_scores(h + 1)
                    for c in ends:
                        split(2 * c + 4)
                    head_probs(h + 1)
                    for c in ends:
                        split(2 * c + 5)
                        if c < 14:
                            w, p = divmod(c - 10, 2)
                            acc_wait(l, p)
                            g = bg[:, w, :, p * NC:(p + 1) * NC]
                            if c == 10:
                                dve.wait_ge(mix_in, 64 * l + 64)
                            V.tensor_tensor(g, acc[:, p], mix_par[:, w, p * NC:(p + 1) * NC].unsqueeze(1)
                                            .to_broadcast([P, NT, NC]), ALU.add).then_inc(acc_read[p], 1)
                            if c == 13:
                                dve.drain().then_inc(mix_free, 1)
                        else:
                            gate_branch0(c)
                n_aux[2].k += H1
                for t in range(NT):
                    acc_wait(l, t)
                    for half in range(2):
                        g1 = bg[:, 1, t, half * NC:(half + 1) * NC]
                        last = V.scalar_tensor_tensor(g1, g1, 1.0, acc[:, half, t, :], ALU.add, ALU.mult)
                    last.then_inc(acc_read[t], 1)
                    dve.drain()
                    g0 = bg[:, 0, t, :]
                    V.tensor_tensor(g0, g0, bg[:, 1, t, :], ALU.add).then_inc(m_ready, 1)
                    if t == 0:
                        split(36)
                        split(37)
                        low_T(l, places_x([0]), yTl, yTh)
                        split(38)
                dve.drain().then_inc(small_free, 1)
                split(39)
                low_T(l, places_x([1]), yTl, yTh)
                add_tile(l, 0)
                norm_tile(l, 1, 0)
                split(40)
                split(41)
                low_T(l, places_x([0]), xTl, xTh)
                add_tile(l, 1)
                norm_tile(l, 1, 1)

            for s in [*slot_lo, *acc_read, *aux_read, ln_free, mix_free]:
                dve.sem_inc(s, 1)
            dve.wait_ge(x_in, 16)
            dve.sem_inc(x_ready, 4)
            dve.wait_ge(angle_in, 2 * 16)
            pos_f = lam_t[:, 0:NT]
            V.tensor_copy(pos_f, pos_i[:])
            dve.drain()
            for t in range(NT):
                V.tensor_scalar(ang[:, 0, t, :], inv_freq, pos_f[:, t:t + 1], None, ALU.mult)
            dve.drain()
            big = 12582912.0
            parts = two_pi_parts()
            for k, turn in enumerate((0.0, 0.25)):
                V.tensor_scalar(turns[:, k], ang[:, 0], 1.0 / (2 * PI), turn, ALU.mult, ALU.add)
            dve.drain()
            for op in (ALU.add, ALU.subtract):
                V.tensor_scalar(turns, turns, big, None, op)
                dve.drain()
            for c in parts:
                for k in range(2):
                    src = ang[:, 0] if c == parts[0] else ang[:, 2 + k]
                    V.scalar_tensor_tensor(ang[:, 2 + k], turns[:, k], -c, src, ALU.mult, ALU.add)
                dve.drain()
            V.tensor_scalar(ang[:, 3], ang[:, 3], PI / 2, None, ALU.add)
            dve.drain()
            V.tensor_scalar(ang[:, 2:4], ang[:, 2:4], PI32, -PI32, ALU.min, ALU.max)
            dve.drain().then_inc(angles, 1)
            dve.wait_ge(sines, 1)
            hr = ROPE2 // 2
            V.tensor_copy(rope2[:, 0, :, 0:hr], ang[:, 3])
            V.tensor_copy(rope2[:, 0, :, hr:ROPE2], ang[:, 3])
            V.tensor_scalar(rope2[:, 1, :, 0:hr], ang[:, 2], -1.0, None, ALU.mult)
            V.tensor_copy(rope2[:, 1, :, hr:ROPE2], ang[:, 2])
            dve.drain().then_inc(small_free, 1)

            for s in range(2):
                low(s, 0)
            with dve.Fori(0, DEPTH) as l:
                low_T(l, places_x([0]), xTl, xTh)
                for which in range(2):
                    feed_forward(l, lambda s: ffn_n(l, which, s), [0, 1, 2],
                                 (2 * l + which) * NT * NF, lambda t: aux[:, t, FB:2 * FB], FB, [2], NF,
                                 lambda: low_T(l, places_x([1]), xTl, xTh), last_slot=3)
                    if which == 0:
                        mixer(l)
                for t in range(NT):
                    add_tile(l, t)
                    norm_tile(l, 2, t)
                for c in n_aux + n_acc + [n_hi]:
                    c.layer_ends()

            l = L2
            n_norm = [0]
            n_root = [RSTD_LAYER * DEPTH]

            def low_unit(u):
                g = job_of_unit(u)
                if g["units"] is None:
                    s = (g["s0"] + u - g["u0"]) % RING
                    low(s, slot_n2(s, g["n0"][s]))
                else:
                    s, n = g["slots"][u - g["u0"]]
                    k0, k1, cols = g["units"][u - g["u0"]][:3]
                    low(s, slot_n2(s, n), (k1 - k0) * cols)

            def split_after(name):
                for u in units_after(JOB[name]):
                    low_unit(u)

            def split_unit(name, j):
                u = JOB[name]["u0"] + RING + j
                if u < N_UNITS and not in_ff(u):
                    low_unit(u)

            def in_sbuf(name, t=0):
                p, n = JOB[name]["acc"][t]
                dve.wait_ge(acc_read[p], acc_n2(p, n) + 2)

            def add_x(name, t):
                dve.wait_ge(acc_full[t], acc_n2(*JOB[name]["acc"][t]) + 1)
                for half in range(2):
                    c = slice(half * NC, (half + 1) * NC)
                    last = V.tensor_tensor(x[:, t, c], x[:, t, c], acc[:, half, t, :], ALU.add)
                last.then_inc(acc_read[t], 1)
                dve.drain().then_inc(x_ready, 1)

            def norm_x(t):
                if t == 0:
                    n_norm[0] += 1
                n = n_norm[0] - 1
                dve.wait_ge(sumsq, 2 * n + t + 1)
                n_root[0] += 1
                dve.wait_ge(rstd_ready, n_root[0])
                if n > 0:
                    dve.wait_ge(ln_in, 96 * DEPTH + 32 * n)
                else:
                    dve.wait_ge(gain0_in, 16)
                par = ln_par if n else mix_par
                for half in range(2):
                    c = slice(half * NC, (half + 1) * NC)
                    V.scalar_tensor_tensor(bv[:, t, c], x[:, t, c], nx[:, t:t + 1], par[:, 0, c],
                                           ALU.mult, ALU.mult).then_inc(xn_ready, 1)
                if t == NT - 1:
                    dve.drain().then_inc(ln_free, 1)

            def newton(n):
                v, y, z = nv[:, 0:n], ny[:, 0:n], nz[:, 0:n]
                dve.drain()
                V.tensor_scalar(z.bitcast(I32), v.bitcast(I32), 1, None, ALU.logical_shift_right)
                dve.drain()
                V.tensor_scalar(y.bitcast(I32), z.bitcast(I32), -1.0, RSQRT_MAGIC, ALU.mult, ALU.add)
                for _ in range(3):
                    dve.drain()
                    V.scalar_tensor_tensor(z, y, -0.5, y, ALU.mult, ALU.mult)
                    dve.drain()
                    V.tensor_tensor(z, z, v, ALU.mult)
                    dve.drain()
                    V.scalar_tensor_tensor(y, z, 1.5, y, ALU.add, ALU.mult)
                dve.drain()

            def group_vars(sq, n, at=0, scale=1.0):
                groups = sq.shape[1]
                V.tensor_reduce(nv[:, at:at + groups], sq, AX_X, ALU.add)
                dve.drain()
                V.tensor_scalar(nv[:, at:at + groups], nv[:, at:at + groups], 1.0 / (n * scale ** 2),
                                EPS / scale ** 2, ALU.mult, ALU.add)

            def group_scale(src, dst, gain, n, tmp, at=0, signal=None):
                groups = src.shape[1]
                last = V.tensor_tensor(dst if gain is None else tmp, src,
                                       ny[:, at:at + groups].unsqueeze(2).to_broadcast([P, groups, n]), ALU.mult)
                if gain is not None:
                    dve.drain()
                    last = V.tensor_tensor(dst, tmp, gain.unsqueeze(1).to_broadcast([P, groups, n]), ALU.mult)
                if signal is not None:
                    last.then_inc(signal, 1)
                else:
                    dve.drain()

            def rotate2(v, tmp, heads, signal=None):
                hr = ROPE2 // 2
                a_, b_ = tmp
                for t in range(NT):
                    g = slice(t * heads, (t + 1) * heads)

                    def table(k, c0, c1):
                        return rope2[:, k, t, c0:c1].unsqueeze(1).to_broadcast([P, heads, c1 - c0])

                    V.tensor_tensor(a_[:, g], v[:, g], table(0, 0, ROPE2), ALU.mult)
                    V.tensor_tensor(b_[:, g, 0:hr], v[:, g, hr:ROPE2], table(1, 0, hr), ALU.mult)
                    V.tensor_tensor(b_[:, g, hr:ROPE2], v[:, g, 0:hr], table(1, hr, ROPE2), ALU.mult)
                dve.drain()
                last = V.tensor_tensor(v, a_, b_, ALU.add)
                if signal is not None:
                    last.then_inc(signal, 1)
                else:
                    dve.drain()

            n_s = [DEPTH * H1]

            def heads2(n_heads, score, count=None, splits=()):
                n0 = n_s[0]
                n_s[0] += n_heads
                units = [u for name in splits for u in units_after(JOB[name])]

                def scores(h):
                    dve.wait_ge(score_full, n0 - DEPTH * H1 + h + 1)
                    score(probs(h), score_bank(h), h)
                    dve.drain()
                    V.tensor_reduce(row(rmax, h, 0), probs(h)[:, 0:P], AX_X, ALU.max, negate=True)
                    V.tensor_reduce(row(rmax, h, 1), probs(h)[:, P:3 * P], AX_X, ALU.max, negate=True)\
                        .then_inc(s_ready, 1)

                def outputs(g):
                    dve.wait_ge(t_hi, n_hi.take(l) + 1)
                    V.tensor_tensor(yTl[:, g % KT, :], o_pair(g), cast(yTh[:, g % KT, :]), ALU.subtract)\
                        .then_inc(o_read, 1)

                scores(0)
                scores(1)
                for h in range(n_heads):
                    dve.wait_ge(e_ready, n0 + h + 1)
                    tiles = ((0, slice(0, P)), (1, slice(P, 3 * P)))
                    if count is not None:
                        for t, c in tiles:
                            V.scalar_tensor_tensor(probs(h)[:, c], probs(h)[:, c], 1.0, count[:, c],
                                                   ALU.mult, ALU.mult, accum_out=row(rsum, h, t))
                        dve.drain()
                    for t, c in tiles:
                        V.reciprocal(row(rinv, h, t), row(rsum, h, t))
                    dve.drain()
                    for t, c in tiles:
                        last = V.tensor_scalar(probs(h)[:, c], probs(h)[:, c], row(rinv, h, t), None, ALU.mult)
                    last.then_inc(a_ready, 1)
                    if h + 2 < n_heads:
                        scores(h + 2)
                    if h % 2 and h > 1:
                        outputs((n0 - DEPTH * H1 + h - 3) // 2)
                    if h >= 2 and h % 2 == 0 and units:
                        low_unit(units.pop(0))
                outputs((n0 - DEPTH * H1 + n_heads) // 2 - 1)
                for b in (2, 3):
                    n_aux[b].k += n_heads // 2

            def ff_and_side(i):
                g = JOB[f"ff{i}"]
                end = g["u0"] + g["nu"]
                feed_forward(l, lambda s: slot_n2(s, g["n0"][s]), [(g["s0"] + j) % RING for j in range(RING)],
                             2 * DEPTH * NT * NF + i * NT * NF2, lambda t: aux[:, t, :], NC, [2, 3], NF2,
                             lambda: low_T(l, places_x([1]), xTl, xTh),
                             lambda: low_T(l, [place_pair(0, 0)], yTl, yTh))
                add_x(f"ff{i}", 0)
                norm_x(0)
                add_x(f"ff{i}", 1)
                low_unit(end + 2)
                low_T(l, places_x([0]), xTl, xTh)
                norm_x(1)
                low_unit(end + 3)
                low_unit(end + 4)
                low_T(l, places_x([1]), xTl, xTh)
                name = f"g{i}"
                for t in range(NT):
                    in_sbuf(name, t)
                    gate = bg[:, 0, t, :]
                    V.scalar_tensor_tensor(gate, gate, 1.0, bg[:, 1, t, :], ALU.add, ALU.mult)
                    dve.drain()
                    V.scalar_tensor_tensor(x[:, t, :], gate, 0.5, x[:, t, :], ALU.mult, ALU.add)\
                        .then_inc(x_ready, 1)
                    if i == 0:
                        norm_x(t)
                        if t == 0:
                            split_unit(name, 0)
                            split_unit(name, 1)
                        low_T(l, places_x([t]), xTl, xTh)
                        if t == 0:
                            split_unit(name, 2)
                            split_unit(name, 3)

            def out_norm(name):
                add_x(name, 0)
                norm_x(0)
                for j in range(2):
                    split_unit(name, j)
                low_T(l, places_x([0]), xTl, xTh)
                add_x(name, 1)
                norm_x(1)

            norm_x(0)
            norm_x(1)
            low_T(l, places_x([0]), xTl, xTh)
            for u in (2, 3):
                low_unit(u)
            low_T(l, places_x([1]), xTl, xTh)
            mixf, bkf = flat(mix_par), flat(bk)
            gain, c0 = {}, 0
            for name, w in EVEN_GAINS:
                gain[name] = ln_par[:, 1, c0:c0 + w]
                c0 += w

            def tmp(groups, n, at=0):
                return bkf[:, at:at + groups * n].rearrange("p (g c) -> p g c", c=n)

            for j in range(3):
                split_unit("c", j)
            for t in range(NT):
                in_sbuf("c", t)
            dve.wait_ge(gains_in, 16 * len(EVEN_GAINS))
            for k, q in (("e_kn_nope_2", "e_qn_nope_2"), ("e_dil_kn_2", "e_dil_qn_2")):
                V.tensor_tensor(gain[k], gain[k], gain[q], ALU.mult)
            V.tensor_scalar(nv[:, 0:NT], ssq[:, :, 1], 1.0 / Q_LORA, None, ALU.mult)
            V.tensor_scalar(nv[:, NT:2 * NT], ssq[:, :, 2], 1.0 / KV_LORA, None, ALU.mult).then_inc(var_ready, 1)
            n_root[0] += 1
            dve.wait_ge(rstd_ready, n_root[0])
            for t in range(NT):
                v = mixf[:, t * Q_LORA:(t + 1) * Q_LORA]
                last = V.scalar_tensor_tensor(v, v, ny[:, t:t + 1], gain["e_cq_norm_2"], ALU.mult, ALU.mult)
            last.then_inc(low_ready, 1)
            split_unit("c", 3)
            kv = mixf[:, NT * Q_LORA:NT * (Q_LORA + KV_LORA + ROPE2)].rearrange("p (t c) -> p t c", t=NT)
            for t in range(NT):
                v = kv[:, t, 0:KV_LORA]
                last = V.scalar_tensor_tensor(v, v, ny[:, NT + t:NT + t + 1], gain["e_ckv_norm_2"], ALU.mult, ALU.mult)
            last.then_inc(low_ready, 1)
            split_after("qb")
            low_T(l, places_cq(), yTl, yTh)
            low_T(l, [place_pair(2, 3)], yTl, yTh)
            split_after("kb")
            in_sbuf("qb")
            kr = kv[:, :, KV_LORA:]
            qb, kb = (bg_flat[:, k * D:(k + 1) * D].rearrange("p (g c) -> p g c", c=HD) for k in range(2))
            V.tensor_tensor(k_rope, kr, kr, ALU.mult)
            dve.drain()
            group_vars(k_rope, ROPE2, 32)
            group_vars(tmp(16, HD), HD, 0, scale=HD ** -0.5)
            in_sbuf("kb")
            group_vars(tmp(16, HD, D), HD, 16)
            split_after("vb")
            newton(34)
            group_scale(kr, k_rope[:, :, :], gain["e_kn_rope_2"], ROPE2, tmp(NT, ROPE2), 32)
            rotate2(k_rope[:, :, :], (tmp(NT, ROPE2), tmp(NT, ROPE2, 1024)), 1)
            group_scale(qb, qb, None, HD, None, 0, heads_ready)
            group_scale(kb, kb, gain["e_dil_kn_2"], HD, tmp(16, HD, D), 16, heads_ready)
            in_sbuf("uq0")
            in_sbuf("uq1")
            qa = flat(bu)[:, 0:16 * MLA_D].rearrange("p (g c) -> p g c", c=MLA_D)
            kva = flat(bval).rearrange("p (g c) -> p g c", c=P)
            ka = mixf[:, 0:16 * MLA_D].rearrange("p (g c) -> p g c", c=MLA_D)
            dve.drain()
            sq = flat(bq)[:, 0:16 * MLA_D].rearrange("p (g c) -> p g c", c=MLA_D)
            group_vars(sq[:, :, 0:MLA_N], MLA_N, 0)
            group_vars(sq[:, :, MLA_N:], ROPE2, 16)
            in_sbuf("ukv0")
            in_sbuf("ukv1")
            group_vars(flat(bv).rearrange("p (g c) -> p g c", c=P)[:, :, 0:MLA_N], MLA_N, 32)
            newton(48)
            group_scale(qa[:, :, 0:MLA_N], qa[:, :, 0:MLA_N], None, MLA_N, None, 0)
            group_scale(qa[:, :, MLA_N:], qa[:, :, MLA_N:], gain["e_qn_rope_2"], ROPE2, tmp(16, ROPE2, D), 16)
            rotate2(qa[:, :, MLA_N:], (tmp(16, ROPE2, D), tmp(16, ROPE2, D + 512)), MLA_H, signal=heads_ready)
            group_scale(kva[:, :, 0:MLA_N], ka[:, :, 0:MLA_N], gain["e_kn_nope_2"], MLA_N, tmp(16, MLA_N), 32)
            for t in range(NT):
                last = V.tensor_copy(ka[:, t * MLA_H:(t + 1) * MLA_H, MLA_N:],
                                     k_rope[:, t:t + 1, :].to_broadcast([P, MLA_H, ROPE2]))
            last.then_inc(heads_ready, 1)
            for b, k in ((0, 4), (1, 4), (2, 2), (3, 2)):
                n_aux[b].k += k
            split_after("uq0")
            split_after("uq1")
            heads2(MLA_H, lambda o, s, h: V.scalar_tensor_tensor(o, s, MLA_D ** -0.5, causal[:], ALU.mult, ALU.add),
                   splits=("ukv0", "ukv1"))
            heads2(DIL_H, lambda o, s, h: V.scalar_tensor_tensor(o, dist[:, 1, :], slope(h, DIL_H), s, ALU.mult,
                                                                 ALU.add), times)
            out_norm("eout")
            ff_and_side(0)
            og = [ln_par[:, 1, k * HD:(k + 1) * HD] for k in range(2)]
            for k in range(1, 4):
                if k == 1:
                    for j in range(RING):
                        split_unit("z01", j)
                elif k < 4:
                    split_after(f"z{k}")
                if k in (1, 3):
                    if k == 1:
                        for t in range(NT):
                            in_sbuf("z01", t)
                    else:
                        in_sbuf("z2")
                        in_sbuf("z3")
                    if k == 1:
                        dve.wait_ge(gains_in, 16 * (len(EVEN_GAINS) + len(ODD_GAINS)))
                        V.tensor_tensor(og[1], og[1], og[0], ALU.mult)
                    v = flat(bq if k == 1 else bu).rearrange("p (g c) -> p g c", c=HD)
                    dve.drain()
                    group_vars(tmp(32, HD), HD, 0, scale=HD ** -0.5 if k == 1 else 1.0)
                    newton(32)
                    group_scale(v, v, None if k == 1 else og[1], HD, tmp(32, HD), 0, heads_ready)
            for b in range(4):
                n_aux[b].k += 2
            split_after("z4")
            heads2(MOBA_H, lambda o, s, h: V.scalar_tensor_tensor(o, dist[:, 0, :], slope(h, MOBA_H), s, ALU.mult,
                                                                  ALU.add), splits=("z5",))
            out_norm("oout")
            ff_and_side(1)


PI32 = float(np.float32(3.1415925))


def two_pi_parts():
    parts, rest = [], 2 * np.pi
    for _ in range(2):
        _, e = np.frexp(rest)
        step = 2.0 ** (e - 11)
        c = float(np.floor(rest / step) * step)
        parts.append(c)
        rest -= c
    return parts + [float(np.float32(rest))]


def constants():
    r = np.arange(P)
    q, k = r[:, None], r[None, :]
    tri = (q <= k).astype(np.float32)
    d = np.concatenate([q - k, q + P - k, q - k], axis=1)
    causal = np.where(d >= 0, 0.0, NEG).astype(np.float32)
    times = ((d >= 0) & (d <= 128)).astype(np.float32)
    for dil in (4, 16):
        times += ((d >= 0) & (d % dil == 0)).astype(np.float32)
    dist = np.stack([np.where(d >= 0, -d, NEG), np.where(times > 0, -d, NEG)], axis=1).astype(np.float32)
    pos = np.arange(S, dtype=np.float32)
    inv = (np.float32(10000.0) ** (-np.arange(0, HD, 2, dtype=np.float32) / np.float32(HD))).astype(np.float32)
    ang = (pos[:, None] * inv[None, :]).astype(np.float32).astype(np.float64)
    cos, sin = np.cos(ang), np.sin(ang)
    rope = np.stack([np.concatenate([cos, cos], 1), np.concatenate([-sin, sin], 1)])
    rope = rope.reshape(2, NT, P, HD).transpose(2, 0, 1, 3).astype(np.float32)
    lam = 0.8 - 0.6 * np.exp(-0.3 * np.arange(DEPTH))
    half = ROPE2 // 2
    inv2 = (np.float32(10000.0) ** (-np.arange(half, dtype=np.float32) / np.float32(half))).astype(np.float32)
    return {
        "c_ident": np.eye(P, dtype=np.float32),
        "c_tri": tri,
        "c_causal": causal,
        "c_rope": np.ascontiguousarray(rope),
        "c_lam": np.stack([lam, 1.0 - lam], axis=1).astype(np.float32),
        "c_dist": np.ascontiguousarray(dist),
        "c_times": times,
        "c_inv_freq": np.broadcast_to(inv2, (P, half)).copy(),
    }


SHAPES = {
    "w_in": (DEPTH * D, -1), "gate_b": (DEPTH * 2, D), "sgu_w": (DEPTH * 8, P, P), "sgu_b": (DEPTH * 8, P),
    "lam": (DEPTH, 4 * HD), "w_branch": (DEPTH * 2 * D, D), "w_out": (DEPTH * D, D),
    "ffn_w1": (DEPTH * 2 * D, F1), "ffn_w3": (DEPTH * 2 * D, F1), "ffn_w2": (DEPTH * 2 * F1, D),
    "ln_g": (DEPTH * 3, D), "ln_b": (DEPTH * 3, D),
    "p_2": (DEPTH * S, 256), "e_w_in_2": (D, -1), "e_w_uq_2": (Q_LORA, -1), "e_w_ukv_2": (KV_LORA, -1),
    "e_w_out_2": (D, D), "o_w_in_2": (D, -1), "o_w_out_2": (D, D), "w_ff1_2": (DEPTH * D, F2),
    "w_ff2_2": (DEPTH * F2, D), "w_ple_gate_2": (DEPTH * D, D), "w_ple_proj_2": (DEPTH * 256, D),
}


def kernel(**inputs):
    from concourse.bacc import Bacc
    from concourse.bass_utils import run_bass_kernel_spmd

    nc = Bacc("TRN2", target_bir_lowering=False, num_devices=1, dynamic_dma_scratch_size=4096)
    arrays, args = {}, {}
    for name, value in {**inputs, **constants()}.items():
        v = np.ascontiguousarray(value)
        if name in SHAPES:
            v = v.reshape(SHAPES[name])
        arrays[name] = v
        args[name] = nc.dram_tensor(name, v.shape, mybir.dt.from_np(v.dtype), kind="ExternalInput").ap()
    out = nc.dram_tensor("out", (1, S, D), F32, kind="ExternalOutput").ap()
    build(nc, args, out)
    return run_bass_kernel_spmd(nc, [arrays], core_ids=[0]).results[0]["out"]
```
